# Optimizing a Trainium2 kernel written in Bass

```python
import math
import jax
import jax.numpy as jnp
from jax import lax
import numpy as np

D_MODEL = 1024
BATCH = 1
SEQ = 256
DEPTH = 2

CTX_LEN = 256
GRID_W = 64
EPS = 1e-6
N_MOD = 6
HEAD_DIM = 64
ATTN_WIDTH = D_MODEL // 2
N_HEADS = ATTN_WIDTH // HEAD_DIM
N_KV_HEADS = 2
Q_PER_KV = N_HEADS // N_KV_HEADS
ROPE_THETA = 10000.0
ATTN_BLOCK = 128
SSD_WIDTH = D_MODEL - ATTN_WIDTH
SSD_HEAD_DIM = 64
SSD_HEADS = SSD_WIDTH // SSD_HEAD_DIM
SSD_GROUPS = 2
HEADS_PER_GROUP = SSD_HEADS // SSD_GROUPS
D_STATE = 128
CONV_WIDTH = 5
SSD_CHUNK = 128
D_FF = -(-8 * D_MODEL // (3 * 256)) * 256
Q_DIM = N_HEADS * HEAD_DIM
KV_DIM = N_KV_HEADS * HEAD_DIM
BC_DIM = SSD_GROUPS * D_STATE
XBC_DIM = SSD_WIDTH + 2 * BC_DIM
IN_DIM = Q_DIM + 2 * KV_DIM + SSD_WIDTH + XBC_DIM + SSD_HEADS
IN_SPLITS = (Q_DIM, Q_DIM + KV_DIM, Q_DIM + 2 * KV_DIM, Q_DIM + 2 * KV_DIM + SSD_WIDTH,
             Q_DIM + 2 * KV_DIM + SSD_WIDTH + XBC_DIM)


def rmsnorm(x, w):
    xf = x.astype(jnp.float32)
    y = xf * lax.rsqrt(jnp.mean(xf * xf, axis=-1, keepdims=True) + EPS)
    return (y * w.astype(jnp.float32)).astype(x.dtype)

def axial_rope_tables(rows):
    row = jnp.repeat(jnp.arange(rows, dtype=jnp.float32), GRID_W)
    col = jnp.tile(jnp.arange(GRID_W, dtype=jnp.float32), rows)
    n_freq = HEAD_DIM // 4
    freqs = ROPE_THETA ** (-jnp.arange(n_freq, dtype=jnp.float32) / n_freq)
    ang = jnp.concatenate([row[:, None] * freqs, col[:, None] * freqs], axis=-1)
    return jnp.cos(ang), jnp.sin(ang)

def apply_rope(x, cos, sin):
    half = HEAD_DIM // 2
    x1, x2 = x[..., :half], x[..., half:]
    c = cos[None, :, None, :].astype(x.dtype)
    s = sin[None, :, None, :].astype(x.dtype)
    return jnp.concatenate([x1 * c - x2 * s, x1 * s + x2 * c], axis=-1)

def block_attention(q, k, v):
    b, n = q.shape[:2]
    nb = n // ATTN_BLOCK
    qb = q.reshape(b, nb, ATTN_BLOCK, N_KV_HEADS, Q_PER_KV, HEAD_DIM).transpose(1, 0, 2, 3, 4, 5)
    scale = HEAD_DIM ** -0.5

    def one_block(q_blk):
        s = jnp.einsum('bqkgd,bskd->bkgqs', q_blk, k).astype(jnp.float32) * scale
        p = jax.nn.softmax(s, axis=-1).astype(v.dtype)
        return jnp.einsum('bkgqs,bskd->bqkgd', p, v)

    o = lax.map(one_block, qb)
    return o.transpose(1, 0, 2, 3, 4, 5).reshape(b, n, N_HEADS * HEAD_DIM)

def depthwise_conv_silu(x, w, bias):
    y = lax.conv_general_dilated(
        x, w[:, None, :].astype(x.dtype), window_strides=(1,),
        padding=[(CONV_WIDTH // 2, CONV_WIDTH // 2)],
        dimension_numbers=('NWC', 'WIO', 'NWC'), feature_group_count=x.shape[-1])
    return jax.nn.silu(y + bias.astype(x.dtype))

def ssd_scan(x, dt, A, B, C, h0):
    b, L, H, P = x.shape
    nc = L // SSD_CHUNK
    f32 = jnp.float32
    Bh = jnp.repeat(B.astype(f32), HEADS_PER_GROUP, axis=2).reshape(b, nc, SSD_CHUNK, H, D_STATE)
    Ch = jnp.repeat(C.astype(f32), HEADS_PER_GROUP, axis=2).reshape(b, nc, SSD_CHUNK, H, D_STATE)
    xdt = (x.astype(f32) * dt[..., None]).reshape(b, nc, SSD_CHUNK, H, P)
    acum = jnp.cumsum((dt * A).reshape(b, nc, SSD_CHUNK, H), axis=2)
    lower = jnp.tril(jnp.ones((SSD_CHUNK, SSD_CHUNK), dtype=bool))[None, None, :, :, None]
    seg = acum[:, :, :, None, :] - acum[:, :, None, :, :]
    decay = jnp.exp(jnp.where(lower, seg, -jnp.inf))
    scores = jnp.einsum('bcihn,bcjhn->bcijh', Ch, Bh) * decay
    y_intra = jnp.einsum('bcijh,bcjhp->bcihp', scores, xdt)
    decay_to_end = jnp.exp(acum[:, :, -1:, :] - acum)
    chunk_states = jnp.einsum('bcjhn,bcjh,bcjhp->bchpn', Bh, decay_to_end, xdt)
    chunk_decay = jnp.exp(acum[:, :, -1, :])

    def step(h, inp):
        s_c, d_c = inp
        return h * d_c[:, :, None, None] + s_c, h

    h_final, h_in = lax.scan(step, h0, (chunk_states.transpose(1, 0, 2, 3, 4), chunk_decay.transpose(1, 0, 2)))
    h_in = h_in.transpose(1, 0, 2, 3, 4)
    y_inter = jnp.einsum('bcihn,bcih,bchpn->bcihp', Ch, jnp.exp(acum), h_in)
    return (y_intra + y_inter).reshape(b, L, H, P), h_final

def hybrid_mixer(h_lat, h_ctx, cos, sin, w_in, q_norm, k_norm, conv_w, conv_b, dt_bias_fwd, dt_bias_bwd,
                 a_log_fwd, a_log_bwd, d_skip, ssd_norm, w_out, with_ctx_out):
    b, n_lat, _ = h_lat.shape
    n_ctx = h_ctx.shape[1]
    f32 = jnp.float32
    q_l, k_l, v_l, z_l, xbc_l, dt_l = jnp.split(h_lat @ w_in, IN_SPLITS, axis=-1)
    q_c, k_c, v_c, z_c, xbc_c, dt_c = jnp.split(h_ctx @ w_in, IN_SPLITS, axis=-1)

    def heads(q, k, v, n):
        q = rmsnorm(q.reshape(b, n, N_HEADS, HEAD_DIM), q_norm)
        k = rmsnorm(k.reshape(b, n, N_KV_HEADS, HEAD_DIM), k_norm)
        return q, k, v.reshape(b, n, N_KV_HEADS, HEAD_DIM)

    q_l, k_l, v_l = heads(q_l, k_l, v_l, n_lat)
    q_c, k_c, v_c = heads(q_c, k_c, v_c, n_ctx)
    q_l = apply_rope(q_l, cos, sin)
    k_l = apply_rope(k_l, cos, sin)
    k_all = jnp.concatenate([k_c, k_l], axis=1)
    v_all = jnp.concatenate([v_c, v_l], axis=1)
    attn_l = block_attention(q_l, k_all, v_all)

    def ssd_inputs(xbc, n):
        xbc = depthwise_conv_silu(xbc, conv_w, conv_b)
        xs, Bs, Cs = jnp.split(xbc, (SSD_WIDTH, SSD_WIDTH + BC_DIM), axis=-1)
        return (xs.reshape(b, n, SSD_HEADS, SSD_HEAD_DIM), Bs.reshape(b, n, SSD_GROUPS, D_STATE),
                Cs.reshape(b, n, SSD_GROUPS, D_STATE))

    xs_l, B_l, C_l = ssd_inputs(xbc_l, n_lat)
    xs_c, B_c, C_c = ssd_inputs(xbc_c, n_ctx)
    ys_l, ys_c = [], []
    for dt_bias, a_log, reverse in ((dt_bias_fwd, a_log_fwd, False), (dt_bias_bwd, a_log_bwd, True)):
        A = -jnp.exp(a_log.astype(f32))
        d_l = jax.nn.softplus(dt_l.astype(f32) + dt_bias.astype(f32))
        d_c = jax.nn.softplus(dt_c.astype(f32) + dt_bias.astype(f32))
        flip = (lambda t: jnp.flip(t, axis=1)) if reverse else (lambda t: t)
        h0 = jnp.zeros((b, SSD_HEADS, SSD_HEAD_DIM, D_STATE), f32)
        y_c, h_ctx_final = ssd_scan(flip(xs_c), flip(d_c), A, flip(B_c), flip(C_c), h0)
        y_l, _ = ssd_scan(flip(xs_l), flip(d_l), A, flip(B_l), flip(C_l), h_ctx_final)
        ys_l.append(flip(y_l))
        ys_c.append(flip(y_c))

    def ssd_output(y, xs, z, n):
        y = (y + d_skip.astype(f32)[:, None] * xs.astype(f32)).astype(z.dtype).reshape(b, n, SSD_WIDTH)
        return rmsnorm(y * jax.nn.silu(z), ssd_norm)

    out_l = jnp.concatenate([attn_l, ssd_output(ys_l[0] + ys_l[1], xs_l, z_l, n_lat)], axis=-1) @ w_out
    if not with_ctx_out:
        return out_l, None
    attn_c = block_attention(q_c, k_c, v_c)
    out_c = jnp.concatenate([attn_c, ssd_output(ys_c[0] + ys_c[1], xs_c, z_c, n_ctx)], axis=-1) @ w_out
    return out_l, out_c

def swiglu(h, w_gate, w_up, w_down):
    return (jax.nn.silu(h @ w_gate) * (h @ w_up)) @ w_down

def first_inputs(seed: int = 0) -> dict:
    key = jax.random.key(seed)
    ks = jax.random.split(key, 24)
    f32 = jnp.float32
    L = DEPTH

    def nrm(k, shape, scale):
        return jax.random.normal(k, shape, f32) * scale

    def gain(k, shape):
        return 1.0 + 0.05 * jax.random.normal(k, shape, f32)

    dt0 = jnp.exp(jax.random.uniform(ks[14], (L, 2, SSD_HEADS), f32, math.log(1e-3), math.log(1e-1)))
    dt_bias = dt0 + jnp.log(-jnp.expm1(-dt0))
    a_log = jnp.log(jax.random.uniform(ks[15], (L, 2, SSD_HEADS), f32, 1.0, 16.0))
    nk = jax.random.split(ks[6], 4)
    return {
        'x': nrm(ks[0], (BATCH, SEQ, D_MODEL), 1.0),
        'c': nrm(ks[1], (BATCH, D_MODEL), 1.0),
        'ctx': nrm(ks[2], (BATCH, CTX_LEN, D_MODEL), 1.0),
        'c_ctx': nrm(ks[3], (D_MODEL,), 1.0),
        'w_mod': nrm(ks[4], (L, D_MODEL, N_MOD * D_MODEL), 0.5 * D_MODEL ** -0.5),
        'b_mod': nrm(ks[5], (L, N_MOD * D_MODEL), 0.02),
        'norm_mix_pre': gain(nk[0], (L, D_MODEL)),
        'norm_mix_post': gain(nk[1], (L, D_MODEL)),
        'norm_ffn_pre': gain(nk[2], (L, D_MODEL)),
        'norm_ffn_post': gain(nk[3], (L, D_MODEL)),
        'w_in': nrm(ks[10], (L, D_MODEL, IN_DIM), D_MODEL ** -0.5),
        'q_norm': gain(ks[11], (L, HEAD_DIM)),
        'k_norm': gain(ks[12], (L, HEAD_DIM)),
        'conv_w': nrm(ks[13], (L, CONV_WIDTH, XBC_DIM), CONV_WIDTH ** -0.5),
        'conv_b': nrm(ks[16], (L, XBC_DIM), 0.02),
        'dt_bias_fwd': dt_bias[:, 0],
        'dt_bias_bwd': dt_bias[:, 1],
        'a_log_fwd': a_log[:, 0],
        'a_log_bwd': a_log[:, 1],
        'd_skip': 1.0 + 0.1 * jax.random.normal(ks[17], (L, SSD_HEADS), f32),
        'ssd_norm': gain(ks[18], (L, SSD_WIDTH)),
        'w_out': nrm(ks[19], (L, D_MODEL, D_MODEL), D_MODEL ** -0.5),
        'w_gate': nrm(ks[20], (L, D_MODEL, D_FF), D_MODEL ** -0.5),
        'w_up': nrm(ks[21], (L, D_MODEL, D_FF), D_MODEL ** -0.5),
        'w_down': nrm(ks[22], (L, D_FF, D_MODEL), D_FF ** -0.5),
    }

def first_block(x, c, ctx, c_ctx, w_mod, b_mod, norm_mix_pre, norm_mix_post, norm_ffn_pre, norm_ffn_post,
              w_in, q_norm, k_norm, conv_w, conv_b, dt_bias_fwd, dt_bias_bwd, a_log_fwd, a_log_bwd, d_skip,
              ssd_norm, w_out, w_gate, w_up, w_down):
    n_lat = x.shape[1]
    rows = n_lat // GRID_W
    cos, sin = axial_rope_tables(rows)
    silu_c = jax.nn.silu(c)
    silu_cc = jax.nn.silu(c_ctx)
    x_lat, x_ctx = x, ctx
    for l in range(DEPTH):
        update_ctx = l < DEPTH - 1
        mod_l = (silu_c @ w_mod[l] + b_mod[l])[:, None, :]
        mod_c = (silu_cc @ w_mod[l] + b_mod[l])[None, None, :]
        sh1_l, sc1_l, g1_l, sh2_l, sc2_l, g2_l = jnp.split(mod_l, N_MOD, axis=-1)
        sh1_c, sc1_c, g1_c, sh2_c, sc2_c, g2_c = jnp.split(mod_c, N_MOD, axis=-1)

        h_l = rmsnorm(x_lat, norm_mix_pre[l]) * (1.0 + sc1_l) + sh1_l
        h_c = rmsnorm(x_ctx, norm_mix_pre[l]) * (1.0 + sc1_c) + sh1_c
        m_l, m_c = hybrid_mixer(h_l, h_c, cos, sin, w_in[l], q_norm[l], k_norm[l], conv_w[l], conv_b[l],
                                dt_bias_fwd[l], dt_bias_bwd[l], a_log_fwd[l], a_log_bwd[l], d_skip[l],
                                ssd_norm[l], w_out[l], update_ctx)
        x_lat = x_lat + g1_l * rmsnorm(m_l, norm_mix_post[l])

        f_l = rmsnorm(x_lat, norm_ffn_pre[l]) * (1.0 + sc2_l) + sh2_l
        x_lat = x_lat + g2_l * rmsnorm(swiglu(f_l, w_gate[l], w_up[l], w_down[l]), norm_ffn_post[l])

        if update_ctx:
            x_ctx = x_ctx + g1_c * rmsnorm(m_c, norm_mix_post[l])
            f_c = rmsnorm(x_ctx, norm_ffn_pre[l]) * (1.0 + sc2_c) + sh2_c
            x_ctx = x_ctx + g2_c * rmsnorm(swiglu(f_c, w_gate[l], w_up[l], w_down[l]), norm_ffn_post[l])
    return x_lat


N_HEADS_2 = D_MODEL // HEAD_DIM
N_KV_HEADS_2 = 4
GROUP = N_HEADS_2 // N_KV_HEADS_2
RMS_EPS = 1e-6
NEG_INF = -1e30
POS_INF = 1e30
IDX_HEADS = 8
IDX_DIM = HEAD_DIM
DSA_TOPK = 256
DSA_Q_BLOCK = 128
CMP_LEN = 32
CMP_STRIDE = 16
CMP_HIDDEN = 256
SLC_LEN = 64
SLC_TOPN = 16
WINDOW = 512
NSA_Q_BLOCK = 64
N_NSA_BRANCH = 3
D_FF_2 = 256 * ((8 * D_MODEL // 3 + 255) // 256)
N_EXPERTS = 8
TOP_K_EXPERTS = 2
D_FF_EXPERT = 7 * D_MODEL // 2
N_A_LAYERS = max(1, DEPTH // 2)
N_B_LAYERS = DEPTH - N_A_LAYERS
N_DENSE_LAYERS = (DEPTH + 1) // 2
N_MOE_LAYERS = DEPTH // 2
A_WIDTHS = (N_HEADS_2 * HEAD_DIM, N_KV_HEADS_2 * HEAD_DIM, N_KV_HEADS_2 * HEAD_DIM, IDX_HEADS * IDX_DIM, IDX_DIM, IDX_HEADS)
A_IN = sum(A_WIDTHS)
B_IN = N_HEADS_2 * HEAD_DIM + N_NSA_BRANCH * N_HEADS_2
KV_WIDTH = 2 * N_NSA_BRANCH * N_KV_HEADS_2 * HEAD_DIM


F32 = jnp.float32

def rmsnorm_2(x, g):
    xf = x.astype(F32)
    y = xf * lax.rsqrt(jnp.mean(xf * xf, axis=-1, keepdims=True) + RMS_EPS)
    return (y * g.astype(F32)).astype(x.dtype)

def modulate(u, shift, scale):
    return u * (1.0 + scale[:, None, :]) + shift[:, None, :]

def rope_tables(positions, dim):
    inv = 1.0 / (ROPE_THETA ** (jnp.arange(0, dim, 2, dtype=F32) / dim))
    ang = positions.astype(F32)[..., None] * inv
    return jnp.cos(ang), jnp.sin(ang)

def apply_rope_2(x, cos, sin):
    x1, x2 = jnp.split(x.astype(F32), 2, axis=-1)
    c = cos[:, :, None, :]
    s = sin[:, :, None, :]
    return jnp.concatenate([x1 * c - x2 * s, x2 * c + x1 * s], axis=-1).astype(x.dtype)

def masked_softmax(s, mask):
    p = jax.nn.softmax(jnp.where(mask, s, NEG_INF), axis=-1)
    return jnp.where(mask, p, 0.0)

def swiglu_2(u, wg, wu, wd):
    return (jax.nn.silu(u @ wg) * (u @ wu)) @ wd

def moe_swiglu(u, w_router, wg, wu, wd):
    bsz, seq, d = u.shape
    xf = u.reshape(bsz * seq, d)
    logits = (xf @ w_router).astype(F32)
    vals, idx = lax.top_k(logits, TOP_K_EXPERTS)
    w = jax.nn.softmax(vals, axis=-1)
    gate = jnp.sum(jax.nn.one_hot(idx, N_EXPERTS, dtype=F32) * w[..., None], axis=1)
    y = jnp.zeros_like(xf)
    for e in range(N_EXPERTS):
        y = y + gate[:, e:e + 1].astype(xf.dtype) * swiglu_2(xf, wg[e], wu[e], wd[e])
    return y.reshape(bsz, seq, d)

def dsa_mixer(u, cos, sin, w_in, w_out):
    bsz, seq, _ = u.shape
    splits = [int(i) for i in np.cumsum(A_WIDTHS[:-1])]
    q, k, v, iq, ik, iw = jnp.split(u @ w_in, splits, axis=-1)
    q = apply_rope_2(q.reshape(bsz, seq, N_HEADS_2, HEAD_DIM), cos, sin)
    k = apply_rope_2(k.reshape(bsz, seq, N_KV_HEADS_2, HEAD_DIM), cos, sin)
    v = v.reshape(bsz, seq, N_KV_HEADS_2, HEAD_DIM)
    iq = apply_rope_2(iq.reshape(bsz, seq, IDX_HEADS, IDX_DIM), cos, sin).astype(F32)
    ik = apply_rope_2(ik.reshape(bsz, seq, 1, IDX_DIM), cos, sin)[:, :, 0].astype(F32)
    iw = iw.astype(F32) * (IDX_HEADS ** -0.5 * IDX_DIM ** -0.5)
    n_keep = min(DSA_TOPK, seq // 4)
    key_pos = jnp.arange(seq)
    scale = HEAD_DIM ** -0.5

    def block(i):
        q0 = i * DSA_Q_BLOCK
        t = q0 + jnp.arange(DSA_Q_BLOCK)
        qb = lax.dynamic_slice_in_dim(q, q0, DSA_Q_BLOCK, axis=1)
        iqb = lax.dynamic_slice_in_dim(iq, q0, DSA_Q_BLOCK, axis=1)
        iwb = lax.dynamic_slice_in_dim(iw, q0, DSA_Q_BLOCK, axis=1)
        rel = jax.nn.relu(jnp.einsum('bqhd,bsd->bqhs', iqb, ik))
        score = jnp.einsum('bqh,bqhs->bqs', iwb, rel)
        score = jnp.where(key_pos[None, None, :] <= t[None, :, None], score, NEG_INF)
        _, idx = lax.top_k(score, n_keep)
        kg = jax.vmap(lambda kb, ib: kb[ib])(k, idx)
        vg = jax.vmap(lambda vb, ib: vb[ib])(v, idx)
        qg = qb.reshape(bsz, DSA_Q_BLOCK, N_KV_HEADS_2, GROUP, HEAD_DIM)
        s = jnp.einsum('bqgrd,bqkgd->bgrqk', qg, kg).astype(F32) * scale
        valid = (idx <= t[None, :, None])[:, None, None]
        p = masked_softmax(s, valid).astype(vg.dtype)
        o = jnp.einsum('bgrqk,bqkgd->bqgrd', p, vg)
        return o.reshape(bsz, DSA_Q_BLOCK, N_HEADS_2 * HEAD_DIM)

    o = lax.map(block, jnp.arange(seq // DSA_Q_BLOCK))
    o = jnp.transpose(o, (1, 0, 2, 3)).reshape(bsz, seq, N_HEADS_2 * HEAD_DIM)
    return o @ w_out

def compress_blocks(x, blk_idx, pe, w1, w2):
    bsz = x.shape[0]
    n_cmp = blk_idx.shape[0]
    xb = x[:, blk_idx] + pe[None, None, :, None, :]
    xb = jnp.transpose(xb, (0, 1, 3, 2, 4)).reshape(bsz, n_cmp, N_KV_HEADS_2, CMP_LEN * HEAD_DIM)
    return jax.nn.gelu(xb @ w1) @ w2

def nsa_shared_kv(h, c_act, kv_gain, w_kv_ada, b_kv_ada, w_kv, pe_k, w1_k, w2_k, pe_v, w1_v, w2_v, cos, sin):
    bsz, seq, _ = h.shape
    shift, scale = jnp.split(c_act @ w_kv_ada + b_kv_ada, 2, axis=-1)
    u = modulate(rmsnorm_2(h, kv_gain), shift, scale)
    kv = (u @ w_kv).reshape(bsz, seq, 2 * N_NSA_BRANCH, N_KV_HEADS_2, HEAD_DIM)
    k_cmp = apply_rope_2(kv[:, :, 0], cos, sin)
    v_cmp = kv[:, :, 1]
    k_slc = apply_rope_2(kv[:, :, 2], cos, sin)
    v_slc = kv[:, :, 3]
    k_win = apply_rope_2(kv[:, :, 4], cos, sin)
    v_win = kv[:, :, 5]
    n_cmp = (seq - CMP_LEN) // CMP_STRIDE + 1
    blk_idx = np.arange(n_cmp)[:, None] * CMP_STRIDE + np.arange(CMP_LEN)[None, :]
    kc = compress_blocks(k_cmp, blk_idx, pe_k, w1_k, w2_k)
    vc = compress_blocks(v_cmp, blk_idx, pe_v, w1_v, w2_v)
    return kc, vc, k_slc, v_slc, k_win, v_win

def nsa_mixer(u, cos, sin, kc, vc, k_slc, v_slc, k_win, v_win, w_q, w_out):
    bsz, seq, _ = u.shape
    proj = u @ w_q
    q = apply_rope_2(proj[..., :N_HEADS_2 * HEAD_DIM].reshape(bsz, seq, N_HEADS_2, HEAD_DIM), cos, sin)
    gates = jax.nn.sigmoid(proj[..., N_HEADS_2 * HEAD_DIM:].astype(F32)).reshape(bsz, seq, N_HEADS_2, N_NSA_BRANCH)
    n_cmp = kc.shape[1]
    n_slc = seq // SLC_LEN
    n_sel = min(SLC_TOPN, n_slc)
    cmp_start = np.arange(n_cmp) * CMP_STRIDE
    cmp_end = jnp.asarray(cmp_start + CMP_LEN - 1)
    slc_start = np.arange(n_slc) * SLC_LEN
    ov = np.minimum(cmp_start[:, None] + CMP_LEN, slc_start[None, :] + SLC_LEN) - np.maximum(cmp_start[:, None], slc_start[None, :])
    agg = jnp.asarray(np.clip(ov, 0, None) / CMP_LEN, dtype=F32)
    ks_blk = jnp.transpose(k_slc.reshape(bsz, n_slc, SLC_LEN, N_KV_HEADS_2, HEAD_DIM), (0, 3, 1, 2, 4))
    vs_blk = jnp.transpose(v_slc.reshape(bsz, n_slc, SLC_LEN, N_KV_HEADS_2, HEAD_DIM), (0, 3, 1, 2, 4))
    kw_pad = jnp.pad(k_win, ((0, 0), (WINDOW, 0), (0, 0), (0, 0)))
    vw_pad = jnp.pad(v_win, ((0, 0), (WINDOW, 0), (0, 0), (0, 0)))
    blk = jnp.arange(n_slc)
    in_blk = jnp.arange(SLC_LEN)
    scale = HEAD_DIM ** -0.5

    def block(i):
        q0 = i * NSA_Q_BLOCK
        t = q0 + jnp.arange(NSA_Q_BLOCK)
        qb = lax.dynamic_slice_in_dim(q, q0, NSA_Q_BLOCK, axis=1)
        qb = jnp.transpose(qb.reshape(bsz, NSA_Q_BLOCK, N_KV_HEADS_2, GROUP, HEAD_DIM), (0, 2, 3, 1, 4))
        gb = lax.dynamic_slice_in_dim(gates, q0, NSA_Q_BLOCK, axis=1)
        gb = jnp.transpose(gb.reshape(bsz, NSA_Q_BLOCK, N_KV_HEADS_2, GROUP, N_NSA_BRANCH), (0, 2, 3, 1, 4))
        sc = jnp.einsum('bgrqd,bngd->bgrqn', qb, kc).astype(F32) * scale
        pc = masked_softmax(sc, cmp_end[None, :] <= t[:, None])
        oc = jnp.einsum('bgrqn,bngd->bgrqd', pc.astype(vc.dtype), vc)
        imp = jnp.einsum('bgrqn,nj->bgqj', pc, agg)
        jt = t // SLC_LEN
        valid_b = blk[None, :] * SLC_LEN <= t[:, None]
        forced = (blk[None, :] == 0) | (blk[None, :] == jt[:, None]) | (blk[None, :] == jt[:, None] - 1)
        imp = jnp.where(valid_b, jnp.where(forced, POS_INF, imp), NEG_INF)
        _, sel = lax.top_k(imp, n_sel)
        kg = jax.vmap(jax.vmap(lambda kb, sb: kb[sb]))(ks_blk, sel)
        vg = jax.vmap(jax.vmap(lambda vb, sb: vb[sb]))(vs_blk, sel)
        tok = sel[..., None] * SLC_LEN + in_blk
        ss = jnp.einsum('bgrqd,bgqnld->bgrqnl', qb, kg).astype(F32) * scale
        ss = ss.reshape(bsz, N_KV_HEADS_2, GROUP, NSA_Q_BLOCK, n_sel * SLC_LEN)
        ms = (tok <= t[None, None, :, None, None]).reshape(bsz, N_KV_HEADS_2, 1, NSA_Q_BLOCK, n_sel * SLC_LEN)
        ps = masked_softmax(ss, ms)
        os_ = jnp.einsum('bgrqm,bgqmd->bgrqd', ps.astype(vg.dtype), vg.reshape(bsz, N_KV_HEADS_2, NSA_Q_BLOCK, n_sel * SLC_LEN, HEAD_DIM))
        kwb = lax.dynamic_slice_in_dim(kw_pad, q0, NSA_Q_BLOCK + WINDOW, axis=1)
        vwb = lax.dynamic_slice_in_dim(vw_pad, q0, NSA_Q_BLOCK + WINDOW, axis=1)
        s_pos = q0 - WINDOW + jnp.arange(NSA_Q_BLOCK + WINDOW)
        mw = (s_pos[None, :] >= 0) & (s_pos[None, :] <= t[:, None]) & (s_pos[None, :] > t[:, None] - WINDOW)
        sw = jnp.einsum('bgrqd,bkgd->bgrqk', qb, kwb).astype(F32) * scale
        pw = masked_softmax(sw, mw)
        ow = jnp.einsum('bgrqk,bkgd->bgrqd', pw.astype(vwb.dtype), vwb)
        o = gb[..., 0:1] * oc.astype(F32) + gb[..., 1:2] * os_.astype(F32) + gb[..., 2:3] * ow.astype(F32)
        return jnp.transpose(o, (0, 3, 1, 2, 4)).reshape(bsz, NSA_Q_BLOCK, N_HEADS_2 * HEAD_DIM).astype(u.dtype)

    o = lax.map(block, jnp.arange(seq // NSA_Q_BLOCK))
    o = jnp.transpose(o, (1, 0, 2, 3)).reshape(bsz, seq, N_HEADS_2 * HEAD_DIM)
    return o @ w_out

def second_inputs(seed: int = 0) -> dict:
    key = jax.random.key(seed)
    ks = jax.random.split(key, 32)
    d = D_MODEL

    def nrm(k, shape, scale):
        return jax.random.normal(k, shape, F32) * scale

    offset = jax.random.randint(ks[2], (BATCH, 1), 0, 1024, dtype=jnp.int32)
    positions = (offset + jnp.arange(SEQ, dtype=jnp.int32)[None, :]).astype(jnp.int32)
    return {
        'x': nrm(ks[0], (BATCH, SEQ, d), 1.0),
        'c': nrm(ks[1], (BATCH, d), 1.0),
        'positions': positions,
        'attn_gain': 1.0 + nrm(ks[3], (DEPTH, d), 0.05),
        'ffn_gain': 1.0 + nrm(ks[4], (DEPTH, d), 0.05),
        'w_ada': nrm(ks[5], (DEPTH, d, 6 * d), 0.5 * d ** -0.5),
        'b_ada': nrm(ks[6], (DEPTH, 6 * d), 0.01),
        'a_w_in': nrm(ks[7], (N_A_LAYERS, d, A_IN), d ** -0.5),
        'a_w_out': nrm(ks[8], (N_A_LAYERS, N_HEADS_2 * HEAD_DIM, d), (N_HEADS_2 * HEAD_DIM) ** -0.5),
        'b_w_q': nrm(ks[9], (N_B_LAYERS, d, B_IN), d ** -0.5),
        'b_w_out': nrm(ks[10], (N_B_LAYERS, N_HEADS_2 * HEAD_DIM, d), (N_HEADS_2 * HEAD_DIM) ** -0.5),
        'kv_gain': 1.0 + nrm(ks[11], (d,), 0.05),
        'w_kv_ada': nrm(ks[12], (d, 2 * d), 0.5 * d ** -0.5),
        'b_kv_ada': nrm(ks[13], (2 * d,), 0.01),
        'w_kv': nrm(ks[14], (d, KV_WIDTH), d ** -0.5),
        'cmp_pe_k': nrm(ks[15], (CMP_LEN, HEAD_DIM), 0.5),
        'cmp_w1_k': nrm(ks[16], (CMP_LEN * HEAD_DIM, CMP_HIDDEN), (CMP_LEN * HEAD_DIM) ** -0.5),
        'cmp_w2_k': nrm(ks[17], (CMP_HIDDEN, HEAD_DIM), CMP_HIDDEN ** -0.5),
        'cmp_pe_v': nrm(ks[18], (CMP_LEN, HEAD_DIM), 0.5),
        'cmp_w1_v': nrm(ks[19], (CMP_LEN * HEAD_DIM, CMP_HIDDEN), (CMP_LEN * HEAD_DIM) ** -0.5),
        'cmp_w2_v': nrm(ks[20], (CMP_HIDDEN, HEAD_DIM), CMP_HIDDEN ** -0.5),
        'ffn_w_gate': nrm(ks[21], (N_DENSE_LAYERS, d, D_FF_2), d ** -0.5),
        'ffn_w_up': nrm(ks[22], (N_DENSE_LAYERS, d, D_FF_2), d ** -0.5),
        'ffn_w_down': nrm(ks[23], (N_DENSE_LAYERS, D_FF_2, d), D_FF_2 ** -0.5),
        'moe_w_router': nrm(ks[24], (N_MOE_LAYERS, d, N_EXPERTS), d ** -0.5),
        'moe_w_gate': nrm(ks[25], (N_MOE_LAYERS, N_EXPERTS, d, D_FF_EXPERT), d ** -0.5),
        'moe_w_up': nrm(ks[26], (N_MOE_LAYERS, N_EXPERTS, d, D_FF_EXPERT), d ** -0.5),
        'moe_w_down': nrm(ks[27], (N_MOE_LAYERS, N_EXPERTS, D_FF_EXPERT, d), D_FF_EXPERT ** -0.5),
        'final_gain': 1.0 + nrm(ks[28], (d,), 0.05),
    }

def second_block(x, c, positions, attn_gain, ffn_gain, w_ada, b_ada, a_w_in, a_w_out, b_w_q, b_w_out,
              kv_gain, w_kv_ada, b_kv_ada, w_kv, cmp_pe_k, cmp_w1_k, cmp_w2_k, cmp_pe_v, cmp_w1_v, cmp_w2_v,
              ffn_w_gate, ffn_w_up, ffn_w_down, moe_w_router, moe_w_gate, moe_w_up, moe_w_down, final_gain):
    cos, sin = rope_tables(positions, HEAD_DIM)
    c_act = jax.nn.silu(c)
    h = x
    kc = vc = k_slc = v_slc = k_win = v_win = None
    for layer in range(DEPTH):
        mod = c_act @ w_ada[layer] + b_ada[layer]
        a_shift, a_scale, a_gate, f_shift, f_scale, f_gate = jnp.split(mod, 6, axis=-1)
        if layer == N_A_LAYERS:
            kc, vc, k_slc, v_slc, k_win, v_win = nsa_shared_kv(
                h, c_act, kv_gain, w_kv_ada, b_kv_ada, w_kv,
                cmp_pe_k, cmp_w1_k, cmp_w2_k, cmp_pe_v, cmp_w1_v, cmp_w2_v, cos, sin)
        u = modulate(rmsnorm_2(h, attn_gain[layer]), a_shift, a_scale)
        if layer < N_A_LAYERS:
            mix = dsa_mixer(u, cos, sin, a_w_in[layer], a_w_out[layer])
        else:
            j = layer - N_A_LAYERS
            mix = nsa_mixer(u, cos, sin, kc, vc, k_slc, v_slc, k_win, v_win, b_w_q[j], b_w_out[j])
        h = h + a_gate[:, None, :] * mix
        u = modulate(rmsnorm_2(h, ffn_gain[layer]), f_shift, f_scale)
        if layer % 2 == 0:
            ff = swiglu_2(u, ffn_w_gate[layer // 2], ffn_w_up[layer // 2], ffn_w_down[layer // 2])
        else:
            m = layer // 2
            ff = moe_swiglu(u, moe_w_router[m], moe_w_gate[m], moe_w_up[m], moe_w_down[m])
        h = h + f_gate[:, None, :] * ff
    return rmsnorm_2(h, final_gain)


def setup_inputs(seed=0):
    out = dict(first_inputs(seed))
    for name, value in second_inputs(seed + 1).items():
        if name != "x":
            out[name + "_2"] = value
    return out


def reference(
    x, c, ctx, c_ctx, w_mod, b_mod, norm_mix_pre, norm_mix_post, norm_ffn_pre, norm_ffn_post,
    w_in, q_norm, k_norm, conv_w, conv_b, dt_bias_fwd, dt_bias_bwd, a_log_fwd, a_log_bwd,
    d_skip, ssd_norm, w_out, w_gate, w_up, w_down, c_2, positions_2, attn_gain_2, ffn_gain_2,
    w_ada_2, b_ada_2, a_w_in_2, a_w_out_2, b_w_q_2, b_w_out_2, kv_gain_2, w_kv_ada_2,
    b_kv_ada_2, w_kv_2, cmp_pe_k_2, cmp_w1_k_2, cmp_w2_k_2, cmp_pe_v_2, cmp_w1_v_2, cmp_w2_v_2,
    ffn_w_gate_2, ffn_w_up_2, ffn_w_down_2, moe_w_router_2, moe_w_gate_2, moe_w_up_2,
    moe_w_down_2, final_gain_2,
):
    x = first_block(
        x, c, ctx, c_ctx, w_mod, b_mod, norm_mix_pre, norm_mix_post, norm_ffn_pre,
        norm_ffn_post, w_in, q_norm, k_norm, conv_w, conv_b, dt_bias_fwd, dt_bias_bwd,
        a_log_fwd, a_log_bwd, d_skip, ssd_norm, w_out, w_gate, w_up, w_down,
    )
    return second_block(
        x, c_2, positions_2, attn_gain_2, ffn_gain_2, w_ada_2, b_ada_2, a_w_in_2, a_w_out_2,
        b_w_q_2, b_w_out_2, kv_gain_2, w_kv_ada_2, b_kv_ada_2, w_kv_2, cmp_pe_k_2, cmp_w1_k_2,
        cmp_w2_k_2, cmp_pe_v_2, cmp_w1_v_2, cmp_w2_v_2, ffn_w_gate_2, ffn_w_up_2, ffn_w_down_2,
        moe_w_router_2, moe_w_gate_2, moe_w_up_2, moe_w_down_2, final_gain_2,
    )


_drawn_inputs = setup_inputs


def setup_inputs(seed=0):
    import zlib

    import numpy as np

    out = dict(_drawn_inputs(seed))
    spreads = {}
    factors = {'q_norm': 8.0,
     'k_norm': 8.0,
     'conv_b': 3.399,
     'd_skip': 2.742,
     'attn_gain_2': 3.714,
     'b_ada_2': 3.697,
     'kv_gain_2': 8.0,
     'b_kv_ada_2': 8.0,
     'cmp_pe_k_2': 5.642}
    for name, (base, spread) in spreads.items():
        noise = np.random.default_rng([zlib.crc32(name.encode()), seed]).standard_normal(out[name].shape)
        drawn = base * np.exp(spread * noise) if base else spread * noise
        out[name] = jnp.asarray(drawn.astype(out[name].dtype))
    for name, factor in factors.items():
        out[name] = (out[name] * factor).astype(out[name].dtype)
    return out
```

```python
import math

import numpy as np
import concourse.bass as bass
from concourse import mybir

F32 = mybir.dt.float32
I32 = mybir.dt.int32
U32 = mybir.dt.uint32
ALU = mybir.AluOpType
ACT = mybir.ActivationFunctionType
AX = mybir.AxisListType.X

P = 128
D = 1024
KD = D // P
T = 256
NT = T // P
EPS = 1e-6
NEG = -1e30
TAKEN = -3e38
HD = 64
LAT, CTX = 0, 1
Q0, K0, V0, Z0, XBC0, DT0, IN1 = 0, 512, 640, 768, 1280, 2304, 2312
DK0, DV0, IQ0, IK0, IW0, IN2 = 1024, 1280, 1536, 2048, 2112, 2120
IN3 = 1072
TOPK = 64
NCMP, CMPL, CMPS = 15, 32, 16
FCOL = 256
NEXP = 8
FEXP = 3584
FDENSE = 2816
ROPE_THETA = 10000.0
IDX_SCALE = 8 ** -0.5 * 64 ** -0.5


class Engine:

    def __init__(self, nc, engine, name):
        self.e, self.sem, self.n, self.met = engine, nc.alloc_semaphore(name), 0, {}

    def now(self):
        return (self.sem, self.n)

    def wait(self, *marks):
        for sem, value in marks:
            if value > self.met.get(sem.name, 0):
                self.e.wait_ge(sem, value)
                self.met[sem.name] = value

    def op(self, f, *a, after=(), **k):
        self.wait(*after, self.now())
        return self.free(f, *a, **k)

    def free(self, f, *a, **k):
        f(*a, **k).then_inc(self.sem, 1)
        self.n += 1
        return self.now()


class Slot:

    def __init__(self, nc, name, ap):
        self.ap, self.sem, self.n, self.reader = ap, nc.alloc_semaphore(name), 0, None


def bc(ap, axis, n):
    shape = list(ap.shape)
    return ap.unsqueeze(axis).broadcast_to(shape[:axis] + [n] + shape[axis:])


def constants():
    p = np.arange(P)
    tri = (p[:, None] <= p[None, :]).astype(np.float32)
    c = {"ident": np.eye(P, dtype=np.float32), "ones": np.ones((P, P), np.float32)}
    c["tri"] = np.stack([tri, tri.T], 1)
    c["trineg"] = np.where(c["tri"] > 0, 0.0, NEG).astype(np.float32)
    pos = np.arange(T)
    fr = (np.float32(ROPE_THETA) ** (-np.arange(16, dtype=np.float32) / np.float32(16))).astype(np.float32)
    ang = np.concatenate([(pos // 64).astype(np.float32)[:, None] * fr, (pos % 64).astype(np.float32)[:, None] * fr], 1)
    cos, sin = np.cos(ang.astype(np.float64)), np.sin(ang.astype(np.float64))
    tab = np.stack([np.concatenate([cos, cos], 1), np.concatenate([-sin, sin], 1)], 1)
    c["axial"] = tab.reshape(NT, P, 2, HD).transpose(1, 0, 2, 3).astype(np.float32)
    inv = np.float32(1.0) / (np.float32(ROPE_THETA) ** (np.arange(0, HD, 2, dtype=np.float32) / np.float32(HD)))
    c["inv"] = np.broadcast_to(inv.astype(np.float32), (P, 32)).copy()
    key = np.arange(T)
    tok = (np.arange(NT)[None, :] * P + p[:, None])
    c["causal"] = np.where(key[None, None, :] <= tok[:, :, None], 0.0, NEG).astype(np.float32)
    end = np.arange(NCMP) * CMPS + CMPL - 1
    ok = end[None, None, :] <= tok[:, :, None]
    c["cmpmask"] = np.stack([np.where(ok, 0.0, NEG), ok], 2).astype(np.float32)
    c["iota8"] = np.broadcast_to(np.arange(8, dtype=np.float32), (P, 8)).copy()
    sel = np.zeros((2, 2, P), np.float32)
    sel[0, 0], sel[1, 1] = 1.0, 1.0
    c["sel"] = sel
    return c


def build(nc, i, out):
    sp = Engine(nc, nc.sync, "s_sp")
    pe = Engine(nc, nc.tensor, "s_pe")
    ve = Engine(nc, nc.vector, "s_ve")
    ac = Engine(nc, nc.scalar, "s_ac")
    v, a, t = nc.vector, nc.scalar, nc.tensor

    def sb(name, shape, dt=F32):
        return nc.alloc_sbuf_tensor(name, shape, dt)

    x = sb("x", [P, 2, NT, D])
    wide = sb("wide", [P, 6 * D])
    XT = sb("XT", [P, KD, T])
    cat = sb("cat", [P, NT, D])
    gates = sb("gates", [2, 2, D])
    grow = sb("grow", [P, D])
    prow = sb("prow", [P, 2, D])
    xn = sb("xn", [P, D])
    tmp = sb("tmp", [P, D])
    arena = sb("arena", [P, 11904])
    work = sb("work", [P, 3072])
    w_slots = [Slot(nc, f"s_w{s}", sb(f"wslot{s}", [P, 4096])) for s in range(2)]
    d_slots = [Slot(nc, f"s_d{s}", sb(f"dslot{s}", [P, 2048])) for s in range(2)]
    ring = {"w": 0, "d": 0}
    psum = nc.alloc_psum_tensor("psum", [P, 8, 512], F32)
    bank_free = [[] for _ in range(8)]

    const = {}
    s_par = nc.alloc_semaphore("s_par")
    par = [0]

    def param(dst, src):
        nc.scalar.dma_start(dst, src).then_inc(s_par, 16)
        par[0] += 16

    for name, arr in constants().items():
        flat = arr.reshape(arr.shape[0], -1)
        buf = sb("c_" + name, list(flat.shape))
        param(buf[:], nc.inline_tensor(flat, name="k_" + name).ap())
        const[name] = buf
    ident, ones = const["ident"], const["ones"]
    tri = const["tri"][:].rearrange("p (d i) -> p d i", d=2)
    trineg = const["trineg"][:].rearrange("p (d i) -> p d i", d=2)
    axial = const["axial"][:].rearrange("p (t c h) -> p t c h", t=NT, c=2)
    causal = const["causal"][:].rearrange("p (t k) -> p t k", t=NT)
    cmpmask = const["cmpmask"][:].rearrange("p (t c n) -> p t c n", t=NT, c=2)
    sel = const["sel"][:].rearrange("p (s q) -> p s q", s=2)

    ccol = sb("ccol", [P, 3, KD])
    cs = sb("cs", [P, KD, 4])
    gcol = sb("gcol", [P, 9, KD])
    for n, name in enumerate(["c", "c_ctx", "c_2"]):
        src = i[name] if name == "c_ctx" else i[name][0]
        param(ccol[:, n, :], src.rearrange("(p k) -> p k", k=KD))
    gains = [("norm_mix_pre", 0), ("norm_mix_pre", 1), ("norm_ffn_pre", 0), ("norm_ffn_pre", 1),
             ("attn_gain_2", 0), ("attn_gain_2", 1), ("ffn_gain_2", 0), ("ffn_gain_2", 1), ("kv_gain_2", None)]
    for n, (name, l) in enumerate(gains):
        src = i[name] if l is None else i[name][l]
        param(gcol[:, n, :], src.rearrange("(p k) -> p k", k=KD))
    qkn = sb("qkn", [P, 2, 2, HD])
    dtp = sb("dtp", [P, 2, 3, 2, 8])
    ssdn = sb("ssdn", [P, 512])
    for l in range(2):
        param(qkn[:, l, 0, :], i["q_norm"][l].partition_broadcast(P))
        param(qkn[:, l, 1, :], i["k_norm"][l].partition_broadcast(P))
        for d, way in enumerate(("fwd", "bwd")):
            param(dtp[:, l, 0, d, :], i["dt_bias_" + way][l].partition_broadcast(P))
            param(dtp[:, l, 1, d, :], i["a_log_" + way][l].partition_broadcast(P))
        param(dtp[:, l, 2, 0, :], i["d_skip"][l].partition_broadcast(P))
        stage = (xn, tmp)[l]
        param(stage[0:5, :], i["conv_w"][l])
        param(stage[5:6, :], i["conv_b"][l:l + 1])
    posi = sb("posi", [P, NT], I32)
    with nc.allow_non_contiguous_dma(reason="256 positions"):
        param(posi[:], i["positions_2"][0].rearrange("(t p) -> p t", p=P))
    wr = sb("wr", [P, KD, NEXP])
    param(wr[:], i["moe_w_router_2"][0].rearrange("(p k) e -> p k e", k=KD))
    w2 = sb("w2", [P, 2, 2, HD])
    pe16 = sb("pe16", [16, 2, P])
    for n, kv in enumerate("kv"):
        param(w2[:, n], i[f"cmp_w2_{kv}_2"].rearrange("(c p) d -> p c d", p=P))
        param(pe16[:, n, :], i[f"cmp_pe_{kv}_2"].rearrange("(c a) d -> c (a d)", a=2))
    for s, name in ((LAT, "x"), (CTX, "ctx")):
        param(x[:, s], i[name][0].rearrange("(t p) d -> p t d", p=P))
    convp = sb("convp", [P, 2, KD, 6])
    col = sb("col", [P, 2, 3, 2, KD])
    st = sb("st", [P, 64])
    rope2 = sb("rope2", [P, NT, 2, HD])
    params = (s_par, par[0])
    s_row = nc.alloc_semaphore("s_row")
    rows = [0]

    def meet():
        marks = [e.now() for e in (pe, ve, ac)]
        for e in (pe, ve, ac):
            e.wait(*marks)

    def bank_for_pe(b):
        pe.wait(*bank_free[b])
        return psum[:, b, :]

    def read_by(b, *marks):
        bank_free[b] = list(marks)

    def load_rows(*pairs):
        ac.wait(ve.now(), ac.now())
        for dst, src in pairs:
            nc.scalar.dma_start(dst, src).then_inc(s_row, 16)
            rows[0] += 16

    for e in (pe, ve, ac):
        e.wait(params)
    csv = cs[:].rearrange("p k c -> p c k")
    ac.op(a.activation, csv[:, 0:3, :], ccol[:], ACT.Silu)
    ac.op(a.activation, dtp[:, :, 1], dtp[:, :, 1], ACT.Exp)
    ve.op(v.tensor_scalar, dtp[:, :, 1], dtp[:, :, 1], -1.0, None, ALU.mult, after=[ac.now()])
    for l in range(2):
        bk = bank_for_pe(l)
        for k in range(KD):
            pe.free(t.transpose, bk[:, 6 * k:6 * k + 6], (xn, tmp)[l][0:6, k * P:(k + 1) * P], ident[0:6, 0:6])
        ve.op(v.tensor_copy, convp[:, l], bk[:, 0:48].rearrange("p (k j) -> p k j", j=6), after=[pe.now()])
        read_by(l, ve.now())
    pe2 = sb("pe2", [P, 2, 16])
    bk = bank_for_pe(2)
    for n in range(2):
        pe.free(t.transpose, bk[:, 16 * n:16 * n + 16], pe16[:, n, :], ident[0:16, 0:16])
    ve.op(v.tensor_copy, pe2[:], bk[:, 0:32].rearrange("p (a b) -> p a b", a=2), after=[pe.now()])
    read_by(2, ve.now())

    tw = work[:, 0:512].rearrange("p (n t f) -> p n t f", n=8, t=NT)
    ang, kk, r, rc, m = (tw[:, n] for n in range(5))
    c1, c2 = 6.28125, float(np.float32(0.0019350052))
    c3 = 2 * math.pi - c1 - c2
    magic = 12582912.0
    posf = st[:, 0:NT]
    ve.op(v.tensor_copy, posf, posi[:])
    for n in range(NT):
        ve.op(v.tensor_scalar, ang[:, n], const["inv"][:], posf[:, n:n + 1], None, ALU.mult)
    ve.op(v.tensor_scalar, kk, ang, 1 / (2 * math.pi), magic, ALU.mult, ALU.add)
    ve.op(v.tensor_scalar, kk, kk, magic, None, ALU.subtract)
    ve.op(v.scalar_tensor_tensor, r, kk, -c1, ang, ALU.mult, ALU.add)
    ve.op(v.scalar_tensor_tensor, r, kk, -c2, r, ALU.mult, ALU.add)
    ve.op(v.scalar_tensor_tensor, r, kk, -c3, r, ALU.mult, ALU.add)
    ve.op(v.tensor_scalar, rc, r, math.pi / 2, None, ALU.add)
    ve.op(v.tensor_scalar, m, rc, math.pi, -2 * math.pi, ALU.is_gt, ALU.mult)
    ve.op(v.tensor_tensor, rc, rc, m, ALU.add)
    lim = 3.1415925
    for s in (r, rc):
        ve.op(v.tensor_scalar, s, s, lim, -lim, ALU.min, ALU.max)
    ac.op(a.activation, rope2[:, :, 0, 0:32], rc, ACT.Sin, after=[ve.now()])
    ac.op(a.activation, rope2[:, :, 0, 32:64], rc, ACT.Sin)
    ac.op(a.activation, rope2[:, :, 1, 32:64], r, ACT.Sin)
    ve.op(v.tensor_scalar, rope2[:, :, 1, 0:32], rope2[:, :, 1, 32:64], -1.0, None, ALU.mult, after=[ac.now()])

    def w_slot():
        s = w_slots[ring["w"] % 2]
        ring["w"] += 1
        return s

    def fetch(slot, *pairs):
        if slot.reader:
            sp.wait(slot.reader)
        for dst, src in pairs:
            nc.sync.dma_start(dst, src).then_inc(slot.sem, 16)
            slot.n += 16
        return (slot.sem, slot.n)

    s_mod = nc.alloc_semaphore("s_mod")
    s_modv = nc.alloc_semaphore("s_modv")
    mods = [0]

    def modulation(w, b, tiles, first, m_rows):
        modrow = wide[0:m_rows, 0:tiles * 512]
        meet()
        load_rows((modrow, b.partition_broadcast(m_rows)))
        ve.wait((s_row, rows[0]))
        wv = w.rearrange("(p k) n -> p k n", k=KD)
        base = mods[0]
        slots = [w_slot(), w_slot()]

        def step(j, u, r):
            slot = slots[u]
            if r is None:
                if slot.reader:
                    sp.wait(slot.reader)
                landed = slot.n + 16
            else:
                nc.sync.wait_ge(s_mod, j + (base - 1))
                landed = r * 16 + (slot.n + 16)
            nc.sync.dma_start(slot.ap[:].rearrange("p (k n) -> p k n", k=KD),
                              wv[:, :, bass.ds(j * 512, 512)]).then_inc(slot.sem, 16)
            t.wait_ge(slot.sem, landed)
            if r is not None:
                t.wait_ge(s_modv, j + (base - 1))
            for k in range(KD):
                mm = t.matmul(psum[0:m_rows, 6 + u, :], cs[:, k, first:first + m_rows],
                              slot.ap[:, k * 512:(k + 1) * 512], start=(k == 0), stop=(k == KD - 1))
            mm.then_inc(s_mod, 1)
            v.wait_ge(s_mod, j + (base + 1))
            dst = wide[0:m_rows, bass.ds(j * 512, 512)]
            v.tensor_tensor(dst, dst, psum[0:m_rows, 6 + u, :], ALU.add).then_inc(s_modv, 1)

        for u in range(2):
            step(u, u, None)
            slots[u].n += 16
        if tiles > 2:
            with nc.Fori(0, tiles // 2 - 1) as r:
                for u in range(2):
                    step(r * 2 + (2 + u), u, r)
            for u in range(2):
                slots[u].n += 16 * (tiles // 2 - 1)
        mods[0] = base + tiles
        for u in range(2):
            slots[u].reader = (s_mod, mods[0])
        for e in (pe, ve, ac):
            e.wait((s_modv, mods[0]))

    def columns(dst, row0, m_rows):
        bk = bank_for_pe(5)
        for k in range(KD):
            pe.free(t.matmul, bk[:, k * m_rows:(k + 1) * m_rows], wide[0:m_rows, row0 + k:row0 + D:KD],
                    ident[0:m_rows, 0:m_rows], start=True, stop=True)
        for s in range(m_rows):
            ve.op(v.tensor_copy, dst(s), bk[:, s:KD * m_rows:m_rows], after=[pe.now()])
        read_by(5, ve.now())

    def norm_columns(which, row_shift, row_scale, gain, m_rows):
        columns(lambda s: col[:, s, which, 1, :], row_shift, m_rows)
        columns(lambda s: col[:, s, which, 0, :], row_scale, m_rows)
        for s in range(m_rows):
            c0 = col[:, s, which, 0, :]
            ve.op(v.scalar_tensor_tensor, c0, c0, 1.0, gcol[:, gain, :], ALU.add, ALU.mult)

    def layer_modulation(w, b, first, m_rows, mix_gain, ffn_gain):
        modulation(w, b, 12, first, m_rows)
        norm_columns(0, 0, D, mix_gain, m_rows)
        norm_columns(1, 3 * D, 4 * D, ffn_gain, m_rows)
        for n, row in enumerate((2 * D, 5 * D)):
            ve.op(v.tensor_copy, gates[0:m_rows, n, :], wide[0:m_rows, row:row + D])
        meet()

    def rstd(dst, n, width):
        m_ = st[:, 48:48 + width]
        ve.op(v.tensor_scalar, m_, dst, 1.0 / n, EPS, ALU.mult, ALU.add, after=[ac.now()])
        ac.op(a.activation, dst, m_, ACT.Sqrt, after=[ve.now()])
        ve.op(v.reciprocal, dst, dst, after=[ac.now()])
        ve.op(v.tensor_tensor, m_, m_, dst, ALU.mult)
        ve.op(v.tensor_tensor, m_, m_, dst, ALU.mult)
        ve.op(v.tensor_scalar, m_, m_, -0.5, 1.5, ALU.mult, ALU.add)
        ve.op(v.tensor_tensor, dst, dst, m_, ALU.mult)

    def normed_T(s, which):
        for tt in range(NT):
            ss = st[:, tt:tt + 1]
            ac.op(a.activation, xn[:], x[:, s, tt, :], ACT.Square, accum_out=ss, after=[ve.now(), pe.now()])
            rstd(ss, D, 1)
            ac.op(a.activation, xn[:], x[:, s, tt, :], ACT.Copy, scale=ss, after=[ve.now()])
            for half in range(2):
                bk = bank_for_pe(half)
                pe.wait(ac.now())
                for k in range(4):
                    pe.free(t.transpose, bk[:, k * P:(k + 1) * P], xn[:, 4 * half + k:D:KD], ident[:])
                for k in range(4):
                    kk_ = 4 * half + k
                    ve.op(v.tensor_scalar, XT[:, kk_, tt * P:(tt + 1) * P], bk[:, k * P:(k + 1) * P],
                          col[:, s, which, 0, kk_:kk_ + 1], col[:, s, which, 1, kk_:kk_ + 1],
                          ALU.mult, ALU.add, after=[pe.now()])
                read_by(half, ve.now())

    def cat_T():
        for tt in range(NT):
            for half in range(2):
                b = 4 + half
                bk = bank_for_pe(b)
                pe.wait(ve.now(), ac.now())
                for k in range(4):
                    pe.free(t.transpose, bk[:, k * P:(k + 1) * P], cat[:, tt, 4 * half + k:D:KD], ident[:])
                ve.op(v.tensor_copy, XT[:, 4 * half:4 * half + 4, tt * P:(tt + 1) * P],
                      bk.rearrange("p (k q) -> p k q", k=4), after=[pe.now()])
                read_by(b, ve.now())

    def product(w, c0, c1, sink, banks):
        wv = w.rearrange("(p k) n -> p k n", k=KD)
        nb = 0
        for c in range(c0, c1, 512):
            n = min(512, c1 - c)
            slot = w_slot()
            tile = slot.ap[:, 0:KD * n].rearrange("p (k n) -> p k n", k=KD)
            pe.wait(fetch(slot, (tile, wv[:, :, c:c + n])))
            pe.wait(ve.now())
            for tt in range(NT):
                b = banks[nb % len(banks)]
                nb += 1
                bk = bank_for_pe(b)
                for k in range(KD):
                    mm = t.matmul(bk[:, 0:n], XT[:, k, tt * P:(tt + 1) * P], tile[:, k, :],
                                  start=(k == 0), stop=(k == KD - 1))
                mm.then_inc(pe.sem, 1)
                pe.n += 1
                sink(tt, c, n, b)
            slot.reader = pe.now()

    def keep_in(buf):
        def sink(tt, c, n, b):
            if tt == 0:
                ac.op(a.activation, buf[:, tt, c:c + n], psum[:, b, 0:n], ACT.Copy, after=[pe.now()])
                read_by(b, ac.now())
            else:
                ve.op(v.tensor_copy, buf[:, tt, c:c + n], psum[:, b, 0:n], after=[pe.now()])
                read_by(b, ve.now())
        return sink

    def gate_row(s, n):
        for h in range(2):
            bk = bank_for_pe(6 + h)
            pe.wait(ve.now())
            pe.free(t.matmul, bk, sel[0:2, s, :] if s is not None else ones[0:1, :],
                    gates[0:2, n, h * 512:(h + 1) * 512] if s is not None else gates[0:1, n, h * 512:(h + 1) * 512],
                    start=True, stop=True)
            ve.op(v.tensor_copy, grow[:, h * 512:(h + 1) * 512], bk, after=[pe.now()])
            read_by(6 + h, ve.now())

    def add_normed(s, n):
        gate_row(s, n)
        ve.op(v.tensor_tensor, grow[:], grow[:], prow[:, n, :], ALU.mult, after=[(s_row, rows[0])])
        for tt in range(NT):
            acc = psum[:, 2 * tt:2 * tt + 2, :].rearrange("p b n -> p (b n)")
            ss = st[:, tt:tt + 1]
            ac.op(a.activation, xn[:], acc, ACT.Square, accum_out=ss, after=[ve.now(), pe.now()])
            rstd(ss, D, 1)
            ve.op(v.scalar_tensor_tensor, tmp[:], acc, ss, grow[:], ALU.mult, ALU.mult, after=[pe.now()])
            for b in (2 * tt, 2 * tt + 1):
                read_by(b, ve.now(), ac.now())
            ve.op(v.tensor_tensor, x[:, s, tt, :], x[:, s, tt, :], tmp[:], ALU.add)

    def add_gated(n, source):
        gate_row(None, n)
        for tt in range(NT):
            ve.op(v.tensor_tensor, tmp[:], source(tt), grow[:], ALU.mult, after=[pe.now()])
            for b in (2 * tt, 2 * tt + 1):
                read_by(b, ve.now())
            ve.op(v.tensor_tensor, x[:, LAT, tt, :], x[:, LAT, tt, :], tmp[:], ALU.add)

    def project_out(w):
        cat_T()
        product(w, 0, D, lambda tt, c, n, b: None, [0, 2, 1, 3])

    def acc_tile(tt):
        return psum[:, 2 * tt:2 * tt + 2, :].rearrange("p b n -> p (b n)")

    names = ["gu", "silu", "h", "tr", "ev", "dn", "acc"]
    fs = {n: nc.alloc_semaphore("s_f" + n) for n in names}
    fn = dict.fromkeys(names, 0)
    sg = work[:, 0:512].rearrange("p (t n) -> p t n", t=NT)
    hb = work[:, 512:1024].rearrange("p (t n) -> p t n", t=NT)
    hT = work[:, 1024:2048].rearrange("p (a k q) -> p a k q", a=2, k=2)
    moe_y = cat[:]

    def ffn(steps, gate_up, down, experts=None, after_expert=None):
        meet()
        base = dict(fn)
        ws, ds = [w_slot(), w_slot()], d_slots[:]
        if ring["d"] % 2:
            ds.reverse()
        wn, dn_ = [s.n for s in ws], [s.n for s in ds]
        for s in ws + ds:
            if s.reader:
                sp.wait(s.reader)

        def hold(engine, sem, value):
            if not isinstance(value, int) or value > 0:
                engine.wait_ge(sem, value)

        def run(e, count):
            def at(name, per, plus):
                return e * (steps * per) + (base[name] + plus) if experts else base[name] + plus

            def value(name, per, i_, plus):
                return i_ * per + at(name, per, plus)

            def landed(which, n0, u, i_):
                per = 32 if which == "w" else 16
                first = (i_ - u) * (per // 2) + (n0[u] + per)
                return first + e * (steps * per // 2) if experts else first

            def load(i_, u):
                hold(nc.sync, fs["gu"], value("gu", 2, i_, -2))
                tile = ws[u].ap[:].rearrange("p (k c n) -> p k c n", k=KD, c=2)
                for c in range(2):
                    nc.sync.dma_start(tile[:, :, c, :], gate_up(c, e, i_)).then_inc(ws[u].sem, 16)
                hold(nc.sync, fs["dn"], value("dn", 1, i_, -1))
                nc.sync.dma_start(ds[u].ap[:].rearrange("p (k n) -> p k n", k=2),
                                  down(e, i_)).then_inc(ds[u].sem, 16)

            def up(i_, u, tt, peeled=False):
                hold(t, ws[u].sem, landed("w", wn, u, i_))
                hold(t, fs["h"], value("h", 2, i_, tt - 1))
                for k in range(KD):
                    mm = t.matmul(psum[:, 4 + tt, :], XT[:, k, tt * P:(tt + 1) * P],
                                  ws[u].ap[:, k * 512:(k + 1) * 512], start=(k == 0), stop=(k == KD - 1))
                mm.then_inc(fs["gu"], 1)
                hold(a, fs["gu"], value("gu", 2, i_, tt + 1))
                hold(a, fs["h"], value("h", 2, i_, tt - 1))
                a.activation(sg[:, tt, :], psum[:, 4 + tt, 0:FCOL], ACT.Silu).then_inc(fs["silu"], 1)

            def hidden(i_, tt):
                hold(v, fs["silu"], value("silu", 2, i_, tt + 1))
                hold(v, fs["tr"], value("tr", 2, i_, tt - 1))
                v.tensor_tensor(hb[:, tt, :], sg[:, tt, :], psum[:, 4 + tt, FCOL:512],
                                ALU.mult).then_inc(fs["h"], 1)

            def turn(i_, u, tt):
                hold(t, fs["h"], value("h", 2, i_, tt + 1))
                hold(t, fs["ev"], value("ev", 2, i_, tt - 1))
                for k in range(2):
                    mm = t.transpose(psum[:, 6 + tt, k * P:(k + 1) * P], hb[:, tt, k:FCOL:2], ident[:])
                mm.then_inc(fs["tr"], 1)
                hold(v, fs["tr"], value("tr", 2, i_, tt + 1))
                hold(v, fs["dn"], value("dn", 1, i_, -1))
                v.tensor_copy(hT[:, u, :, tt * P:(tt + 1) * P],
                              psum[:, 6 + tt, 0:256].rearrange("p (k q) -> p k q", k=2)).then_inc(fs["ev"], 1)

            def downs(i_, u, start, stop):
                hold(t, ds[u].sem, landed("d", dn_, u, i_))
                hold(t, fs["ev"], value("ev", 2, i_, 2))
                hold(t, fs["acc"], e + base["acc"] if experts else base["acc"])
                for tt in range(NT):
                    for k in range(2):
                        for h in range(2):
                            mm = t.matmul(psum[:, 2 * tt + h, :], hT[:, u, k, tt * P:(tt + 1) * P],
                                          ds[u].ap[:, k * D + h * 512:k * D + (h + 1) * 512],
                                          start=start and k == 0, stop=stop and k == 1)
                mm.then_inc(fs["dn"], 1)

            def step(i_, u, first=False):
                load(i_, u)
                up(i_, u, 0)
                if not first:
                    turn(i_ - 1, 1 - u, 1)
                hidden(i_, 0)
                up(i_, u, 1)
                hidden(i_, 1)
                turn(i_, u, 0)
                return

            step(0, 0, first=True)
            step(1, 1)
            downs(0, 0, True, False)
            pairs = (steps - 2) // 2
            with nc.Fori(0, pairs) as r:
                for u in range(2):
                    step(r * 2 + (2 + u), u)
                    downs(r * 2 + (1 + u), 1 - u, False, False)
            last = 2 + 2 * pairs
            if last < steps:
                step(last, 0)
                downs(last - 1, 1, False, False)
                last += 1
            turn(steps - 1, (steps - 1) % 2, 1)
            downs(steps - 1, (steps - 1) % 2, False, True)
            if after_expert:
                after_expert(e, e * steps + (base["dn"] + steps))

        if experts:
            with nc.Fori(0, experts) as e:
                run(e, experts)
        else:
            run(0, 1)
        total = (experts or 1) * steps
        for n in ("gu", "silu", "h", "tr", "ev"):
            fn[n] += 2 * total
        fn["dn"] += total
        fn["acc"] += experts or 0
        if total % 2:
            ring["w"] += 1
            ring["d"] += 1
        for u in range(2):
            cnt = (total + 1 - u) // 2
            ws[u].n += 32 * cnt
            ds[u].n += 16 * cnt
            ws[u].reader = (fs["gu"], fn["gu"])
            ds[u].reader = (fs["dn"], fn["dn"])
        for e_ in (pe, ve, ac):
            e_.wait((fs["dn"], fn["dn"]), (fs["ev"], fn["ev"]))
            if experts:
                e_.wait((fs["acc"], fn["acc"]))

    def dense(wg, wu, wd):
        gv = [w.rearrange("(p k) n -> p k n", k=KD) for w in (wg, wu)]
        dv = wd.rearrange("(i p k) n -> p i k n", p=P, k=2)
        ffn(FDENSE // FCOL, lambda c, e, i_: gv[c][:, :, bass.ds(i_ * FCOL, FCOL)],
            lambda e, i_: dv[:, bass.ds(i_, 1)].rearrange("p i k n -> p (i k) n"))

    def heads_T(src, tt, heads, dst, offset):
        for h0 in range(0, heads, 4):
            n = min(4, heads - h0)
            b = 4 + (h0 // 4) % 2
            bk = bank_for_pe(b)
            pe.wait(ve.now(), ac.now())
            for h in range(n):
                pe.free(t.transpose, bk[0:HD, h * P:(h + 1) * P], src[:, (h0 + h) * HD:(h0 + h + 1) * HD], ident[:])
            ac.op(a.activation, dst[0:HD, h0:h0 + n, offset + tt * P:offset + (tt + 1) * P],
                  bk[0:HD, 0:n * P].rearrange("p (h q) -> p h q", h=n), ACT.Copy, after=[pe.now()])
            read_by(b, ac.now())

    def rope(src, heads, cos, sin):
        d = src.rearrange("p (h f) -> p h f", f=HD)
        o = tmp[:, 0:heads * HD].rearrange("p (h f) -> p h f", f=HD)
        ve.op(v.tensor_tensor, o[:, :, 0:32], d[:, :, 32:64], bc(sin[:, 0:32], 1, heads), ALU.mult, after=[ac.now(), pe.now()])
        ve.op(v.tensor_tensor, o[:, :, 32:64], d[:, :, 0:32], bc(sin[:, 32:64], 1, heads), ALU.mult)
        ve.op(v.tensor_tensor, d, d, bc(cos, 1, heads), ALU.mult)
        ve.op(v.tensor_tensor, d, d, o, ALU.add)

    Sb = work[:, 0:1024].rearrange("p (a n) -> p a n", a=2)
    Pm = work[:, 1024:2048].rearrange("p (a n) -> p a n", a=2)
    PT = work[:, 2048:3072].rearrange("p (a n) -> p a n", a=2)
    msum = st[:, 16:48]

    def attention(heads, per_kv, qT, kT, keys, vals, bias, finish):
        units = [(tt, h) for tt in range(NT) for h in range(heads)]
        marks = {}

        def scores(u):
            tt, h = units[u]
            nk, par_ = keys(tt), u % 2
            bk = bank_for_pe(par_)
            pe.wait(ac.now(), ve.now())
            pe.free(t.matmul, bk[:, 0:nk], qT[0:HD, h, tt * P:(tt + 1) * P], kT[0:HD, h // per_kv, 0:nk],
                    start=True, stop=True)
            mx = msum[:, par_:par_ + 1]
            sm = msum[:, 2 + 8 * ((u // 8) % 2) + u % 8:][:, 0:1]
            if bias is None:
                src = bk[:, 0:nk]
                ve.op(v.tensor_reduce, mx, src, AX, ALU.max, after=[pe.now(), ac.now()])
                ve.op(v.tensor_scalar, mx, mx, -0.125, None, ALU.mult)
                m_ = ac.op(a.activation, Pm[:, par_, 0:nk], src, ACT.Exp, bias=mx, scale=0.125,
                           accum_out=sm, after=[ve.now()])
                read_by(par_, m_, ve.now())
            else:
                src = Sb[:, par_, 0:nk]
                ve.op(v.scalar_tensor_tensor, src, bk[:, 0:nk], 0.125, bias(tt)[:, 0:nk], ALU.mult, ALU.add,
                      after=[pe.now(), ac.now()])
                read_by(par_, ve.now())
                ve.op(v.tensor_reduce, mx, src, AX, ALU.max, negate=True)
                m_ = ac.op(a.activation, Pm[:, par_, 0:nk], src, ACT.Exp, bias=mx, scale=1.0,
                           accum_out=sm, after=[ve.now()])
            marks[u] = m_

        def values(u):
            tt, h = units[u]
            nk, par_ = keys(tt), u % 2
            bk = bank_for_pe(2 + par_)
            pe.wait(marks[u])
            for b in range(nk // P):
                pe.free(t.transpose, bk[:, b * P:(b + 1) * P], Pm[:, par_, b * P:(b + 1) * P], ident[:])
            ve.op(v.tensor_copy, PT[:, par_, 0:nk], bk[:, 0:nk], after=[pe.now()])
            read_by(2 + par_, ve.now())
            ob = 4 + (u // 8) % 2
            o = bank_for_pe(ob)
            pe.wait(ve.now())
            for b in range(nk // P):
                mm = t.matmul(o[:, (h % 8) * HD:(h % 8 + 1) * HD], PT[:, par_, b * P:(b + 1) * P],
                              vals(h // per_kv, b), start=(b == 0), stop=(b == nk // P - 1))
            mm.then_inc(pe.sem, 1)
            pe.n += 1
            if h % 8 == 7:
                sums = msum[:, 2 + 8 * ((u // 8) % 2):][:, 0:8]
                ve.op(v.reciprocal, sums, sums, after=[pe.now(), ac.now()])
                finish(tt, h - 7, o.rearrange("p (h f) -> p h f", f=HD), sums)
                read_by(ob, ve.now())

        for u in range(len(units) + 1):
            if u < len(units):
                scores(u)
            if u >= 1:
                values(u - 1)

    def into_cat(tt, h0, o, inv):
        ve.op(v.tensor_tensor, cat[:, tt, h0 * HD:(h0 + 8) * HD].rearrange("p (h f) -> p h f", f=HD),
              o, bc(inv, 2, HD), ALU.mult)

    proj = wide[:, 0:NT * IN1].rearrange("p (t n) -> p t n", t=NT)
    off = [0]

    def cut(n):
        off[0] += n
        return arena[:, off[0] - n:off[0]]

    qT = cut(2048).rearrange("p (h q) -> p h q", h=8)
    kT = cut(1024).rearrange("p (g q) -> p g q", g=2)
    vctx = cut(256).rearrange("p (t n) -> p t n", t=NT)
    xbcT = cut(2080).rearrange("p (b q) -> p b q", b=8)
    convT = cut(2048).rearrange("p (b q) -> p b q", b=8)
    xtok = cut(1024).rearrange("p (t n) -> p t n", t=NT)
    btok = cut(512).rearrange("p (t n) -> p t n", t=NT)
    smat = cut(512).rearrange("p (t g q) -> p t g q", t=NT, g=2)
    state = cut(1024).rearrange("p (d n) -> p d n", d=2)
    xdt = cut(512)
    xde = cut(512)
    dts = cut(256).rearrange("p (n t d h) -> p n t d h", n=8, t=NT, d=2)
    ex = cut(64)
    dec = work[:, 0:1024].rearrange("p (h q) -> p h q", h=8)
    dtB = work[:, 1024:2048].rearrange("p (h q) -> p h q", h=8)

    def ssd(l, s, with_y):
        meet()
        ve.op(v.memset, xbcT[:, :, 0:2], 0.0)
        ve.op(v.memset, xbcT[:, :, 258:260], 0.0)
        for b2 in range(0, 8, 2):
            b = (b2 // 2) % 2
            bk = bank_for_pe(b)
            for n in range(4):
                blk, tt = b2 + n // 2, n % 2
                pe.free(t.transpose, bk[:, n * P:(n + 1) * P], proj[:, tt, XBC0 + blk * P:XBC0 + (blk + 1) * P], ident[:])
            ac.op(a.activation, xbcT[:, b2:b2 + 2, 2:258], bk.rearrange("p (b q) -> p b q", b=2), ACT.Copy, after=[pe.now()])
            read_by(b, ac.now())
        for b in range(8):
            acc_ = convT[:, b, :]
            ve.op(v.tensor_scalar, acc_, xbcT[:, b, 0:T], convp[:, l, b, 0:1], None, ALU.mult, after=[ac.now()])
            for j in range(1, 5):
                ve.op(v.scalar_tensor_tensor, acc_, xbcT[:, b, j:j + T], convp[:, l, b, j:j + 1], acc_, ALU.mult, ALU.add)
            ac.op(a.activation, acc_, acc_, ACT.Silu, bias=convp[:, l, b, 5:6], after=[ve.now()])
        for tt in range(NT):
            bk = bank_for_pe(2)
            pe.wait(ac.now())
            for b in range(4):
                pe.free(t.transpose, bk[:, b * P:(b + 1) * P], convT[:, b, tt * P:(tt + 1) * P], ident[:])
            ve.op(v.tensor_copy, xtok[:, tt, :], bk, after=[pe.now()])
            read_by(2, ve.now())
            bk = bank_for_pe(3)
            for b in range(2):
                pe.free(t.transpose, bk[:, b * P:(b + 1) * P], convT[:, 4 + b, tt * P:(tt + 1) * P], ident[:])
            ve.op(v.tensor_copy, btok[:, tt, :], bk[:, 0:256], after=[pe.now()])
            read_by(3, ve.now())
        xx, e_, u_, ln, m_, dt, dtA, sp_ = (dts[:, n] for n in range(8))
        for d in range(2):
            ve.op(v.tensor_tensor, xx[:, :, d, :], proj[:, :, DT0:DT0 + 8], bc(dtp[:, l, 0, d, :], 1, NT), ALU.add)
        ve.op(v.tensor_scalar, e_, xx, -1.0, None, ALU.mult)
        ve.op(v.tensor_tensor, e_, e_, xx, ALU.min)
        ac.op(a.activation, e_, e_, ACT.Exp, after=[ve.now()])
        ve.op(v.tensor_scalar, u_, e_, 1.0, None, ALU.add, after=[ac.now()])
        ac.op(a.activation, ln, u_, ACT.Ln, after=[ve.now()])
        ve.op(v.tensor_scalar, u_, u_, 1.0, None, ALU.subtract, after=[ac.now()])
        ve.op(v.tensor_scalar, m_, u_, 0.0, None, ALU.is_equal)
        ve.op(v.tensor_tensor, ln, ln, m_, ALU.add)
        ve.op(v.tensor_tensor, ln, ln, e_, ALU.mult)
        ve.op(v.tensor_tensor, u_, u_, m_, ALU.add)
        ve.op(v.reciprocal, u_, u_)
        ve.op(v.tensor_tensor, ln, ln, u_, ALU.mult)
        ve.op(v.tensor_scalar, xx, xx, 0.0, None, ALU.max)
        ve.op(v.tensor_tensor, dt, xx, ln, ALU.add)
        for d in range(2):
            ve.op(v.tensor_tensor, dtA[:, :, d, :], dt[:, :, d, :], bc(dtp[:, l, 1, d, :], 1, NT), ALU.mult)
        if with_y:
            bk = bank_for_pe(2)
            pe.wait(ac.now())
            for n in range(4):
                tt, g = n // 2, n % 2
                pe.free(t.matmul, bk[:, n * P:(n + 1) * P], convT[:, 4 + g, tt * P:(tt + 1) * P],
                        convT[:, 6 + g, tt * P:(tt + 1) * P], start=True, stop=True)
            ve.op(v.tensor_copy, smat, bk.rearrange("p (t g q) -> p t g q", t=2, g=2), after=[pe.now()])
            read_by(2, ve.now())
        for d in range(2):
            for n, tt in enumerate((0, 1) if d == 0 else (1, 0)):
                fresh = s == CTX and n == 0
                last = s == LAT and n == 1
                dA, dtc = dtA[:, tt, d, :], dt[:, tt, d, :]
                bk = bank_for_pe(0)
                pe.wait(ve.now())
                pe.free(t.matmul, bk[:, 0:8], tri[:, d, :], dA, start=True, stop=True)
                pe.free(t.matmul, bk[:, 8:16], ones[:], dA, start=True, stop=True)
                acum, tot, dte, ea, cd = (ex[:, 8 * j:8 * j + 8] for j in range(5))
                ve.op(v.tensor_copy, ex[:, 0:16], bk[:, 0:16], after=[pe.now(), ac.now()])
                read_by(0, ve.now())
                ve.op(v.tensor_tensor, dte, tot, acum, ALU.subtract)
                ac.op(a.activation, dte, dte, ACT.Exp, after=[ve.now()])
                ac.op(a.activation, ea, acum, ACT.Exp)
                ac.op(a.activation, cd, tot, ACT.Exp)
                xh = xtok[:, tt, :].rearrange("p (h f) -> p h f", f=HD)
                ve.op(v.tensor_tensor, xdt.rearrange("p (h f) -> p h f", f=HD), xh, bc(dtc, 2, HD), ALU.mult)
                ve.op(v.tensor_tensor, xde.rearrange("p (h f) -> p h f", f=HD), xdt.rearrange("p (h f) -> p h f", f=HD),
                      bc(dte, 2, HD), ALU.mult, after=[ac.now()])
                if with_y:
                    ve.op(v.tensor_copy, dtB, bc(dA, 2, P))
                    pe.wait(*bank_free[6], *bank_free[7], ve.now())
                    for h in range(8):
                        pe.free(t.matmul, psum[:, 6 + h // 4, (h % 4) * P:(h % 4 + 1) * P], dtB[:, h, :], tri[:, d, :],
                                start=True, stop=True)
                    pair = psum[:, 6:8, :].rearrange("p b (h q) -> p (b h) q", q=P)
                    ve.op(v.tensor_tensor, dec, pair, bc(acum, 2, P), ALU.subtract, after=[pe.now()])
                    read_by(6, ve.now())
                    read_by(7, ve.now())
                    ve.op(v.tensor_tensor, dec, dec, bc(trineg[:, d, :], 1, 8), ALU.add)
                    ac.op(a.activation, dec, dec, ACT.Exp, after=[ve.now()])
                    for g in range(2):
                        ve.op(v.tensor_tensor, dec[:, 4 * g:4 * g + 4, :], dec[:, 4 * g:4 * g + 4, :],
                              bc(smat[:, tt, g, :], 1, 4), ALU.mult, after=[ac.now()])
                    o = bank_for_pe(4)
                    pe.wait(ve.now())
                    for h in range(8):
                        pe.free(t.matmul, o[:, h * HD:(h + 1) * HD], dec[:, h, :], xdt[:, h * HD:(h + 1) * HD],
                                start=True, stop=True)
                    y = cat[:, tt, 512:1024]
                    if d == 0:
                        ve.op(v.tensor_copy, y, o, after=[pe.now()])
                    else:
                        ve.op(v.tensor_tensor, y, y, o, ALU.add, after=[pe.now()])
                    read_by(4, ve.now())
                    if not fresh:
                        o = bank_for_pe(5)
                        for g in range(2):
                            pe.free(t.matmul, o[:, g * 256:(g + 1) * 256], convT[:, 6 + g, tt * P:(tt + 1) * P],
                                    state[:, d, g * 256:(g + 1) * 256], start=True, stop=True)
                        th = tmp[:, 0:512]
                        ve.op(v.tensor_tensor, th.rearrange("p (h f) -> p h f", f=HD),
                              o.rearrange("p (h f) -> p h f", f=HD), bc(ea, 2, HD), ALU.mult, after=[pe.now(), ac.now()])
                        read_by(5, ve.now())
                        ve.op(v.tensor_tensor, y, y, th, ALU.add)
                if not last:
                    bk = bank_for_pe(1)
                    pe.wait(ve.now())
                    for g in range(2):
                        pe.free(t.matmul, bk[:, g * 256:(g + 1) * 256], btok[:, tt, g * P:(g + 1) * P],
                                xde[:, g * 256:(g + 1) * 256], start=True, stop=True)
                    sh_ = state[:, d, :].rearrange("p (h f) -> p h f", f=HD)
                    if fresh:
                        ve.op(v.tensor_copy, state[:, d, :], bk, after=[pe.now()])
                    else:
                        ve.op(v.tensor_tensor, sh_, sh_, bc(cd, 2, HD), ALU.mult, after=[pe.now(), ac.now()])
                        ve.op(v.tensor_tensor, state[:, d, :], state[:, d, :], bk, ALU.add)
                    read_by(1, ve.now())
        if with_y:
            for tt in range(NT):
                y, th = cat[:, tt, 512:1024], tmp[:, 0:512]
                ve.op(v.tensor_tensor, th.rearrange("p (h f) -> p h f", f=HD),
                      xtok[:, tt, :].rearrange("p (h f) -> p h f", f=HD), bc(dtp[:, l, 2, 0, :], 2, HD), ALU.mult, after=[ac.now()])
                ve.op(v.tensor_tensor, y, y, th, ALU.add)
                ac.op(a.activation, xn[:, 0:512], proj[:, tt, Z0:Z0 + 512], ACT.Silu, after=[ve.now()])
                ve.op(v.tensor_tensor, y, y, xn[:, 0:512], ALU.mult, after=[ac.now()])
                ss = st[:, tt:tt + 1]
                ac.op(a.activation, xn[:, 0:512], y, ACT.Square, accum_out=ss, after=[ve.now()])
                rstd(ss, 512, 1)
                ve.op(v.scalar_tensor_tensor, y, y, ss, ssdn[:], ALU.mult, ALU.mult, after=[(s_row, rows[0])])

    def mixer_in(l, s):
        normed_T(s, 0)
        product(i["w_in"][l], 0, IN1, keep_in(proj), [0, 1, 2, 3])
        for tt in range(NT):
            qk = proj[:, tt, 0:640]
            q3 = qk.rearrange("p (h f) -> p h f", f=HD)
            sq = tmp[:, 0:640]
            ve.op(v.tensor_tensor, sq, qk, qk, ALU.mult, after=[ac.now()])
            ss = st[:, 0:10]
            ve.op(v.tensor_reduce, ss, sq.rearrange("p (h f) -> p h f", f=HD), AX, ALU.add)
            rstd(ss, HD, 10)
            ve.op(v.tensor_tensor, q3, q3, bc(ss, 2, HD), ALU.mult)
            ve.op(v.tensor_tensor, q3[:, 0:8], q3[:, 0:8], bc(qkn[:, l, 0, :], 1, 8), ALU.mult)
            ve.op(v.tensor_tensor, q3[:, 8:10], q3[:, 8:10], bc(qkn[:, l, 1, :], 1, 2), ALU.mult)
            if s == LAT:
                rope(qk, 10, axial[:, tt, 0, :], axial[:, tt, 1, :])
            heads_T(proj[:, tt, 0:512], tt, 8, qT, 0)
            heads_T(proj[:, tt, 512:640], tt, 2, kT, 0 if s == CTX else T)
            if s == CTX:
                ve.op(v.tensor_copy, vctx[:, tt, :], proj[:, tt, V0:V0 + 128], after=[ac.now(), pe.now()])

    def mixer(l, s, with_out):
        mixer_in(l, s)
        if with_out:
            nkeys = T if s == CTX else 2 * T

            def vals(g, b):
                if b < NT:
                    return vctx[:, b, g * HD:(g + 1) * HD]
                return proj[:, b - NT, V0 + g * HD:V0 + (g + 1) * HD]
            attention(8, 4, qT, kT, lambda tt: nkeys, vals, None, into_cat)
        ssd(l, s, with_out)
        if with_out:
            project_out(i["w_out"][l])
            add_normed(s, 0)

    for l in range(2):
        layer_modulation(i["w_mod"][l], i["b_mod"][l], 0, 2, l, 2 + l)
        load_rows((ssdn[:], i["ssd_norm"][l].partition_broadcast(P)),
                  (prow[:, 0, :], i["norm_mix_post"][l].partition_broadcast(P)),
                  (prow[:, 1, :], i["norm_ffn_post"][l].partition_broadcast(P)))
        for s in (CTX, LAT):
            mixer(l, s, s == LAT or l == 0)
        for s in ((CTX, LAT) if l == 0 else (LAT,)):
            normed_T(s, 1)
            dense(i["w_gate"][l], i["w_up"][l], i["w_down"][l])
            add_normed(s, 1)

    layer_modulation(i["w_ada_2"][0], i["b_ada_2"][0], 2, 1, 4, 6)
    off[0] = 0
    proj2 = wide[:, 0:NT * IN2].rearrange("p (t n) -> p t n", t=NT)
    qT2 = cut(4096).rearrange("p (h q) -> p h q", h=16)
    keep = off[0]
    kT2 = cut(1024).rearrange("p (g q) -> p g q", g=4)
    iqT = cut(2304).rearrange("p (h q) -> p h q", h=9)
    score = cut(512).rearrange("p (t k) -> p t k", t=NT)
    left = cut(256)
    rel = cut(512).rearrange("p (a k) -> p a k", a=2)
    m8 = cut(8)
    keys2 = lambda tt: (tt + 1) * P

    normed_T(LAT, 0)
    product(i["a_w_in_2"][0], 0, IN2, keep_in(proj2), [0, 1, 2, 3])
    for tt in range(NT):
        cos, sin = rope2[:, tt, 0, :], rope2[:, tt, 1, :]
        rope(proj2[:, tt, 0:1024], 16, cos, sin)
        rope(proj2[:, tt, DK0:DV0], 4, cos, sin)
        rope(proj2[:, tt, IQ0:IW0], 9, cos, sin)
        heads_T(proj2[:, tt, 0:1024], tt, 16, qT2, 0)
        heads_T(proj2[:, tt, DK0:DV0], tt, 4, kT2, 0)
        heads_T(proj2[:, tt, IQ0:IW0], tt, 9, iqT, 0)
        ve.op(v.tensor_scalar, proj2[:, tt, IW0:IN2], proj2[:, tt, IW0:IN2], IDX_SCALE, None, ALU.mult)
    for tt in range(NT):
        nk = keys2(tt)
        sc = score[:, tt, 0:nk]
        for h in range(8):
            u = h % 2
            bk = bank_for_pe(u)
            pe.wait(ac.now())
            pe.free(t.matmul, bk[:, 0:nk], iqT[0:HD, h, tt * P:(tt + 1) * P], iqT[0:HD, 8, 0:nk], start=True, stop=True)
            ac.op(a.activation, rel[:, u, 0:nk], bk[:, 0:nk], ACT.Relu, after=[pe.now(), ve.now()])
            read_by(u, ac.now())
            wi = proj2[:, tt, IW0 + h:IW0 + h + 1]
            if h == 0:
                ve.op(v.tensor_scalar, sc, rel[:, u, 0:nk], wi, None, ALU.mult, after=[ac.now()])
            else:
                ve.op(v.scalar_tensor_tensor, sc, rel[:, u, 0:nk], wi, sc, ALU.mult, ALU.add, after=[ac.now()])
        ve.op(v.tensor_tensor, sc, sc, causal[:, tt, 0:nk], ALU.add)
        ve.op(v.tensor_copy, left[:, 0:nk], sc)
        for _ in range(TOPK // 8):
            ve.op(v.max, m8, left[:, 0:nk])
            ve.op(v.match_replace, left[:, 0:nk], m8, left[:, 0:nk], TAKEN)
        ve.op(v.tensor_scalar, sc, left[:, 0:nk], TAKEN / 2, NEG, ALU.is_gt, ALU.mult)
        ve.op(v.tensor_tensor, sc, sc, causal[:, tt, 0:nk], ALU.add)
    meet()
    attention(16, 4, qT2, kT2, keys2, lambda g, b: proj2[:, b, DV0 + g * HD:DV0 + (g + 1) * HD],
              lambda tt: score[:, tt, :], into_cat)
    project_out(i["a_w_out_2"][0])
    add_gated(0, acc_tile)
    normed_T(LAT, 1)
    dense(i["ffn_w_gate_2"][0], i["ffn_w_up_2"][0], i["ffn_w_down_2"][0])
    add_gated(1, acc_tile)

    modulation(i["w_kv_ada_2"], i["b_kv_ada_2"], 4, 2, 1)
    norm_columns(2, 0, D, 8, 1)
    meet()
    layer_modulation(i["w_ada_2"][1], i["b_ada_2"][1], 2, 1, 5, 7)
    off[0] = keep
    kv = wide[:, 0:NT * 1536].rearrange("p (t n) -> p t n", t=NT)
    projq = wide[:, 3072:3072 + NT * IN3].rearrange("p (t n) -> p t n", t=NT)
    ksT = cut(1024).rearrange("p (g q) -> p g q", g=4)
    kwT = cut(1024).rearrange("p (g q) -> p g q", g=4)
    dup = cut(512).rearrange("p (h a f) -> p h a f", h=4, a=2)
    win = cut(1024).rearrange("p (h q) -> p h q", h=4)
    xw = cut(16 * 60).rearrange("p (c h n) -> p c h n", c=16, h=4)
    hid = cut(256)
    hidT = cut(120).rearrange("p (c r) -> p c r", c=2)
    kcT = cut(60)
    vc = cut(256).rearrange("p (g f) -> p g f", g=4)
    pc = cut(240).rearrange("p (h n) -> p h n", h=16)
    pcT = cut(1024).rearrange("p (a h q) -> p a h q", a=2, h=4)
    gcf = cut(96).rearrange("p (t g) -> p t g", t=NT)
    cmx = cut(32)

    normed_T(LAT, 2)
    product(i["w_kv_2"], 0, 1536, keep_in(kv), [0, 1, 2, 3])
    for tt in range(NT):
        cos, sin = rope2[:, tt, 0, :], rope2[:, tt, 1, :]
        for kind in (0, 2, 4):
            rope(kv[:, tt, kind * 256:(kind + 1) * 256], 4, cos, sin)
        heads_T(kv[:, tt, 512:768], tt, 4, ksT, 0)
        heads_T(kv[:, tt, 1024:1280], tt, 4, kwT, 0)
    for n in range(2):
        for tt in range(NT):
            ve.op(v.tensor_copy, dup, bc(kv[:, tt, n * 256:(n + 1) * 256].rearrange("p (h f) -> p h f", f=HD), 2, 2),
                  after=[ac.now(), pe.now()])
            bk = bank_for_pe(2)
            pe.wait(ve.now())
            for h in range(4):
                pe.free(t.transpose, bk[:, h * P:(h + 1) * P], dup[:, h].rearrange("p a f -> p (a f)"), ident[:])
            b3 = bk.rearrange("p (h q) -> p h q", h=4)
            ve.op(v.tensor_copy, win[0:HD, :, tt * P:(tt + 1) * P], b3[0:HD], after=[pe.now()])
            lo = 1 if tt == 0 else 0
            ve.op(v.tensor_copy, win[HD:P, :, tt * P + lo - 1:(tt + 1) * P - 1], b3[HD:P, :, lo:P])
            read_by(2, ve.now())
        for c in range(16):
            ve.op(v.tensor_scalar, xw[:, c], win[:, :, 2 * c:2 * c + CMPS * (NCMP - 1) + 1:CMPS], pe2[:, n, c:c + 1], None,
                  ALU.add)
        slot = w_slot()
        tile = slot.ap[:].rearrange("p (c n) -> p c n", c=16)
        pe.wait(fetch(slot, (tile, i["cmp_w1_%s_2" % "kv"[n]].rearrange("(c p) n -> p c n", p=P))))
        bk = bank_for_pe(3)
        pe.wait(ve.now())
        for c in range(16):
            pe.free(t.matmul, bk[0:60, 0:256], xw[:, c].rearrange("p h n -> p (h n)"), tile[:, c, :],
                    start=(c == 0), stop=(c == 15))
        slot.reader = pe.now()
        ac.op(a.activation, hid[0:60], bk[0:60, 0:256], ACT.Gelu_apprx_tanh, after=[pe.now()])
        read_by(3, ac.now())
        bk = bank_for_pe(2)
        pe.wait(ac.now())
        for c in range(2):
            pe.free(t.transpose, bk[:, c * 60:(c + 1) * 60], hid[0:60, c * P:(c + 1) * P], ident[0:60, 0:60])
        ve.op(v.tensor_copy, hidT, bk[:, 0:120].rearrange("p (c r) -> p c r", c=2), after=[pe.now()])
        read_by(2, ve.now())
        bk = bank_for_pe(3)
        pe.wait(ve.now())
        if n == 0:
            for c in range(2):
                pe.free(t.matmul, bk[0:HD, 0:60], w2[:, n, c, :], hidT[:, c, :], start=(c == 0), stop=(c == 1))
            ve.op(v.tensor_copy, kcT[0:HD], bk[0:HD, 0:60], after=[pe.now()])
        else:
            for g in range(4):
                for c in range(2):
                    pe.free(t.matmul, bk[0:NCMP, g * HD:(g + 1) * HD], hidT[:, c, g * NCMP:(g + 1) * NCMP], w2[:, n, c, :],
                            start=(c == 0), stop=(c == 1))
            ve.op(v.tensor_copy, vc[0:NCMP], bk[0:NCMP, 0:256].rearrange("p (g f) -> p g f", g=4), after=[pe.now()])
        read_by(3, ve.now())
    normed_T(LAT, 0)
    product(i["b_w_q_2"][0], 0, IN3, keep_in(projq), [0, 1, 2, 3])
    for tt in range(NT):
        rope(projq[:, tt, 0:1024], 16, rope2[:, tt, 0, :], rope2[:, tt, 1, :])
        heads_T(projq[:, tt, 0:1024], tt, 16, qT2, 0)
    ac.op(a.activation, gcf, projq[:, :, 1024:IN3], ACT.Exp, scale=-1.0, after=[ve.now()])
    ve.op(v.tensor_scalar, gcf, gcf, 1.0, None, ALU.add, after=[ac.now()])
    ve.op(v.reciprocal, gcf, gcf)
    for tt in range(NT):
        bk = bank_for_pe(0)
        pe.wait(ac.now())
        for h in range(16):
            pe.free(t.matmul, bk[:, h * NCMP:(h + 1) * NCMP], qT2[0:HD, h, tt * P:(tt + 1) * P],
                    kcT[0:HD, (h // 4) * NCMP:(h // 4 + 1) * NCMP], start=True, stop=True)
        s3 = bk[:, 0:240].rearrange("p (h n) -> p h n", h=16)
        ve.op(v.tensor_scalar, pc, s3, 0.125, None, ALU.mult, after=[pe.now()])
        read_by(0, ve.now())
        ve.op(v.tensor_tensor, pc, pc, bc(cmpmask[:, tt, 0, :], 1, 16), ALU.add)
        ve.op(v.tensor_reduce, cmx[:, 0:16], pc, AX, ALU.max)
        ve.op(v.tensor_tensor, pc, pc, bc(cmx[:, 0:16], 2, NCMP), ALU.subtract)
        ac.op(a.activation, pc, pc, ACT.Exp, after=[ve.now()])
        ve.op(v.tensor_reduce, cmx[:, 16:32], pc, AX, ALU.add, after=[ac.now()])
        ve.op(v.tensor_tensor, pc, pc, bc(cmpmask[:, tt, 1, :], 1, 16), ALU.mult)
        ve.op(v.reciprocal, cmx[:, 16:32], cmx[:, 16:32])
        ve.op(v.tensor_tensor, cmx[:, 16:32], cmx[:, 16:32], gcf[:, tt, 0:48:3], ALU.mult)
        for h0 in range(0, 16, 4):
            u = (h0 // 4) % 2
            bk = bank_for_pe(2 + u)
            pe.wait(ve.now())
            for h in range(4):
                pe.free(t.transpose, bk[0:NCMP, h * P:(h + 1) * P], pc[:, h0 + h, :], ident[:])
            ve.op(v.tensor_copy, pcT[0:NCMP, u], bk[0:NCMP, :].rearrange("p (h q) -> p h q", h=4), after=[pe.now()])
            read_by(2 + u, ve.now())
            o = bank_for_pe(4 + h0 // 8)
            pe.wait(ve.now())
            for h in range(4):
                c0 = ((h0 + h) % 8) * HD
                pe.free(t.matmul, o[:, c0:c0 + HD], pcT[0:NCMP, u, h, :], vc[0:NCMP, h0 // 4, :], start=True, stop=True)
            if h0 % 8 == 4:
                ve.wait(pe.now())
                into_cat(tt, h0 - 4, o.rearrange("p (h f) -> p h f", f=HD), cmx[:, 16 + h0 - 4:16 + h0 + 4])
                read_by(4 + h0 // 8, ve.now())

    def add_branch(branch):
        def finish(tt, h0, o, inv):
            ve.op(v.tensor_tensor, inv, inv, gcf[:, tt, 3 * h0 + branch:3 * h0 + branch + 22:3], ALU.mult)
            th = tmp[:, 0:512].rearrange("p (h f) -> p h f", f=HD)
            ve.op(v.tensor_tensor, th, o, bc(inv, 2, HD), ALU.mult)
            dst = cat[:, tt, h0 * HD:(h0 + 8) * HD]
            ve.op(v.tensor_tensor, dst, dst, tmp[:, 0:512], ALU.add)
        return finish

    for branch, kTb, v0 in ((1, ksT, 768), (2, kwT, 1280)):
        attention(16, 4, qT2, kTb, keys2, lambda g, b: kv[:, b, v0 + g * HD:v0 + (g + 1) * HD],
                  lambda tt: causal[:, tt, :], add_branch(branch))
    project_out(i["b_w_out_2"][0])
    add_gated(0, acc_tile)

    normed_T(LAT, 1)
    load_rows((prow[:, 0, :], i["final_gain_2"].partition_broadcast(P)))
    gate = sb("gate", [P, NT, NEXP])
    top = sb("top", [P, 8])
    topi = sb("topi", [P, 8], U32)
    topf = sb("topf", [P, 8])
    sm8 = sb("sm8", [P, 8])
    for tt in range(NT):
        bk = bank_for_pe(4)
        pe.wait(ve.now())
        for k in range(KD):
            pe.free(t.matmul, bk[:, 0:NEXP], XT[:, k, tt * P:(tt + 1) * P], wr[:, k, :], start=(k == 0), stop=(k == KD - 1))
        ve.op(v.tensor_copy, sm8[:], bk[:, 0:NEXP], after=[pe.now()])
        read_by(4, ve.now())
        ve.op(v.max, top[:], sm8[:])
        ve.op(v.max_index, topi[:], top[:], sm8[:])
        ve.op(v.tensor_copy, topf[:], topi[:])
        ve.op(v.tensor_tensor, top[:, 2:3], top[:, 1:2], top[:, 0:1], ALU.subtract)
        ac.op(a.activation, top[:, 3:4], top[:, 2:3], ACT.Exp, after=[ve.now()])
        ve.op(v.tensor_scalar, top[:, 4:5], top[:, 3:4], 1.0, None, ALU.add, after=[ac.now()])
        ve.op(v.reciprocal, top[:, 5:6], top[:, 4:5])
        ve.op(v.tensor_tensor, top[:, 6:7], top[:, 3:4], top[:, 5:6], ALU.mult)
        ve.op(v.tensor_scalar, gate[:, tt, :], const["iota8"][:], topf[:, 0:1], top[:, 5:6], ALU.is_equal, ALU.mult)
        ve.op(v.tensor_scalar, sm8[:], const["iota8"][:], topf[:, 1:2], top[:, 6:7], ALU.is_equal, ALU.mult)
        ve.op(v.tensor_tensor, gate[:, tt, :], gate[:, tt, :], sm8[:], ALU.add)
    meet()
    ve.wait(ve.now())
    v.memset(moe_y, 0.0).then_inc(fs["acc"], 1)
    fn["acc"] += 1
    gv = [i[n][0].rearrange("e (p k) n -> p e k n", k=KD) for n in ("moe_w_gate_2", "moe_w_up_2")]
    dv = i["moe_w_down_2"][0].rearrange("e (i p k) n -> p (e i) k n", p=P, k=2)
    steps = FEXP // FCOL
    s_moe = nc.alloc_semaphore("s_moe")
    moe_n = [0]

    def weigh(e, done):
        v.wait_ge(fs["dn"], done)
        v.wait_ge(fs["acc"], e + 1)
        for tt in range(NT):
            ins = v.scalar_tensor_tensor(moe_y[:, tt, :], acc_tile(tt), gate[:, tt, bass.ds(e, 1)], moe_y[:, tt, :],
                                         ALU.mult, ALU.add)
            if tt == 0:
                ins.then_inc(s_moe, 1)
                v.wait_ge(s_moe, e + 1)
            else:
                ins.then_inc(fs["acc"], 1)

    ffn(steps, lambda c, e, i_: gv[c][:, bass.ds(e, 1), :, bass.ds(i_ * FCOL, FCOL)].rearrange("p e k n -> p (e k) n"),
        lambda e, i_: dv[:, bass.ds(e * steps + i_, 1)].rearrange("p i k n -> p (i k) n"),
        experts=NEXP, after_expert=weigh)
    add_gated(1, lambda tt: moe_y[:, tt, :])

    s_out = nc.alloc_semaphore("s_out")
    ov = out[0].rearrange("(t p) d -> p t d", p=P)
    for tt in range(NT):
        ss = st[:, tt:tt + 1]
        ac.op(a.activation, xn[:], x[:, LAT, tt, :], ACT.Square, accum_out=ss, after=[ve.now()])
        rstd(ss, D, 1)
        ve.op(v.scalar_tensor_tensor, cat[:, tt, :], x[:, LAT, tt, :], ss, prow[:, 0, :], ALU.mult, ALU.mult,
              after=[(s_row, rows[0])])
        nc.sync.wait_ge(ve.sem, ve.n)
        nc.sync.dma_start(ov[:, tt, :], cat[:, tt, :]).then_inc(s_out, 16)
    nc.sync.wait_ge(s_out, 16 * NT)


NAMES = ["x", "c", "ctx", "c_ctx", "w_mod", "b_mod", "norm_mix_pre", "norm_mix_post", "norm_ffn_pre",
         "norm_ffn_post", "w_in", "q_norm", "k_norm", "conv_w", "conv_b", "dt_bias_fwd", "dt_bias_bwd",
         "a_log_fwd", "a_log_bwd", "d_skip", "ssd_norm", "w_out", "w_gate", "w_up", "w_down", "c_2",
         "positions_2", "attn_gain_2", "ffn_gain_2", "w_ada_2", "b_ada_2", "a_w_in_2", "a_w_out_2",
         "b_w_q_2", "b_w_out_2", "kv_gain_2", "w_kv_ada_2", "b_kv_ada_2", "w_kv_2", "cmp_pe_k_2",
         "cmp_w1_k_2", "cmp_w2_k_2", "cmp_pe_v_2", "cmp_w1_v_2", "cmp_w2_v_2", "ffn_w_gate_2",
         "ffn_w_up_2", "ffn_w_down_2", "moe_w_router_2", "moe_w_gate_2", "moe_w_up_2", "moe_w_down_2",
         "final_gain_2"]


def kernel(**inputs):
    import numpy as _np
    import concourse.bacc as _bacc
    from concourse import mybir as _mybir
    from concourse.bass_utils import run_bass_kernel_spmd as _run

    nc = _bacc.Bacc("TRN2", target_bir_lowering=False, num_devices=1)
    arrays, args = {}, {}
    for name in NAMES:
        a = _np.ascontiguousarray(inputs[name])
        arrays["in_" + name] = a
        args[name] = nc.dram_tensor("in_" + name, a.shape, _mybir.dt.from_np(a.dtype), kind="ExternalInput").ap()
    out = nc.dram_tensor("out", (1, T, D), F32, kind="ExternalOutput").ap()
    build(nc, args, out)
    r = _run(nc, [arrays], core_ids=[0])
    return r.results[0]["out"]
```

```python
import math

import numpy as np
import concourse.bass as bass
from concourse import mybir

F32 = mybir.dt.float32
I32 = mybir.dt.int32
U32 = mybir.dt.uint32
ALU = mybir.AluOpType
ACT = mybir.ActivationFunctionType
AX = mybir.AxisListType.X

P = 128
D = 1024
KD = D // P
T = 256
NT = T // P
EPS = 1e-6
NEG = -1e30
TAKEN = -3e38
HD = 64
LAT, CTX = 0, 1
Q0, K0, V0, Z0, XBC0, DT0, IN1 = 0, 512, 640, 768, 1280, 2304, 2312
DK0, DV0, IQ0, IK0, IW0, IN2 = 1024, 1280, 1536, 2048, 2112, 2120
IN3 = 1072
TOPK = 64
NCMP, CMPL, CMPS = 15, 32, 16
FCOL = 256
NEXP = 8
FEXP = 3584
FDENSE = 2816
ROPE_THETA = 10000.0
IDX_SCALE = 8 ** -0.5 * 64 ** -0.5


class Engine:

    def __init__(self, nc, engine, name):
        self.e, self.sem, self.n, self.met = engine, nc.alloc_semaphore(name), 0, {}

    def now(self):
        return (self.sem, self.n)

    def wait(self, *marks):
        for sem, value in marks:
            if value > self.met.get(sem.name, 0):
                self.e.wait_ge(sem, value)
                self.met[sem.name] = value

    def op(self, f, *a, after=(), **k):
        self.wait(*after, self.now())
        return self.free(f, *a, **k)

    def free(self, f, *a, **k):
        f(*a, **k).then_inc(self.sem, 1)
        self.n += 1
        return self.now()


class Slot:

    def __init__(self, nc, name, ap):
        self.ap, self.sem, self.n, self.reader = ap, nc.alloc_semaphore(name), 0, None


def bc(ap, axis, n):
    shape = list(ap.shape)
    return ap.unsqueeze(axis).broadcast_to(shape[:axis] + [n] + shape[axis:])


def constants():
    p = np.arange(P)
    tri = (p[:, None] <= p[None, :]).astype(np.float32)
    c = {"ident": np.eye(P, dtype=np.float32), "ones": np.ones((P, P), np.float32)}
    c["tri"] = np.stack([tri, tri.T], 1)
    c["trineg"] = np.where(c["tri"] > 0, 0.0, NEG).astype(np.float32)
    pos = np.arange(T)
    fr = (np.float32(ROPE_THETA) ** (-np.arange(16, dtype=np.float32) / np.float32(16))).astype(np.float32)
    ang = np.concatenate([(pos // 64).astype(np.float32)[:, None] * fr, (pos % 64).astype(np.float32)[:, None] * fr], 1)
    cos, sin = np.cos(ang.astype(np.float64)), np.sin(ang.astype(np.float64))
    tab = np.stack([np.concatenate([cos, cos], 1), np.concatenate([-sin, sin], 1)], 1)
    c["axial"] = tab.reshape(NT, P, 2, HD).transpose(1, 0, 2, 3).astype(np.float32)
    inv = np.float32(1.0) / (np.float32(ROPE_THETA) ** (np.arange(0, HD, 2, dtype=np.float32) / np.float32(HD)))
    c["inv"] = np.broadcast_to(inv.astype(np.float32), (P, 32)).copy()
    key = np.arange(T)
    tok = (np.arange(NT)[None, :] * P + p[:, None])
    c["causal"] = np.where(key[None, None, :] <= tok[:, :, None], 0.0, NEG).astype(np.float32)
    end = np.arange(NCMP) * CMPS + CMPL - 1
    ok = end[None, None, :] <= tok[:, :, None]
    c["cmpmask"] = np.stack([np.where(ok, 0.0, NEG), ok], 2).astype(np.float32)
    c["iota"] = np.broadcast_to(np.arange(P, dtype=np.float32), (P, P)).copy()
    sel = np.zeros((2, 2, P), np.float32)
    sel[0, 0], sel[1, 1] = 1.0, 1.0
    c["sel"] = sel
    return c


def build(nc, i, out):
    sp = Engine(nc, nc.sync, "s_sp")
    pe = Engine(nc, nc.tensor, "s_pe")
    ve = Engine(nc, nc.vector, "s_ve")
    ac = Engine(nc, nc.scalar, "s_ac")
    v, a, t = nc.vector, nc.scalar, nc.tensor

    def sb(name, shape, dt=F32):
        return nc.alloc_sbuf_tensor(name, shape, dt)

    x = sb("x", [P, 2, NT, D])
    wide = sb("wide", [P, 6 * D])
    XT = sb("XT", [P, KD, T])
    cat = sb("cat", [P, NT, D])
    gates = sb("gates", [2, 2, D])
    grow = sb("grow", [P, D])
    prow = sb("prow", [P, 2, D])
    xn = sb("xn", [P, D])
    tmp = sb("tmp", [P, D])
    arena = sb("arena", [P, 11904])
    work = sb("work", [P, 3072])
    w_slots = [Slot(nc, f"s_w{s}", sb(f"wslot{s}", [P, 4096])) for s in range(2)]
    d_slots = [Slot(nc, f"s_d{s}", sb(f"dslot{s}", [P, 2048])) for s in range(2)]
    ring = {"w": 0, "d": 0}
    psum = nc.alloc_psum_tensor("psum", [P, 8, 512], F32)
    bank_free = [[] for _ in range(8)]

    const = {}
    s_par = nc.alloc_semaphore("s_par")
    par = [0]

    def param(dst, src):
        nc.scalar.dma_start(dst, src).then_inc(s_par, 16)
        par[0] += 16

    for name, arr in constants().items():
        flat = arr.reshape(arr.shape[0], -1)
        buf = sb("c_" + name, list(flat.shape))
        param(buf[:], nc.inline_tensor(flat, name="k_" + name).ap())
        const[name] = buf
    ident, ones = const["ident"], const["ones"]
    tri = const["tri"][:].rearrange("p (d i) -> p d i", d=2)
    trineg = const["trineg"][:].rearrange("p (d i) -> p d i", d=2)
    axial = const["axial"][:].rearrange("p (t c h) -> p t c h", t=NT, c=2)
    causal = const["causal"][:].rearrange("p (t k) -> p t k", t=NT)
    cmpmask = const["cmpmask"][:].rearrange("p (t c n) -> p t c n", t=NT, c=2)
    sel = const["sel"][:].rearrange("p (s q) -> p s q", s=2)

    ccol = sb("ccol", [P, 3, KD])
    cs = sb("cs", [P, KD, 4])
    gcol = sb("gcol", [P, 9, KD])
    for n, name in enumerate(["c", "c_ctx", "c_2"]):
        src = i[name] if name == "c_ctx" else i[name][0]
        param(ccol[:, n, :], src.rearrange("(p k) -> p k", k=KD))
    gains = [("norm_mix_pre", 0), ("norm_mix_pre", 1), ("norm_ffn_pre", 0), ("norm_ffn_pre", 1),
             ("attn_gain_2", 0), ("attn_gain_2", 1), ("ffn_gain_2", 0), ("ffn_gain_2", 1), ("kv_gain_2", None)]
    for n, (name, l) in enumerate(gains):
        src = i[name] if l is None else i[name][l]
        param(gcol[:, n, :], src.rearrange("(p k) -> p k", k=KD))
    qkn = sb("qkn", [P, 2, 2, HD])
    dtp = sb("dtp", [P, 2, 3, 2, 8])
    ssdn = sb("ssdn", [P, 512])
    for l in range(2):
        param(qkn[:, l, 0, :], i["q_norm"][l].partition_broadcast(P))
        param(qkn[:, l, 1, :], i["k_norm"][l].partition_broadcast(P))
        for d, way in enumerate(("fwd", "bwd")):
            param(dtp[:, l, 0, d, :], i["dt_bias_" + way][l].partition_broadcast(P))
            param(dtp[:, l, 1, d, :], i["a_log_" + way][l].partition_broadcast(P))
        param(dtp[:, l, 2, 0, :], i["d_skip"][l].partition_broadcast(P))
        stage = (xn, tmp)[l]
        param(stage[0:5, :], i["conv_w"][l])
        param(stage[5:6, :], i["conv_b"][l:l + 1])
    posi = sb("posi", [P, NT], I32)
    with nc.allow_non_contiguous_dma(reason="256 positions"):
        param(posi[:], i["positions_2"][0].rearrange("(t p) -> p t", p=P))
    wr = sb("wr", [P, KD, NEXP])
    param(wr[:], i["moe_w_router_2"][0].rearrange("(p k) e -> p k e", k=KD))
    w2 = sb("w2", [P, 2, 2, HD])
    pe16 = sb("pe16", [16, 2, P])
    for n, kv in enumerate("kv"):
        param(w2[:, n], i[f"cmp_w2_{kv}_2"].rearrange("(c p) d -> p c d", p=P))
        param(pe16[:, n, :], i[f"cmp_pe_{kv}_2"].rearrange("(c a) d -> c (a d)", a=2))
    for s, name in ((LAT, "x"), (CTX, "ctx")):
        param(x[:, s], i[name][0].rearrange("(t p) d -> p t d", p=P))
    convp = sb("convp", [P, 2, KD, 6])
    col = sb("col", [P, 2, 3, 2, KD])
    st = sb("st", [P, 64])
    rope2 = sb("rope2", [P, NT, 2, HD])
    params = (s_par, par[0])
    s_row = nc.alloc_semaphore("s_row")
    rows = [0]

    def meet():
        marks = [e.now() for e in (pe, ve, ac)]
        for e in (pe, ve, ac):
            e.wait(*marks)

    def bank_for_pe(b):
        pe.wait(*bank_free[b])
        return psum[:, b, :]

    def read_by(b, *marks):
        bank_free[b] = list(marks)

    def load_rows(*pairs):
        ac.wait(ve.now(), ac.now())
        for dst, src in pairs:
            nc.scalar.dma_start(dst, src).then_inc(s_row, 16)
            rows[0] += 16

    for e in (pe, ve, ac):
        e.wait(params)
    csv = cs[:].rearrange("p k c -> p c k")
    ac.op(a.activation, csv[:, 0:3, :], ccol[:], ACT.Silu)
    ac.op(a.activation, dtp[:, :, 1], dtp[:, :, 1], ACT.Exp)
    ve.op(v.tensor_scalar, dtp[:, :, 1], dtp[:, :, 1], -1.0, None, ALU.mult, after=[ac.now()])
    for l in range(2):
        bk = bank_for_pe(l)
        for k in range(KD):
            pe.free(t.transpose, bk[:, 6 * k:6 * k + 6], (xn, tmp)[l][0:6, k * P:(k + 1) * P], ident[0:6, 0:6])
        ve.op(v.tensor_copy, convp[:, l], bk[:, 0:48].rearrange("p (k j) -> p k j", j=6), after=[pe.now()])
        read_by(l, ve.now())
    pe2 = sb("pe2", [P, 2, 16])
    bk = bank_for_pe(2)
    for n in range(2):
        pe.free(t.transpose, bk[:, 16 * n:16 * n + 16], pe16[:, n, :], ident[0:16, 0:16])
    ve.op(v.tensor_copy, pe2[:], bk[:, 0:32].rearrange("p (a b) -> p a b", a=2), after=[pe.now()])
    read_by(2, ve.now())

    tw = work[:, 0:512].rearrange("p (n t f) -> p n t f", n=8, t=NT)
    ang, kk, r, rc, m = (tw[:, n] for n in range(5))
    c1, c2 = 6.28125, float(np.float32(0.0019350052))
    c3 = 2 * math.pi - c1 - c2
    magic = 12582912.0
    posf = st[:, 0:NT]
    ve.op(v.tensor_copy, posf, posi[:])
    for n in range(NT):
        ve.op(v.tensor_scalar, ang[:, n], const["inv"][:], posf[:, n:n + 1], None, ALU.mult)
    ve.op(v.tensor_scalar, kk, ang, 1 / (2 * math.pi), magic, ALU.mult, ALU.add)
    ve.op(v.tensor_scalar, kk, kk, magic, None, ALU.subtract)
    ve.op(v.scalar_tensor_tensor, r, kk, -c1, ang, ALU.mult, ALU.add)
    ve.op(v.scalar_tensor_tensor, r, kk, -c2, r, ALU.mult, ALU.add)
    ve.op(v.scalar_tensor_tensor, r, kk, -c3, r, ALU.mult, ALU.add)
    ve.op(v.tensor_scalar, rc, r, math.pi / 2, None, ALU.add)
    ve.op(v.tensor_scalar, m, rc, math.pi, -2 * math.pi, ALU.is_gt, ALU.mult)
    ve.op(v.tensor_tensor, rc, rc, m, ALU.add)
    lim = 3.1415925
    for s in (r, rc):
        ve.op(v.tensor_scalar, s, s, lim, -lim, ALU.min, ALU.max)
    ac.op(a.activation, rope2[:, :, 0, 0:32], rc, ACT.Sin, after=[ve.now()])
    ac.op(a.activation, rope2[:, :, 0, 32:64], rc, ACT.Sin)
    ac.op(a.activation, rope2[:, :, 1, 32:64], r, ACT.Sin)
    ve.op(v.tensor_scalar, rope2[:, :, 1, 0:32], rope2[:, :, 1, 32:64], -1.0, None, ALU.mult, after=[ac.now()])

    def w_slot():
        s = w_slots[ring["w"] % 2]
        ring["w"] += 1
        return s

    def fetch(slot, *pairs):
        if slot.reader:
            sp.wait(slot.reader)
        for dst, src in pairs:
            nc.sync.dma_start(dst, src).then_inc(slot.sem, 16)
            slot.n += 16
        return (slot.sem, slot.n)

    s_mod = nc.alloc_semaphore("s_mod")
    s_modv = nc.alloc_semaphore("s_modv")
    mods = [0]

    def modulation(w, b, tiles, first, m_rows):
        modrow = wide[0:m_rows, 0:tiles * 512]
        meet()
        load_rows((modrow, b.partition_broadcast(m_rows)))
        ve.wait((s_row, rows[0]))
        wv = w.rearrange("(p k) n -> p k n", k=KD)
        base = mods[0]
        slots = [w_slot(), w_slot()]

        def step(j, u, r):
            slot = slots[u]
            if r is None:
                if slot.reader:
                    sp.wait(slot.reader)
                landed = slot.n + 16
            else:
                nc.sync.wait_ge(s_mod, j + (base - 1))
                landed = r * 16 + (slot.n + 16)
            nc.sync.dma_start(slot.ap[:].rearrange("p (k n) -> p k n", k=KD),
                              wv[:, :, bass.ds(j * 512, 512)]).then_inc(slot.sem, 16)
            t.wait_ge(slot.sem, landed)
            if r is not None:
                t.wait_ge(s_modv, j + (base - 1))
            for k in range(KD):
                mm = t.matmul(psum[0:m_rows, 6 + u, :], cs[:, k, first:first + m_rows],
                              slot.ap[:, k * 512:(k + 1) * 512], start=(k == 0), stop=(k == KD - 1))
            mm.then_inc(s_mod, 1)
            v.wait_ge(s_mod, j + (base + 1))
            dst = wide[0:m_rows, bass.ds(j * 512, 512)]
            v.tensor_tensor(dst, dst, psum[0:m_rows, 6 + u, :], ALU.add).then_inc(s_modv, 1)

        for u in range(2):
            step(u, u, None)
            slots[u].n += 16
        if tiles > 2:
            with nc.Fori(0, tiles // 2 - 1) as r:
                for u in range(2):
                    step(r * 2 + (2 + u), u, r)
            for u in range(2):
                slots[u].n += 16 * (tiles // 2 - 1)
        mods[0] = base + tiles
        for u in range(2):
            slots[u].reader = (s_mod, mods[0])
        for e in (pe, ve, ac):
            e.wait((s_modv, mods[0]))

    def columns(dst, row0, m_rows):
        bk = bank_for_pe(5)
        for k in range(KD):
            pe.free(t.matmul, bk[:, k * m_rows:(k + 1) * m_rows], wide[0:m_rows, row0 + k:row0 + D:KD],
                    ident[0:m_rows, 0:m_rows], start=True, stop=True)
        for s in range(m_rows):
            ve.op(v.tensor_copy, dst(s), bk[:, s:KD * m_rows:m_rows], after=[pe.now()])
        read_by(5, ve.now())

    def norm_columns(which, row_shift, row_scale, gain, m_rows):
        columns(lambda s: col[:, s, which, 1, :], row_shift, m_rows)
        columns(lambda s: col[:, s, which, 0, :], row_scale, m_rows)
        for s in range(m_rows):
            c0 = col[:, s, which, 0, :]
            ve.op(v.scalar_tensor_tensor, c0, c0, 1.0, gcol[:, gain, :], ALU.add, ALU.mult)

    def layer_modulation(w, b, first, m_rows, mix_gain, ffn_gain):
        modulation(w, b, 12, first, m_rows)
        norm_columns(0, 0, D, mix_gain, m_rows)
        norm_columns(1, 3 * D, 4 * D, ffn_gain, m_rows)
        for n, row in enumerate((2 * D, 5 * D)):
            ve.op(v.tensor_copy, gates[0:m_rows, n, :], wide[0:m_rows, row:row + D])
        meet()

    def rstd(dst, n, width):
        m_ = st[:, 48:48 + width]
        ve.op(v.tensor_scalar, m_, dst, 1.0 / n, EPS, ALU.mult, ALU.add, after=[ac.now()])
        ac.op(a.activation, dst, m_, ACT.Sqrt, after=[ve.now()])
        ve.op(v.reciprocal, dst, dst, after=[ac.now()])
        ve.op(v.tensor_tensor, m_, m_, dst, ALU.mult)
        ve.op(v.tensor_tensor, m_, m_, dst, ALU.mult)
        ve.op(v.tensor_scalar, m_, m_, -0.5, 1.5, ALU.mult, ALU.add)
        ve.op(v.tensor_tensor, dst, dst, m_, ALU.mult)

    def normed_T(s, which):
        for tt in range(NT):
            ss = st[:, tt:tt + 1]
            ac.op(a.activation, xn[:], x[:, s, tt, :], ACT.Square, accum_out=ss, after=[ve.now(), pe.now()])
            rstd(ss, D, 1)
            ac.op(a.activation, xn[:], x[:, s, tt, :], ACT.Copy, scale=ss, after=[ve.now()])
            for half in range(2):
                bk = bank_for_pe(half)
                pe.wait(ac.now())
                for k in range(4):
                    pe.free(t.transpose, bk[:, k * P:(k + 1) * P], xn[:, 4 * half + k:D:KD], ident[:])
                for k in range(4):
                    kk_ = 4 * half + k
                    ve.op(v.tensor_scalar, XT[:, kk_, tt * P:(tt + 1) * P], bk[:, k * P:(k + 1) * P],
                          col[:, s, which, 0, kk_:kk_ + 1], col[:, s, which, 1, kk_:kk_ + 1],
                          ALU.mult, ALU.add, after=[pe.now()])
                read_by(half, ve.now())

    def cat_T():
        for tt in range(NT):
            for half in range(2):
                b = 4 + half
                bk = bank_for_pe(b)
                pe.wait(ve.now(), ac.now())
                for k in range(4):
                    pe.free(t.transpose, bk[:, k * P:(k + 1) * P], cat[:, tt, 4 * half + k:D:KD], ident[:])
                ve.op(v.tensor_copy, XT[:, 4 * half:4 * half + 4, tt * P:(tt + 1) * P],
                      bk.rearrange("p (k q) -> p k q", k=4), after=[pe.now()])
                read_by(b, ve.now())

    def product(w, c0, c1, sink, banks):
        wv = w.rearrange("(p k) n -> p k n", k=KD)
        nb = 0
        for c in range(c0, c1, 512):
            n = min(512, c1 - c)
            slot = w_slot()
            tile = slot.ap[:, 0:KD * n].rearrange("p (k n) -> p k n", k=KD)
            pe.wait(fetch(slot, (tile, wv[:, :, c:c + n])))
            pe.wait(ve.now())
            for tt in range(NT):
                b = banks[nb % len(banks)]
                nb += 1
                bk = bank_for_pe(b)
                for k in range(KD):
                    mm = t.matmul(bk[:, 0:n], XT[:, k, tt * P:(tt + 1) * P], tile[:, k, :],
                                  start=(k == 0), stop=(k == KD - 1))
                mm.then_inc(pe.sem, 1)
                pe.n += 1
                sink(tt, c, n, b)
            slot.reader = pe.now()

    def keep_in(buf):
        def sink(tt, c, n, b):
            if tt == 0:
                ac.op(a.activation, buf[:, tt, c:c + n], psum[:, b, 0:n], ACT.Copy, after=[pe.now()])
                read_by(b, ac.now())
            else:
                ve.op(v.tensor_copy, buf[:, tt, c:c + n], psum[:, b, 0:n], after=[pe.now()])
                read_by(b, ve.now())
        return sink

    def gate_row(s, n):
        for h in range(2):
            bk = bank_for_pe(6 + h)
            pe.wait(ve.now())
            pe.free(t.matmul, bk, sel[0:2, s, :] if s is not None else ones[0:1, :],
                    gates[0:2, n, h * 512:(h + 1) * 512] if s is not None else gates[0:1, n, h * 512:(h + 1) * 512],
                    start=True, stop=True)
            ve.op(v.tensor_copy, grow[:, h * 512:(h + 1) * 512], bk, after=[pe.now()])
            read_by(6 + h, ve.now())

    def add_normed(s, n):
        gate_row(s, n)
        ve.op(v.tensor_tensor, grow[:], grow[:], prow[:, n, :], ALU.mult, after=[(s_row, rows[0])])
        for tt in range(NT):
            acc = psum[:, 2 * tt:2 * tt + 2, :].rearrange("p b n -> p (b n)")
            ss = st[:, tt:tt + 1]
            ac.op(a.activation, xn[:], acc, ACT.Square, accum_out=ss, after=[ve.now(), pe.now()])
            rstd(ss, D, 1)
            ve.op(v.scalar_tensor_tensor, tmp[:], acc, ss, grow[:], ALU.mult, ALU.mult, after=[pe.now()])
            for b in (2 * tt, 2 * tt + 1):
                read_by(b, ve.now(), ac.now())
            ve.op(v.tensor_tensor, x[:, s, tt, :], x[:, s, tt, :], tmp[:], ALU.add)

    def add_gated(n, source):
        gate_row(None, n)
        for tt in range(NT):
            ve.op(v.tensor_tensor, tmp[:], source(tt), grow[:], ALU.mult, after=[pe.now()])
            for b in (2 * tt, 2 * tt + 1):
                read_by(b, ve.now())
            ve.op(v.tensor_tensor, x[:, LAT, tt, :], x[:, LAT, tt, :], tmp[:], ALU.add)

    def project_out(w):
        cat_T()
        product(w, 0, D, lambda tt, c, n, b: None, [0, 2, 1, 3])

    def acc_tile(tt):
        return psum[:, 2 * tt:2 * tt + 2, :].rearrange("p b n -> p (b n)")

    names = ["gu", "silu", "h", "tr", "ev", "dn"]
    fs = {n: nc.alloc_semaphore("s_f" + n) for n in names}
    fn = dict.fromkeys(names, 0)
    sg = work[:, 0:512].rearrange("p (t n) -> p t n", t=NT)
    hb = work[:, 512:1024].rearrange("p (t n) -> p t n", t=NT)
    hT = work[:, 1024:2048].rearrange("p (a k q) -> p a k q", a=2, k=2)
    moe_y = cat[:]

    def hold(engine, sem, value):
        if not isinstance(value, int) or value > 0:
            engine.wait_ge(sem, value)

    def open_slots():
        ws, ds = [w_slots[(ring["w"] + u) % 2] for u in range(2)], [d_slots[(ring["d"] + u) % 2] for u in range(2)]
        for s in ws + ds:
            if s.reader:
                sp.wait(s.reader)
        return ws, ds

    def close_slots(ws, ds, total):
        ring["w"] += total
        ring["d"] += total
        for u in range(2):
            steps_u = (total + 1 - u) // 2
            ws[u].n += 32 * steps_u
            ds[u].n += 16 * steps_u
            ws[u].reader = (fs["gu"], fn["gu"])
            ds[u].reader = (fs["dn"], fn["dn"])

    def ffn(steps, gate_up, down):
        meet()
        base = dict(fn)
        ws, ds = open_slots()
        wn, dn_ = [s.n for s in ws], [s.n for s in ds]

        def value(name, per, i_, plus):
            return i_ * per + (base[name] + plus)

        def landed(n0, per, u, i_):
            return (i_ - u) * (per // 2) + (n0[u] + per)

        def load(i_, u):
            hold(nc.sync, fs["gu"], value("gu", 2, i_, -2))
            tile = ws[u].ap[:].rearrange("p (k c n) -> p k c n", k=KD, c=2)
            for c in range(2):
                nc.sync.dma_start(tile[:, :, c, :], gate_up(c, i_)).then_inc(ws[u].sem, 16)
            hold(nc.sync, fs["dn"], value("dn", 1, i_, -1))
            nc.sync.dma_start(ds[u].ap[:].rearrange("p (k n) -> p k n", k=2), down(i_)).then_inc(ds[u].sem, 16)

        def up(i_, u, tt):
            hold(t, ws[u].sem, landed(wn, 32, u, i_))
            hold(t, fs["h"], value("h", 2, i_, tt - 1))
            for k in range(KD):
                mm = t.matmul(psum[:, 4 + tt, :], XT[:, k, tt * P:(tt + 1) * P],
                              ws[u].ap[:, k * 512:(k + 1) * 512], start=(k == 0), stop=(k == KD - 1))
            mm.then_inc(fs["gu"], 1)
            hold(a, fs["gu"], value("gu", 2, i_, tt + 1))
            hold(a, fs["h"], value("h", 2, i_, tt - 1))
            a.activation(sg[:, tt, :], psum[:, 4 + tt, 0:FCOL], ACT.Silu).then_inc(fs["silu"], 1)

        def hidden(i_, tt):
            hold(v, fs["silu"], value("silu", 2, i_, tt + 1))
            hold(v, fs["tr"], value("tr", 2, i_, tt - 1))
            v.tensor_tensor(hb[:, tt, :], sg[:, tt, :], psum[:, 4 + tt, FCOL:512], ALU.mult).then_inc(fs["h"], 1)

        def turn(i_, u, tt):
            hold(t, fs["h"], value("h", 2, i_, tt + 1))
            hold(t, fs["ev"], value("ev", 2, i_, tt - 1))
            for k in range(2):
                mm = t.transpose(psum[:, 6 + tt, k * P:(k + 1) * P], hb[:, tt, k:FCOL:2], ident[:])
            mm.then_inc(fs["tr"], 1)
            hold(v, fs["tr"], value("tr", 2, i_, tt + 1))
            hold(v, fs["dn"], value("dn", 1, i_, -1))
            v.tensor_copy(hT[:, u, :, tt * P:(tt + 1) * P],
                          psum[:, 6 + tt, 0:256].rearrange("p (k q) -> p k q", k=2)).then_inc(fs["ev"], 1)

        def downs(i_, u, start, stop):
            hold(t, ds[u].sem, landed(dn_, 16, u, i_))
            hold(t, fs["ev"], value("ev", 2, i_, 2))
            for tt in range(NT):
                for k in range(2):
                    for h in range(2):
                        mm = t.matmul(psum[:, 2 * tt + h, :], hT[:, u, k, tt * P:(tt + 1) * P],
                                      ds[u].ap[:, k * D + h * 512:k * D + (h + 1) * 512],
                                      start=start and k == 0, stop=stop and k == 1)
            mm.then_inc(fs["dn"], 1)

        def step(i_, u):
            load(i_, u)
            up(i_, u, 0)
            if not isinstance(i_, int) or i_ > 0:
                turn(i_ - 1, 1 - u, 1)
            hidden(i_, 0)
            up(i_, u, 1)
            hidden(i_, 1)
            turn(i_, u, 0)

        step(0, 0)
        step(1, 1)
        downs(0, 0, True, False)
        pairs = (steps - 2) // 2
        with nc.Fori(0, pairs) as r:
            for u in range(2):
                step(r * 2 + (2 + u), u)
                downs(r * 2 + (1 + u), 1 - u, False, False)
        last = 2 + 2 * pairs
        if last < steps:
            step(last, 0)
            downs(last - 1, 1, False, False)
        turn(steps - 1, (steps - 1) % 2, 1)
        downs(steps - 1, (steps - 1) % 2, False, True)
        for n in ("gu", "silu", "h", "tr", "ev"):
            fn[n] += 2 * steps
        fn["dn"] += steps
        close_slots(ws, ds, steps)
        for e_ in (pe, ve, ac):
            e_.wait((fs["dn"], fn["dn"]), (fs["ev"], fn["ev"]))

    def dense(wg, wu, wd):
        gv = [w.rearrange("(p k) n -> p k n", k=KD) for w in (wg, wu)]
        dv = wd.rearrange("(i p k) n -> p i k n", p=P, k=2)
        ffn(FDENSE // FCOL, lambda c, i_: gv[c][:, :, bass.ds(i_ * FCOL, FCOL)],
            lambda i_: dv[:, bass.ds(i_, 1)].rearrange("p i k n -> p (i k) n"))

    def heads_T(src, tt, heads, dst, offset):
        for h0 in range(0, heads, 4):
            n = min(4, heads - h0)
            b = 4 + (h0 // 4) % 2
            bk = bank_for_pe(b)
            pe.wait(ve.now(), ac.now())
            for h in range(n):
                pe.free(t.transpose, bk[0:HD, h * P:(h + 1) * P], src[:, (h0 + h) * HD:(h0 + h + 1) * HD], ident[:])
            ac.op(a.activation, dst[0:HD, h0:h0 + n, offset + tt * P:offset + (tt + 1) * P],
                  bk[0:HD, 0:n * P].rearrange("p (h q) -> p h q", h=n), ACT.Copy, after=[pe.now()])
            read_by(b, ac.now())

    def rope(src, heads, cos, sin):
        d = src.rearrange("p (h f) -> p h f", f=HD)
        o = tmp[:, 0:heads * HD].rearrange("p (h f) -> p h f", f=HD)
        ve.op(v.tensor_tensor, o[:, :, 0:32], d[:, :, 32:64], bc(sin[:, 0:32], 1, heads), ALU.mult, after=[ac.now(), pe.now()])
        ve.op(v.tensor_tensor, o[:, :, 32:64], d[:, :, 0:32], bc(sin[:, 32:64], 1, heads), ALU.mult)
        ve.op(v.tensor_tensor, d, d, bc(cos, 1, heads), ALU.mult)
        ve.op(v.tensor_tensor, d, d, o, ALU.add)

    Pm = work[:, 0:1536].rearrange("p (a n) -> p a n", a=3)
    PT = work[:, 1536:2560].rearrange("p (a n) -> p a n", a=2)
    msum = st[:, 16:40]
    LAG = 2

    def attention(heads, per_kv, qT, kT, keys, vals, bias, finish):
        units = [(tt, h) for tt in range(NT) for h in range(heads)]
        exp_of, pv_of, turned, outs = {}, {}, {}, {}
        pe.wait(ac.now(), ve.now())
        ac.wait(ve.now())
        ve.wait(pe.now(), ac.now())

        def scores(u):
            tt, h = units[u]
            nk, buf = keys(tt), u % 3
            sbank = (0, 1, 6)[buf]
            bk = bank_for_pe(sbank)
            qk = pe.free(t.matmul, bk[:, 0:nk], qT[0:HD, h, tt * P:(tt + 1) * P], kT[0:HD, h // per_kv, 0:nk],
                         start=True, stop=True)
            mx = msum[:, buf:buf + 1]
            sm = msum[:, 3 + 8 * ((u // 8) % 2) + u % 8:][:, 0:1]
            p_ = Pm[:, buf, 0:nk]
            free = [turned[u - 3]] if u >= 3 else []
            if bias is None:
                ve.op(v.tensor_reduce, mx, bk[:, 0:nk], AX, ALU.max, after=[qk] + ([exp_of[u - 3]] if u >= 3 else []))
                m_ = ve.op(v.tensor_scalar, mx, mx, -0.125, None, ALU.mult)
                exp_of[u] = ac.op(a.activation, p_, bk[:, 0:nk], ACT.Exp, bias=mx, scale=0.125, accum_out=sm,
                                  after=[m_] + free + ([outs[u // 8 - 2]] if u // 8 >= 2 else []))
                read_by(sbank, exp_of[u])
            else:
                m_ = ve.op(v.scalar_tensor_tensor, p_, bk[:, 0:nk], 0.125, bias(tt)[:, 0:nk], ALU.mult, ALU.add,
                           after=[qk] + free + ([exp_of[u - 3]] if u >= 3 else []))
                read_by(sbank, m_)
                m_ = ve.op(v.tensor_reduce, mx, p_, AX, ALU.max, negate=True)
                exp_of[u] = ac.op(a.activation, p_, p_, ACT.Exp, bias=mx, scale=1.0, accum_out=sm,
                                  after=[m_] + ([outs[u // 8 - 2]] if u // 8 >= 2 else []))

        def values(u):
            tt, h = units[u]
            nk, par_ = keys(tt), u % 2
            bk = bank_for_pe(2 + par_)
            pe.wait(exp_of[u])
            for b in range(nk // P):
                turned[u] = pe.free(t.transpose, bk[:, b * P:(b + 1) * P], Pm[:, u % 3, b * P:(b + 1) * P], ident[:])
            m_ = ve.op(v.tensor_copy, PT[:, par_, 0:nk], bk[:, 0:nk],
                       after=[turned[u]] + ([pv_of[u - 2]] if u >= 2 else []))
            read_by(2 + par_, m_)
            ob = 4 + (u // 8) % 2
            o = bank_for_pe(ob)
            pe.wait(m_)
            for b in range(nk // P):
                mm = t.matmul(o[:, (h % 8) * HD:(h % 8 + 1) * HD], PT[:, par_, b * P:(b + 1) * P],
                              vals(h // per_kv, b), start=(b == 0), stop=(b == nk // P - 1))
            mm.then_inc(pe.sem, 1)
            pe.n += 1
            pv_of[u] = pe.now()
            if h % 8 == 7:
                sums = msum[:, 3 + 8 * ((u // 8) % 2):][:, 0:8]
                ve.op(v.reciprocal, sums, sums, after=[pv_of[u], exp_of[u]])
                finish(tt, h - 7, o.rearrange("p (h f) -> p h f", f=HD), sums)
                outs[u // 8] = ve.now()
                read_by(ob, ve.now())

        for u in range(len(units) + LAG):
            if u < len(units):
                scores(u)
            if u >= LAG:
                values(u - LAG)

    def into_cat(tt, h0, o, inv):
        ve.op(v.tensor_tensor, cat[:, tt, h0 * HD:(h0 + 8) * HD].rearrange("p (h f) -> p h f", f=HD),
              o, bc(inv, 2, HD), ALU.mult)

    proj = wide[:, 0:NT * IN1].rearrange("p (t n) -> p t n", t=NT)
    off = [0]

    def cut(n):
        off[0] += n
        return arena[:, off[0] - n:off[0]]

    qT = cut(2048).rearrange("p (h q) -> p h q", h=8)
    kT = cut(1024).rearrange("p (g q) -> p g q", g=2)
    vctx = cut(256).rearrange("p (t n) -> p t n", t=NT)
    xbcT = cut(2080).rearrange("p (b q) -> p b q", b=8)
    convT = cut(2048).rearrange("p (b q) -> p b q", b=8)
    xtok = cut(1024).rearrange("p (t n) -> p t n", t=NT)
    btok = cut(512).rearrange("p (t n) -> p t n", t=NT)
    smat = cut(512).rearrange("p (t g q) -> p t g q", t=NT, g=2)
    state = cut(1024).rearrange("p (d n) -> p d n", d=2)
    xdt = cut(512)
    xde = cut(512)
    dts = cut(256).rearrange("p (n t d h) -> p n t d h", n=8, t=NT, d=2)
    ex = cut(64)
    dec = work[:, 0:1024].rearrange("p (h q) -> p h q", h=8)
    dtB = work[:, 1024:2048].rearrange("p (h q) -> p h q", h=8)

    def ssd(l, s, with_y):
        meet()
        ve.op(v.memset, xbcT[:, :, 0:2], 0.0)
        ve.op(v.memset, xbcT[:, :, 258:260], 0.0)
        for b2 in range(0, 8, 2):
            b = (b2 // 2) % 2
            bk = bank_for_pe(b)
            for n in range(4):
                blk, tt = b2 + n // 2, n % 2
                pe.free(t.transpose, bk[:, n * P:(n + 1) * P], proj[:, tt, XBC0 + blk * P:XBC0 + (blk + 1) * P], ident[:])
            ac.op(a.activation, xbcT[:, b2:b2 + 2, 2:258], bk.rearrange("p (b q) -> p b q", b=2), ACT.Copy, after=[pe.now()])
            read_by(b, ac.now())
        for b in range(8):
            acc_ = convT[:, b, :]
            ve.op(v.tensor_scalar, acc_, xbcT[:, b, 0:T], convp[:, l, b, 0:1], None, ALU.mult, after=[ac.now()])
            for j in range(1, 5):
                ve.op(v.scalar_tensor_tensor, acc_, xbcT[:, b, j:j + T], convp[:, l, b, j:j + 1], acc_, ALU.mult, ALU.add)
            ac.op(a.activation, acc_, acc_, ACT.Silu, bias=convp[:, l, b, 5:6], after=[ve.now()])
        for tt in range(NT):
            bk = bank_for_pe(2)
            pe.wait(ac.now())
            for b in range(4):
                pe.free(t.transpose, bk[:, b * P:(b + 1) * P], convT[:, b, tt * P:(tt + 1) * P], ident[:])
            ve.op(v.tensor_copy, xtok[:, tt, :], bk, after=[pe.now()])
            read_by(2, ve.now())
            bk = bank_for_pe(3)
            for b in range(2):
                pe.free(t.transpose, bk[:, b * P:(b + 1) * P], convT[:, 4 + b, tt * P:(tt + 1) * P], ident[:])
            ve.op(v.tensor_copy, btok[:, tt, :], bk[:, 0:256], after=[pe.now()])
            read_by(3, ve.now())
        xx, e_, u_, ln, m_, dt, dtA, sp_ = (dts[:, n] for n in range(8))
        for d in range(2):
            ve.op(v.tensor_tensor, xx[:, :, d, :], proj[:, :, DT0:DT0 + 8], bc(dtp[:, l, 0, d, :], 1, NT), ALU.add)
        ve.op(v.tensor_scalar, e_, xx, -1.0, None, ALU.mult)
        ve.op(v.tensor_tensor, e_, e_, xx, ALU.min)
        ac.op(a.activation, e_, e_, ACT.Exp, after=[ve.now()])
        ve.op(v.tensor_scalar, u_, e_, 1.0, None, ALU.add, after=[ac.now()])
        ac.op(a.activation, ln, u_, ACT.Ln, after=[ve.now()])
        ve.op(v.tensor_scalar, u_, u_, 1.0, None, ALU.subtract, after=[ac.now()])
        ve.op(v.tensor_scalar, m_, u_, 0.0, None, ALU.is_equal)
        ve.op(v.tensor_tensor, ln, ln, m_, ALU.add)
        ve.op(v.tensor_tensor, ln, ln, e_, ALU.mult)
        ve.op(v.tensor_tensor, u_, u_, m_, ALU.add)
        ve.op(v.reciprocal, u_, u_)
        ve.op(v.tensor_tensor, ln, ln, u_, ALU.mult)
        ve.op(v.tensor_scalar, xx, xx, 0.0, None, ALU.max)
        ve.op(v.tensor_tensor, dt, xx, ln, ALU.add)
        for d in range(2):
            ve.op(v.tensor_tensor, dtA[:, :, d, :], dt[:, :, d, :], bc(dtp[:, l, 1, d, :], 1, NT), ALU.mult)
        if with_y:
            bk = bank_for_pe(2)
            pe.wait(ac.now())
            for n in range(4):
                tt, g = n // 2, n % 2
                pe.free(t.matmul, bk[:, n * P:(n + 1) * P], convT[:, 4 + g, tt * P:(tt + 1) * P],
                        convT[:, 6 + g, tt * P:(tt + 1) * P], start=True, stop=True)
            ve.op(v.tensor_copy, smat, bk.rearrange("p (t g q) -> p t g q", t=2, g=2), after=[pe.now()])
            read_by(2, ve.now())
        for d in range(2):
            for n, tt in enumerate((0, 1) if d == 0 else (1, 0)):
                fresh = s == CTX and n == 0
                last = s == LAT and n == 1
                dA, dtc = dtA[:, tt, d, :], dt[:, tt, d, :]
                bk = bank_for_pe(0)
                pe.wait(ve.now())
                pe.free(t.matmul, bk[:, 0:8], tri[:, d, :], dA, start=True, stop=True)
                pe.free(t.matmul, bk[:, 8:16], ones[:], dA, start=True, stop=True)
                acum, tot, dte, ea, cd = (ex[:, 8 * j:8 * j + 8] for j in range(5))
                ve.op(v.tensor_copy, ex[:, 0:16], bk[:, 0:16], after=[pe.now(), ac.now()])
                read_by(0, ve.now())
                ve.op(v.tensor_tensor, dte, tot, acum, ALU.subtract)
                ac.op(a.activation, dte, dte, ACT.Exp, after=[ve.now()])
                ac.op(a.activation, ea, acum, ACT.Exp)
                ac.op(a.activation, cd, tot, ACT.Exp)
                xh = xtok[:, tt, :].rearrange("p (h f) -> p h f", f=HD)
                ve.op(v.tensor_tensor, xdt.rearrange("p (h f) -> p h f", f=HD), xh, bc(dtc, 2, HD), ALU.mult)
                ve.op(v.tensor_tensor, xde.rearrange("p (h f) -> p h f", f=HD), xdt.rearrange("p (h f) -> p h f", f=HD),
                      bc(dte, 2, HD), ALU.mult, after=[ac.now()])
                if with_y:
                    ve.op(v.tensor_copy, dtB, bc(dA, 2, P))
                    pe.wait(*bank_free[6], *bank_free[7], ve.now())
                    for h in range(8):
                        pe.free(t.matmul, psum[:, 6 + h // 4, (h % 4) * P:(h % 4 + 1) * P], dtB[:, h, :], tri[:, d, :],
                                start=True, stop=True)
                    pair = psum[:, 6:8, :].rearrange("p b (h q) -> p (b h) q", q=P)
                    ve.op(v.tensor_tensor, dec, pair, bc(acum, 2, P), ALU.subtract, after=[pe.now()])
                    read_by(6, ve.now())
                    read_by(7, ve.now())
                    ve.op(v.tensor_tensor, dec, dec, bc(trineg[:, d, :], 1, 8), ALU.add)
                    ac.op(a.activation, dec, dec, ACT.Exp, after=[ve.now()])
                    for g in range(2):
                        ve.op(v.tensor_tensor, dec[:, 4 * g:4 * g + 4, :], dec[:, 4 * g:4 * g + 4, :],
                              bc(smat[:, tt, g, :], 1, 4), ALU.mult, after=[ac.now()])
                    o = bank_for_pe(4)
                    pe.wait(ve.now())
                    for h in range(8):
                        pe.free(t.matmul, o[:, h * HD:(h + 1) * HD], dec[:, h, :], xdt[:, h * HD:(h + 1) * HD],
                                start=True, stop=True)
                    y = cat[:, tt, 512:1024]
                    if d == 0:
                        ve.op(v.tensor_copy, y, o, after=[pe.now()])
                    else:
                        ve.op(v.tensor_tensor, y, y, o, ALU.add, after=[pe.now()])
                    read_by(4, ve.now())
                    if not fresh:
                        o = bank_for_pe(5)
                        for g in range(2):
                            pe.free(t.matmul, o[:, g * 256:(g + 1) * 256], convT[:, 6 + g, tt * P:(tt + 1) * P],
                                    state[:, d, g * 256:(g + 1) * 256], start=True, stop=True)
                        th = tmp[:, 0:512]
                        ve.op(v.tensor_tensor, th.rearrange("p (h f) -> p h f", f=HD),
                              o.rearrange("p (h f) -> p h f", f=HD), bc(ea, 2, HD), ALU.mult, after=[pe.now(), ac.now()])
                        read_by(5, ve.now())
                        ve.op(v.tensor_tensor, y, y, th, ALU.add)
                if not last:
                    bk = bank_for_pe(1)
                    pe.wait(ve.now())
                    for g in range(2):
                        pe.free(t.matmul, bk[:, g * 256:(g + 1) * 256], btok[:, tt, g * P:(g + 1) * P],
                                xde[:, g * 256:(g + 1) * 256], start=True, stop=True)
                    sh_ = state[:, d, :].rearrange("p (h f) -> p h f", f=HD)
                    if fresh:
                        ve.op(v.tensor_copy, state[:, d, :], bk, after=[pe.now()])
                    else:
                        ve.op(v.tensor_tensor, sh_, sh_, bc(cd, 2, HD), ALU.mult, after=[pe.now(), ac.now()])
                        ve.op(v.tensor_tensor, state[:, d, :], state[:, d, :], bk, ALU.add)
                    read_by(1, ve.now())
        if with_y:
            for tt in range(NT):
                y, th = cat[:, tt, 512:1024], tmp[:, 0:512]
                ve.op(v.tensor_tensor, th.rearrange("p (h f) -> p h f", f=HD),
                      xtok[:, tt, :].rearrange("p (h f) -> p h f", f=HD), bc(dtp[:, l, 2, 0, :], 2, HD), ALU.mult, after=[ac.now()])
                ve.op(v.tensor_tensor, y, y, th, ALU.add)
                ac.op(a.activation, xn[:, 0:512], proj[:, tt, Z0:Z0 + 512], ACT.Silu, after=[ve.now()])
                ve.op(v.tensor_tensor, y, y, xn[:, 0:512], ALU.mult, after=[ac.now()])
                ss = st[:, tt:tt + 1]
                ac.op(a.activation, xn[:, 0:512], y, ACT.Square, accum_out=ss, after=[ve.now()])
                rstd(ss, 512, 1)
                ve.op(v.scalar_tensor_tensor, y, y, ss, ssdn[:], ALU.mult, ALU.mult, after=[(s_row, rows[0])])

    def mixer_in(l, s):
        normed_T(s, 0)
        product(i["w_in"][l], 0, IN1, keep_in(proj), [0, 1, 2, 3])
        for tt in range(NT):
            qk = proj[:, tt, 0:640]
            q3 = qk.rearrange("p (h f) -> p h f", f=HD)
            sq = tmp[:, 0:640]
            ve.op(v.tensor_tensor, sq, qk, qk, ALU.mult, after=[ac.now()])
            ss = st[:, 0:10]
            ve.op(v.tensor_reduce, ss, sq.rearrange("p (h f) -> p h f", f=HD), AX, ALU.add)
            rstd(ss, HD, 10)
            ve.op(v.tensor_tensor, q3, q3, bc(ss, 2, HD), ALU.mult)
            ve.op(v.tensor_tensor, q3[:, 0:8], q3[:, 0:8], bc(qkn[:, l, 0, :], 1, 8), ALU.mult)
            ve.op(v.tensor_tensor, q3[:, 8:10], q3[:, 8:10], bc(qkn[:, l, 1, :], 1, 2), ALU.mult)
            if s == LAT:
                rope(qk, 10, axial[:, tt, 0, :], axial[:, tt, 1, :])
            heads_T(proj[:, tt, 0:512], tt, 8, qT, 0)
            heads_T(proj[:, tt, 512:640], tt, 2, kT, 0 if s == CTX else T)
            if s == CTX:
                ve.op(v.tensor_copy, vctx[:, tt, :], proj[:, tt, V0:V0 + 128], after=[ac.now(), pe.now()])

    def mixer(l, s, with_out):
        mixer_in(l, s)
        if with_out:
            nkeys = T if s == CTX else 2 * T

            def vals(g, b):
                if b < NT:
                    return vctx[:, b, g * HD:(g + 1) * HD]
                return proj[:, b - NT, V0 + g * HD:V0 + (g + 1) * HD]
            attention(8, 4, qT, kT, lambda tt: nkeys, vals, None, into_cat)
        ssd(l, s, with_out)
        if with_out:
            project_out(i["w_out"][l])
            add_normed(s, 0)

    for l in range(2):
        layer_modulation(i["w_mod"][l], i["b_mod"][l], 0, 2, l, 2 + l)
        load_rows((ssdn[:], i["ssd_norm"][l].partition_broadcast(P)),
                  (prow[:, 0, :], i["norm_mix_post"][l].partition_broadcast(P)),
                  (prow[:, 1, :], i["norm_ffn_post"][l].partition_broadcast(P)))
        for s in (CTX, LAT):
            mixer(l, s, s == LAT or l == 0)
        for s in ((CTX, LAT) if l == 0 else (LAT,)):
            normed_T(s, 1)
            dense(i["w_gate"][l], i["w_up"][l], i["w_down"][l])
            add_normed(s, 1)

    layer_modulation(i["w_ada_2"][0], i["b_ada_2"][0], 2, 1, 4, 6)
    off[0] = 0
    proj2 = wide[:, 0:NT * IN2].rearrange("p (t n) -> p t n", t=NT)
    qT2 = cut(4096).rearrange("p (h q) -> p h q", h=16)
    keep = off[0]
    kT2 = cut(1024).rearrange("p (g q) -> p g q", g=4)
    iqT = cut(2304).rearrange("p (h q) -> p h q", h=9)
    score = cut(512).rearrange("p (t k) -> p t k", t=NT)
    left = cut(256)
    rel = cut(512).rearrange("p (a k) -> p a k", a=2)
    m8 = cut(8)
    keys2 = lambda tt: (tt + 1) * P

    normed_T(LAT, 0)
    product(i["a_w_in_2"][0], 0, IN2, keep_in(proj2), [0, 1, 2, 3])
    for tt in range(NT):
        cos, sin = rope2[:, tt, 0, :], rope2[:, tt, 1, :]
        rope(proj2[:, tt, 0:1024], 16, cos, sin)
        rope(proj2[:, tt, DK0:DV0], 4, cos, sin)
        rope(proj2[:, tt, IQ0:IW0], 9, cos, sin)
        heads_T(proj2[:, tt, 0:1024], tt, 16, qT2, 0)
        heads_T(proj2[:, tt, DK0:DV0], tt, 4, kT2, 0)
        heads_T(proj2[:, tt, IQ0:IW0], tt, 9, iqT, 0)
        ve.op(v.tensor_scalar, proj2[:, tt, IW0:IN2], proj2[:, tt, IW0:IN2], IDX_SCALE, None, ALU.mult)
    for tt in range(NT):
        nk = keys2(tt)
        sc = score[:, tt, 0:nk]
        for h in range(8):
            u = h % 2
            bk = bank_for_pe(u)
            pe.wait(ac.now())
            pe.free(t.matmul, bk[:, 0:nk], iqT[0:HD, h, tt * P:(tt + 1) * P], iqT[0:HD, 8, 0:nk], start=True, stop=True)
            ac.op(a.activation, rel[:, u, 0:nk], bk[:, 0:nk], ACT.Relu, after=[pe.now(), ve.now()])
            read_by(u, ac.now())
            wi = proj2[:, tt, IW0 + h:IW0 + h + 1]
            if h == 0:
                ve.op(v.tensor_scalar, sc, rel[:, u, 0:nk], wi, None, ALU.mult, after=[ac.now()])
            else:
                ve.op(v.scalar_tensor_tensor, sc, rel[:, u, 0:nk], wi, sc, ALU.mult, ALU.add, after=[ac.now()])
        ve.op(v.tensor_tensor, sc, sc, causal[:, tt, 0:nk], ALU.add)
        ve.op(v.tensor_copy, left[:, 0:nk], sc)
        for _ in range(TOPK // 8):
            ve.op(v.max, m8, left[:, 0:nk])
            ve.op(v.match_replace, left[:, 0:nk], m8, left[:, 0:nk], TAKEN)
        ve.op(v.tensor_scalar, sc, left[:, 0:nk], TAKEN / 2, NEG, ALU.is_gt, ALU.mult)
        ve.op(v.tensor_tensor, sc, sc, causal[:, tt, 0:nk], ALU.add)
    meet()
    attention(16, 4, qT2, kT2, keys2, lambda g, b: proj2[:, b, DV0 + g * HD:DV0 + (g + 1) * HD],
              lambda tt: score[:, tt, :], into_cat)
    project_out(i["a_w_out_2"][0])
    add_gated(0, acc_tile)
    normed_T(LAT, 1)
    dense(i["ffn_w_gate_2"][0], i["ffn_w_up_2"][0], i["ffn_w_down_2"][0])
    add_gated(1, acc_tile)

    modulation(i["w_kv_ada_2"], i["b_kv_ada_2"], 4, 2, 1)
    norm_columns(2, 0, D, 8, 1)
    meet()
    layer_modulation(i["w_ada_2"][1], i["b_ada_2"][1], 2, 1, 5, 7)
    off[0] = keep
    kv = wide[:, 0:NT * 1536].rearrange("p (t n) -> p t n", t=NT)
    projq = wide[:, 3072:3072 + NT * IN3].rearrange("p (t n) -> p t n", t=NT)
    ksT = cut(1024).rearrange("p (g q) -> p g q", g=4)
    kwT = cut(1024).rearrange("p (g q) -> p g q", g=4)
    dup = cut(512).rearrange("p (h a f) -> p h a f", h=4, a=2)
    win = cut(1024).rearrange("p (h q) -> p h q", h=4)
    xw = cut(16 * 60).rearrange("p (c h n) -> p c h n", c=16, h=4)
    hid = cut(256)
    hidT = cut(120).rearrange("p (c r) -> p c r", c=2)
    kcT = cut(60)
    vc = cut(256).rearrange("p (g f) -> p g f", g=4)
    pc = cut(240).rearrange("p (h n) -> p h n", h=16)
    pcT = cut(1024).rearrange("p (a h q) -> p a h q", a=2, h=4)
    gcf = cut(96).rearrange("p (t g) -> p t g", t=NT)
    cmx = cut(32)

    normed_T(LAT, 2)
    product(i["w_kv_2"], 0, 1536, keep_in(kv), [0, 1, 2, 3])
    for tt in range(NT):
        cos, sin = rope2[:, tt, 0, :], rope2[:, tt, 1, :]
        for kind in (0, 2, 4):
            rope(kv[:, tt, kind * 256:(kind + 1) * 256], 4, cos, sin)
        heads_T(kv[:, tt, 512:768], tt, 4, ksT, 0)
        heads_T(kv[:, tt, 1024:1280], tt, 4, kwT, 0)
    for n in range(2):
        for tt in range(NT):
            ve.op(v.tensor_copy, dup, bc(kv[:, tt, n * 256:(n + 1) * 256].rearrange("p (h f) -> p h f", f=HD), 2, 2),
                  after=[ac.now(), pe.now()])
            bk = bank_for_pe(2)
            pe.wait(ve.now())
            for h in range(4):
                pe.free(t.transpose, bk[:, h * P:(h + 1) * P], dup[:, h].rearrange("p a f -> p (a f)"), ident[:])
            b3 = bk.rearrange("p (h q) -> p h q", h=4)
            ve.op(v.tensor_copy, win[0:HD, :, tt * P:(tt + 1) * P], b3[0:HD], after=[pe.now()])
            lo = 1 if tt == 0 else 0
            ve.op(v.tensor_copy, win[HD:P, :, tt * P + lo - 1:(tt + 1) * P - 1], b3[HD:P, :, lo:P])
            read_by(2, ve.now())
        for c in range(16):
            ve.op(v.tensor_scalar, xw[:, c], win[:, :, 2 * c:2 * c + CMPS * (NCMP - 1) + 1:CMPS], pe2[:, n, c:c + 1], None,
                  ALU.add)
        slot = w_slot()
        tile = slot.ap[:].rearrange("p (c n) -> p c n", c=16)
        pe.wait(fetch(slot, (tile, i["cmp_w1_%s_2" % "kv"[n]].rearrange("(c p) n -> p c n", p=P))))
        bk = bank_for_pe(3)
        pe.wait(ve.now())
        for c in range(16):
            pe.free(t.matmul, bk[0:60, 0:256], xw[:, c].rearrange("p h n -> p (h n)"), tile[:, c, :],
                    start=(c == 0), stop=(c == 15))
        slot.reader = pe.now()
        ac.op(a.activation, hid[0:60], bk[0:60, 0:256], ACT.Gelu_apprx_tanh, after=[pe.now()])
        read_by(3, ac.now())
        bk = bank_for_pe(2)
        pe.wait(ac.now())
        for c in range(2):
            pe.free(t.transpose, bk[:, c * 60:(c + 1) * 60], hid[0:60, c * P:(c + 1) * P], ident[0:60, 0:60])
        ve.op(v.tensor_copy, hidT, bk[:, 0:120].rearrange("p (c r) -> p c r", c=2), after=[pe.now()])
        read_by(2, ve.now())
        bk = bank_for_pe(3)
        pe.wait(ve.now())
        if n == 0:
            for c in range(2):
                pe.free(t.matmul, bk[0:HD, 0:60], w2[:, n, c, :], hidT[:, c, :], start=(c == 0), stop=(c == 1))
            ve.op(v.tensor_copy, kcT[0:HD], bk[0:HD, 0:60], after=[pe.now()])
        else:
            for g in range(4):
                for c in range(2):
                    pe.free(t.matmul, bk[0:NCMP, g * HD:(g + 1) * HD], hidT[:, c, g * NCMP:(g + 1) * NCMP], w2[:, n, c, :],
                            start=(c == 0), stop=(c == 1))
            ve.op(v.tensor_copy, vc[0:NCMP], bk[0:NCMP, 0:256].rearrange("p (g f) -> p g f", g=4), after=[pe.now()])
        read_by(3, ve.now())
    normed_T(LAT, 0)
    product(i["b_w_q_2"][0], 0, IN3, keep_in(projq), [0, 1, 2, 3])
    for tt in range(NT):
        rope(projq[:, tt, 0:1024], 16, rope2[:, tt, 0, :], rope2[:, tt, 1, :])
        heads_T(projq[:, tt, 0:1024], tt, 16, qT2, 0)
    ac.op(a.activation, gcf, projq[:, :, 1024:IN3], ACT.Exp, scale=-1.0, after=[ve.now()])
    ve.op(v.tensor_scalar, gcf, gcf, 1.0, None, ALU.add, after=[ac.now()])
    ve.op(v.reciprocal, gcf, gcf)
    for tt in range(NT):
        bk = bank_for_pe(0)
        pe.wait(ac.now())
        for h in range(16):
            pe.free(t.matmul, bk[:, h * NCMP:(h + 1) * NCMP], qT2[0:HD, h, tt * P:(tt + 1) * P],
                    kcT[0:HD, (h // 4) * NCMP:(h // 4 + 1) * NCMP], start=True, stop=True)
        s3 = bk[:, 0:240].rearrange("p (h n) -> p h n", h=16)
        ve.op(v.tensor_scalar, pc, s3, 0.125, None, ALU.mult, after=[pe.now()])
        read_by(0, ve.now())
        ve.op(v.tensor_tensor, pc, pc, bc(cmpmask[:, tt, 0, :], 1, 16), ALU.add)
        ve.op(v.tensor_reduce, cmx[:, 0:16], pc, AX, ALU.max)
        ve.op(v.tensor_tensor, pc, pc, bc(cmx[:, 0:16], 2, NCMP), ALU.subtract)
        ac.op(a.activation, pc, pc, ACT.Exp, after=[ve.now()])
        ve.op(v.tensor_reduce, cmx[:, 16:32], pc, AX, ALU.add, after=[ac.now()])
        ve.op(v.tensor_tensor, pc, pc, bc(cmpmask[:, tt, 1, :], 1, 16), ALU.mult)
        ve.op(v.reciprocal, cmx[:, 16:32], cmx[:, 16:32])
        ve.op(v.tensor_tensor, cmx[:, 16:32], cmx[:, 16:32], gcf[:, tt, 0:48:3], ALU.mult)
        for h0 in range(0, 16, 4):
            u = (h0 // 4) % 2
            bk = bank_for_pe(2 + u)
            pe.wait(ve.now())
            for h in range(4):
                pe.free(t.transpose, bk[0:NCMP, h * P:(h + 1) * P], pc[:, h0 + h, :], ident[:])
            ve.op(v.tensor_copy, pcT[0:NCMP, u], bk[0:NCMP, :].rearrange("p (h q) -> p h q", h=4), after=[pe.now()])
            read_by(2 + u, ve.now())
            o = bank_for_pe(4 + h0 // 8)
            pe.wait(ve.now())
            for h in range(4):
                c0 = ((h0 + h) % 8) * HD
                pe.free(t.matmul, o[:, c0:c0 + HD], pcT[0:NCMP, u, h, :], vc[0:NCMP, h0 // 4, :], start=True, stop=True)
            if h0 % 8 == 4:
                ve.wait(pe.now())
                into_cat(tt, h0 - 4, o.rearrange("p (h f) -> p h f", f=HD), cmx[:, 16 + h0 - 4:16 + h0 + 4])
                read_by(4 + h0 // 8, ve.now())

    def add_branch(branch):
        def finish(tt, h0, o, inv):
            ve.op(v.tensor_tensor, inv, inv, gcf[:, tt, 3 * h0 + branch:3 * h0 + branch + 22:3], ALU.mult)
            th = tmp[:, 0:512].rearrange("p (h f) -> p h f", f=HD)
            ve.op(v.tensor_tensor, th, o, bc(inv, 2, HD), ALU.mult)
            dst = cat[:, tt, h0 * HD:(h0 + 8) * HD]
            ve.op(v.tensor_tensor, dst, dst, tmp[:, 0:512], ALU.add)
        return finish

    for branch, kTb, v0 in ((1, ksT, 768), (2, kwT, 1280)):
        attention(16, 4, qT2, kTb, keys2, lambda g, b: kv[:, b, v0 + g * HD:v0 + (g + 1) * HD],
                  lambda tt: causal[:, tt, :], add_branch(branch))
    project_out(i["b_w_out_2"][0])
    add_gated(0, acc_tile)

    normed_T(LAT, 1)
    load_rows((prow[:, 0, :], i["final_gain_2"].partition_broadcast(P)))
    off[0] = 0
    utok = cut(2 * D).rearrange("p (t n) -> p t n", t=NT)
    XTe = cut(D).rearrange("p (k q) -> p k q", k=KD)
    onehot = cut(256).rearrange("p (t q) -> p t q", t=NT)
    gated = cut(256).rearrange("p (t q) -> p t q", t=NT)
    scat = cut(256).rearrange("p (t q) -> p t q", t=NT)
    yexp = cut(D)
    gate = cut(2 * 9).rearrange("p (t e) -> p t e", t=NT)
    slot_of = cut(4 * 9).rearrange("p (c t e) -> p c t e", c=2, t=NT)
    member = cut(16).rearrange("p (t e) -> p t e", t=NT)
    top, topf, one, cnt = (cut(8) for _ in range(4))
    topi, full = sb("topi", [P, 8], U32), sb("full", [P, 1], I32)
    ve.op(v.memset, gate, 0.0)
    ve.op(v.memset, slot_of, -1.0)
    ve.op(v.memset, moe_y, 0.0)
    iota8, iotas = const["iota"][:, 0:8], const["iota"][:]
    for tt in range(NT):
        bk = bank_for_pe(4)
        pe.wait(ve.now())
        for k in range(KD):
            pe.free(t.matmul, bk[:, 0:NEXP], XT[:, k, tt * P:(tt + 1) * P], wr[:, k, :], start=(k == 0), stop=(k == KD - 1))
        ve.op(v.tensor_copy, one, bk[:, 0:NEXP], after=[pe.now()])
        read_by(4, ve.now())
        ve.op(v.max, top, one)
        ve.op(v.max_index, topi[:], top, one)
        ve.op(v.tensor_copy, topf, topi[:])
        ve.op(v.tensor_tensor, top[:, 2:3], top[:, 1:2], top[:, 0:1], ALU.subtract)
        ac.op(a.activation, top[:, 3:4], top[:, 2:3], ACT.Exp, after=[ve.now()])
        ve.op(v.tensor_scalar, top[:, 4:5], top[:, 3:4], 1.0, None, ALU.add, after=[ac.now()])
        ve.op(v.reciprocal, top[:, 5:6], top[:, 4:5])
        ve.op(v.tensor_tensor, top[:, 6:7], top[:, 3:4], top[:, 5:6], ALU.mult)
        g8, m8_ = gate[:, tt, 0:8], member[:, tt, :]
        ve.op(v.tensor_scalar, g8, iota8, topf[:, 0:1], top[:, 5:6], ALU.is_equal, ALU.mult)
        ve.op(v.tensor_scalar, one, iota8, topf[:, 1:2], top[:, 6:7], ALU.is_equal, ALU.mult)
        ve.op(v.tensor_tensor, g8, g8, one, ALU.add)
        ve.op(v.tensor_scalar, m8_, iota8, topf[:, 0:1], None, ALU.is_equal)
        ve.op(v.tensor_scalar, one, iota8, topf[:, 1:2], None, ALU.is_equal)
        ve.op(v.tensor_tensor, m8_, m8_, one, ALU.add)
    bk = bank_for_pe(4)
    pe.wait(ve.now())
    pe.free(t.matmul, bk[:, 0:8], tri[:, 0, :], member[:, 0, :], start=True, stop=True)
    pe.free(t.matmul, bk[:, 8:16], ones[:], member[:, 0, :], start=True, stop=False)
    pe.free(t.matmul, bk[:, 8:16], tri[:, 0, :], member[:, 1, :], start=False, stop=True)
    pe.free(t.matmul, bk[:, 16:24], ones[:], member[:, 0, :], start=True, stop=False)
    pe.free(t.matmul, bk[:, 16:24], ones[:], member[:, 1, :], start=False, stop=True)
    ve.op(v.tensor_tensor, slot_of[:, 0, :, 0:8], bk[:, 0:16].rearrange("p (t e) -> p t e", t=NT), member, ALU.mult,
          after=[pe.now()])
    ve.op(v.tensor_reduce, cnt[:, 0:1], bk[:, 16:24], AX, ALU.max)
    read_by(4, ve.now())
    ve.op(v.tensor_scalar, slot_of[:, 0, :, 0:8], slot_of[:, 0, :, 0:8], 1.0, None, ALU.subtract)
    ve.op(v.tensor_scalar, slot_of[:, 1, :, 0:8], slot_of[:, 0, :, 0:8], float(P), None, ALU.subtract)
    ve.op(v.tensor_scalar, full[:], cnt[:, 0:1], float(P), None, ALU.is_gt)
    for tt in range(NT):
        for half in range(2):
            bk = bank_for_pe(5)
            for k in range(4):
                pe.free(t.transpose, bk[:, k * P:(k + 1) * P], XT[:, 4 * half + k, tt * P:(tt + 1) * P], ident[:])
            ve.op(v.tensor_copy, utok[:, tt, half * 512:(half + 1) * 512], bk, after=[pe.now()])
            read_by(5, ve.now())
    gv = [i[n][0].rearrange("e (p k) n -> p e k n", k=KD) for n in ("moe_w_gate_2", "moe_w_up_2")]
    dv = i["moe_w_down_2"][0].rearrange("e (i p k) n -> p (e i) k n", p=P, k=2)
    steps = FEXP // FCOL
    for n in ("onehot", "xsum", "xte", "gated", "scat_t", "scat", "yexp", "back", "ysum"):
        fs[n] = nc.alloc_semaphore("s_m" + n)
        nc.gpsimd.sem_inc(fs[n], 1)
        fn[n] = 1
    s_start = nc.alloc_semaphore("s_start")
    nc.gpsimd.drain().then_inc(s_start, 1)
    for e_ in (pe, ve, ac):
        e_.wait((s_start, 1))
    meet()

    def moe(c):
        base = dict(fn)
        ws, ds = open_slots()
        wn, dn_ = [s.n for s in ws], [s.n for s in ds]
        sg1, hb1 = sg, hb
        hT1 = hT[:, :, :, 0:P]

        def run(e):
            def at(name, i_, plus):
                return e * steps + i_ + (base[name] + plus)

            def of(name, per, plus):
                return e * per + (base[name] + plus)

            def landed(n0, per, u, i_):
                return (e * steps + i_) * (per // 2) + (n0[u] + per - u * (per // 2))

            def load(i_, u):
                nc.sync.wait_ge(fs["gu"], at("gu", i_, -1))
                tile = ws[u].ap[:].rearrange("p (k c n) -> p k c n", k=KD, c=2)
                for g in range(2):
                    src = gv[g][:, bass.ds(e, 1), :, bass.ds(i_ * FCOL, FCOL)].rearrange("p e k n -> p (e k) n")
                    nc.sync.dma_start(tile[:, :, g, :], src).then_inc(ws[u].sem, 16)

            def load_down(i_, u):
                nc.sync.wait_ge(fs["dn"], at("dn", i_, -1))
                nc.sync.dma_start(ds[u].ap[:].rearrange("p (k n) -> p k n", k=2),
                                  dv[:, bass.ds(e * steps + i_, 1)].rearrange("p i k n -> p (i k) n")).then_inc(ds[u].sem, 16)

            def up(i_, u):
                t.wait_ge(ws[u].sem, landed(wn, 32, u, i_))
                t.wait_ge(fs["h"], at("h", i_, -1))
                if isinstance(i_, int) and i_ == 0:
                    t.wait_ge(fs["xte"], of("xte", 2, 2))
                for k in range(KD):
                    mm = t.matmul(psum[:, 2 + u, :], XTe[:, k, :], ws[u].ap[:, k * 512:(k + 1) * 512],
                                  start=(k == 0), stop=(k == KD - 1))
                mm.then_inc(fs["gu"], 1)
                a.wait_ge(fs["gu"], at("gu", i_, 1))
                a.wait_ge(fs["h"], at("h", i_, -1))
                a.activation(sg1[:, u, :], psum[:, 2 + u, 0:FCOL], ACT.Silu).then_inc(fs["silu"], 1)

            def hidden(i_, u):
                v.wait_ge(fs["silu"], at("silu", i_, 1))
                v.wait_ge(fs["tr"], at("tr", i_, -1))
                v.tensor_tensor(hb1[:, u, :], sg1[:, u, :], psum[:, 2 + u, FCOL:512], ALU.mult).then_inc(fs["h"], 1)

            def turn(i_, u):
                t.wait_ge(fs["h"], at("h", i_, 1))
                t.wait_ge(fs["ev"], at("ev", i_, -1))
                for k in range(2):
                    mm = t.transpose(psum[:, 4 + u, k * P:(k + 1) * P], hb1[:, u, k:FCOL:2], ident[:])
                mm.then_inc(fs["tr"], 1)
                v.wait_ge(fs["tr"], at("tr", i_, 1))
                v.wait_ge(fs["dn"], at("dn", i_, -1))
                v.tensor_copy(hT1[:, u], psum[:, 4 + u, 0:256].rearrange("p (k q) -> p k q", k=2)).then_inc(fs["ev"], 1)

            def downs(i_, u, start=False, stop=False):
                t.wait_ge(ds[u].sem, landed(dn_, 16, u, i_))
                t.wait_ge(fs["ev"], at("ev", i_, 1))
                if start:
                    t.wait_ge(fs["yexp"], of("yexp", 2, 0))
                for k in range(2):
                    for h in range(2):
                        mm = t.matmul(psum[:, h, :], hT1[:, u, k, :], ds[u].ap[:, k * D + h * 512:k * D + (h + 1) * 512],
                                      start=start and k == 0, stop=stop and k == 1)
                mm.then_inc(fs["dn"], 1)

            def step(i_, u):
                load(i_, u)
                up(i_, u)
                if not isinstance(i_, int) or i_ > 0:
                    load_down(i_ - 1, 1 - u)
                    turn(i_ - 1, 1 - u)
                hidden(i_, u)
                if not isinstance(i_, int) or i_ > 1:
                    downs(i_ - 2, u, start=isinstance(i_, int) and i_ == 2)

            for i_ in range(4):
                step(i_, i_ % 2)
            with nc.Fori(0, (steps - 4) // 2) as r:
                for u in range(2):
                    step(r * 2 + (4 + u), u)
            load_down(steps - 1, 1)
            gather(e + 1, of)
            turn(steps - 1, 1)
            downs(steps - 2, 0)
            v.wait_ge(fs["scat_t"], of("scat_t", 1, 0))
            for tt in range(NT):
                ins = v.tensor_scalar(gated[:, tt, :], iotas, slot_of[:, c, tt, bass.ds(e, 1)], gate[:, tt, bass.ds(e, 1)],
                                      ALU.is_equal, ALU.mult)
            ins.then_inc(fs["gated"], 1)
            t.wait_ge(fs["gated"], of("gated", 1, 1))
            t.wait_ge(fs["xte"], of("xte", 2, 4))
            for tt in range(NT):
                mm = t.transpose(psum[:, 6, tt * P:(tt + 1) * P], gated[:, tt, :], ident[:])
            mm.then_inc(fs["scat_t"], 1)
            v.wait_ge(fs["scat_t"], of("scat_t", 1, 1))
            v.wait_ge(fs["back"], of("back", 4, 0))
            v.tensor_copy(scat, psum[:, 6, 0:256].rearrange("p (t q) -> p t q", t=NT)).then_inc(fs["scat"], 1)
            downs(steps - 1, 1, stop=True)
            a.wait_ge(fs["dn"], at("dn", steps, 0))
            a.wait_ge(fs["back"], of("back", 4, 0))
            for h in range(2):
                a.activation(yexp[:, h * 512:(h + 1) * 512], psum[:, h, :], ACT.Copy).then_inc(fs["yexp"], 1)
            t.wait_ge(fs["scat"], of("scat", 1, 1))
            for q in range(4):
                h, tt = q // 2, q % 2
                t.wait_ge(fs["yexp"], of("yexp", 2, h + 1))
                if q >= 2:
                    t.wait_ge(fs["ysum"], of("ysum", 4, q - 1))
                t.matmul(psum[:, 6 + tt, :], scat[:, tt, :], yexp[:, h * 512:(h + 1) * 512],
                         start=True, stop=True).then_inc(fs["back"], 1)
                v.wait_ge(fs["back"], of("back", 4, q + 1))
                v.wait_ge(fs["ysum"], of("ysum", 4, 0))
                y = moe_y[:, tt, h * 512:(h + 1) * 512]
                v.tensor_tensor(y, y, psum[:, 6 + tt, :], ALU.add).then_inc(fs["ysum"], 1)

        def gather(e, of):
            v.wait_ge(fs["xsum"], of("xsum", 2, 2))
            for tt in range(NT):
                ins = v.tensor_scalar(onehot[:, tt, :], iotas, slot_of[:, c, tt, bass.ds(e, 1)], None, ALU.is_equal)
            ins.then_inc(fs["onehot"], 1)
            t.wait_ge(fs["onehot"], of("onehot", 1, 2))
            t.wait_ge(fs["ysum"], of("ysum", 4, 0))
            for half in range(2):
                for k in range(4):
                    kk_ = 4 * half + k
                    for tt in range(NT):
                        mm = t.matmul(psum[:, 6 + half, k * P:(k + 1) * P], utok[:, tt, kk_ * P:(kk_ + 1) * P],
                                      onehot[:, tt, :], start=(tt == 0), stop=(tt == NT - 1))
                mm.then_inc(fs["xsum"], 1)
                a.wait_ge(fs["xsum"], of("xsum", 2, 3 + half))
                a.activation(XTe[:, 4 * half:4 * half + 4, :], psum[:, 6 + half, :].rearrange("p (k q) -> p k q", k=4),
                             ACT.Copy).then_inc(fs["xte"], 1)

        gather(0, lambda name, per, plus: base[name] + plus - (per if name != "ysum" else 0))
        with nc.Fori(0, NEXP) as e:
            run(e)
        total = NEXP * steps
        for n in ("gu", "silu", "h", "tr", "ev", "dn"):
            fn[n] += total
        for n, per, more in (("onehot", 1, 1), ("xsum", 2, 2), ("xte", 2, 2), ("gated", 1, 0), ("scat_t", 1, 0),
                             ("scat", 1, 0), ("yexp", 2, 0), ("back", 4, 0), ("ysum", 4, 0)):
            fn[n] += per * NEXP + more
        close_slots(ws, ds, total)
        for e_ in (nc.tensor, nc.vector, nc.scalar):
            e_.wait_ge(fs["ysum"], fn["ysum"])
            e_.wait_ge(fs["xte"], fn["xte"])

    moe(0)
    for e_ in (nc.tensor, nc.vector, nc.scalar, nc.sync, nc.gpsimd):
        e_.wait_ge(ve.sem, ve.n)
    overfull = nc.values_load(full[0:1, 0:1], min_val=0, max_val=1)
    with nc.If(overfull > 0):
        moe(1)
    add_gated(1, lambda tt: moe_y[:, tt, :])

    s_out = nc.alloc_semaphore("s_out")
    ov = out[0].rearrange("(t p) d -> p t d", p=P)
    for tt in range(NT):
        ss = st[:, tt:tt + 1]
        ac.op(a.activation, xn[:], x[:, LAT, tt, :], ACT.Square, accum_out=ss, after=[ve.now()])
        rstd(ss, D, 1)
        ve.op(v.scalar_tensor_tensor, cat[:, tt, :], x[:, LAT, tt, :], ss, prow[:, 0, :], ALU.mult, ALU.mult,
              after=[(s_row, rows[0])])
        nc.sync.wait_ge(ve.sem, ve.n)
        nc.sync.dma_start(ov[:, tt, :], cat[:, tt, :]).then_inc(s_out, 16)
    nc.sync.wait_ge(s_out, 16 * NT)


NAMES = ["x", "c", "ctx", "c_ctx", "w_mod", "b_mod", "norm_mix_pre", "norm_mix_post", "norm_ffn_pre",
         "norm_ffn_post", "w_in", "q_norm", "k_norm", "conv_w", "conv_b", "dt_bias_fwd", "dt_bias_bwd",
         "a_log_fwd", "a_log_bwd", "d_skip", "ssd_norm", "w_out", "w_gate", "w_up", "w_down", "c_2",
         "positions_2", "attn_gain_2", "ffn_gain_2", "w_ada_2", "b_ada_2", "a_w_in_2", "a_w_out_2",
         "b_w_q_2", "b_w_out_2", "kv_gain_2", "w_kv_ada_2", "b_kv_ada_2", "w_kv_2", "cmp_pe_k_2",
         "cmp_w1_k_2", "cmp_w2_k_2", "cmp_pe_v_2", "cmp_w1_v_2", "cmp_w2_v_2", "ffn_w_gate_2",
         "ffn_w_up_2", "ffn_w_down_2", "moe_w_router_2", "moe_w_gate_2", "moe_w_up_2", "moe_w_down_2",
         "final_gain_2"]


def kernel(**inputs):
    import numpy as _np
    import concourse.bacc as _bacc
    from concourse import mybir as _mybir
    from concourse.bass_utils import run_bass_kernel_spmd as _run

    nc = _bacc.Bacc("TRN2", target_bir_lowering=False, num_devices=1)
    arrays, args = {}, {}
    for name in NAMES:
        a = _np.ascontiguousarray(inputs[name])
        arrays["in_" + name] = a
        args[name] = nc.dram_tensor("in_" + name, a.shape, _mybir.dt.from_np(a.dtype), kind="ExternalInput").ap()
    out = nc.dram_tensor("out", (1, T, D), F32, kind="ExternalOutput").ap()
    build(nc, args, out)
    r = _run(nc, [arrays], core_ids=[0])
    return r.results[0]["out"]
```

```python
import math

import numpy as np
import concourse.bass as bass
from concourse import mybir

F32 = mybir.dt.float32
I32 = mybir.dt.int32
U32 = mybir.dt.uint32
F32R = mybir.dt.float32r
ALU = mybir.AluOpType
ACT = mybir.ActivationFunctionType
AX = mybir.AxisListType.X

P = 128
D = 1024
KD = D // P
T = 256
NT = T // P
EPS = 1e-6
NEG = -1e30
TAKEN = -3e38
HD = 64
LAT, CTX = 0, 1
Q0, K0, V0, Z0, XBC0, DT0, IN1 = 0, 512, 640, 768, 1280, 2304, 2312
DK0, DV0, IQ0, IK0, IW0, IN2 = 1024, 1280, 1536, 2048, 2112, 2120
IN3 = 1072
TOPK = 64
NCMP, CMPL, CMPS = 15, 32, 16
FCOL = 256
NEXP = 8
FEXP = 3584
FDENSE = 2816
ROPE_THETA = 10000.0
IDX_SCALE = 8 ** -0.5 * 64 ** -0.5


class Engine:

    def __init__(self, nc, engine, name):
        self.e, self.sem, self.n, self.met = engine, nc.alloc_semaphore(name), 0, {}

    def now(self):
        return (self.sem, self.n)

    def wait(self, *marks):
        for sem, value in marks:
            if value > self.met.get(sem.name, 0):
                self.e.wait_ge(sem, value)
                self.met[sem.name] = value

    def op(self, f, *a, after=(), **k):
        self.wait(*after, self.now())
        return self.free(f, *a, **k)

    def free(self, f, *a, **k):
        f(*a, **k).then_inc(self.sem, 1)
        self.n += 1
        return self.now()


class Slot:

    def __init__(self, nc, name, ap):
        self.ap, self.sem, self.n, self.reader = ap, nc.alloc_semaphore(name), 0, None


def bc(ap, axis, n):
    shape = list(ap.shape)
    return ap.unsqueeze(axis).broadcast_to(shape[:axis] + [n] + shape[axis:])


def constants():
    p = np.arange(P)
    tri = (p[:, None] <= p[None, :]).astype(np.float32)
    c = {"ident": np.eye(P, dtype=np.float32), "ones": np.ones((P, P), np.float32)}
    c["tri"] = np.stack([tri, tri.T], 1)
    c["trineg"] = np.where(c["tri"] > 0, 0.0, NEG).astype(np.float32)
    pos = np.arange(T)
    fr = (np.float32(ROPE_THETA) ** (-np.arange(16, dtype=np.float32) / np.float32(16))).astype(np.float32)
    ang = np.concatenate([(pos // 64).astype(np.float32)[:, None] * fr, (pos % 64).astype(np.float32)[:, None] * fr], 1)
    cos, sin = np.cos(ang.astype(np.float64)), np.sin(ang.astype(np.float64))
    tab = np.stack([np.concatenate([cos, cos], 1), np.concatenate([-sin, sin], 1)], 1)
    c["axial"] = tab.reshape(NT, P, 2, HD).transpose(1, 0, 2, 3).astype(np.float32)
    inv = np.float32(1.0) / (np.float32(ROPE_THETA) ** (np.arange(0, HD, 2, dtype=np.float32) / np.float32(HD)))
    c["inv"] = np.broadcast_to(inv.astype(np.float32), (P, 32)).copy()
    key = np.arange(T)
    tok = (np.arange(NT)[None, :] * P + p[:, None])
    c["causal"] = np.where(key[None, None, :] <= tok[:, :, None], 0.0, NEG).astype(np.float32)
    end = np.arange(NCMP) * CMPS + CMPL - 1
    ok = end[None, None, :] <= tok[:, :, None]
    c["cmpmask"] = np.stack([np.where(ok, 0.0, NEG), ok], 2).astype(np.float32)
    c["iota"] = np.broadcast_to(np.arange(P, dtype=np.float32), (P, P)).copy()
    sel = np.zeros((2, 2, P), np.float32)
    sel[0, 0], sel[1, 1] = 1.0, 1.0
    c["sel"] = sel
    return c


def build(nc, i, out):
    sp = Engine(nc, nc.sync, "s_sp")
    pe = Engine(nc, nc.tensor, "s_pe")
    ve = Engine(nc, nc.vector, "s_ve")
    ac = Engine(nc, nc.scalar, "s_ac")
    po = Engine(nc, nc.gpsimd, "s_po")
    v, a, t = nc.vector, nc.scalar, nc.tensor

    def sb(name, shape, dt=F32):
        return nc.alloc_sbuf_tensor(name, shape, dt)

    views = {}

    def sb_r(name, shape):
        buf = sb(name, shape)
        start = nc.sbuf_base - 4 * int(np.prod(shape[1:]))
        views[buf.name] = nc.alloc_sbuf_tensor_at(name + "_r", shape, F32R, offset=start)
        return buf

    def one_pass(ap):
        return bass.AP(tensor=views[ap.tensor.name], offset=ap.offset, ap=ap.ap)

    x = sb("x", [P, 2, NT, D])
    wide = sb_r("wide", [P, 5216])
    XT = sb_r("XT", [P, KD, T])
    cat = sb_r("cat", [P, NT, D])
    stage = sb("stage", [2, 3 * 512])
    grow = sb("grow", [P, 2, D])
    prow = sb("prow", [P, 2, D])
    scratch = sb_r("scratch", [P, 2 * D])
    xn, tmp = scratch[:, 0:D], scratch[:, D:2 * D]
    arena = sb_r("arena", [P, 11904])
    work = sb_r("work", [P, 3072])
    w_slots = [Slot(nc, f"s_w{s}", sb_r(f"wslot{s}", [P, 4096])) for s in range(2)]
    d_slots = [Slot(nc, f"s_d{s}", sb_r(f"dslot{s}", [P, 2048])) for s in range(2)]
    ring = {"w": 0, "d": 0}
    psum = nc.alloc_psum_tensor("psum", [P, 8, 512], F32)
    bank_free = [[] for _ in range(8)]

    ccol = sb("ccol", [P, 3, KD])
    s_cond = nc.alloc_semaphore("s_cond")
    for n, name in enumerate(["c", "c_ctx", "c_2"]):
        src = i[name] if name == "c_ctx" else i[name][0]
        nc.scalar.dma_start(ccol[:, n, :], src.rearrange("(p k) -> p k", k=KD)).then_inc(s_cond, 16)

    cs = sb("cs", [P, KD, 4])
    conditioned = ac.op(a.activation, cs[:].rearrange("p k c -> p c k")[:, 0:3, :], ccol[:], ACT.Silu,
                        after=[(s_cond, 48)])

    const = {}
    s_par = nc.alloc_semaphore("s_par")
    par = [0]

    def param(dst, src):
        nc.scalar.dma_start(dst, src).then_inc(s_par, 16)
        par[0] += 16

    for name, arr in constants().items():
        flat = arr.reshape(arr.shape[0], -1)
        buf = sb("c_" + name, list(flat.shape))
        param(buf[:], nc.inline_tensor(flat, name="k_" + name).ap())
        const[name] = buf
    ident, ones = const["ident"], const["ones"]
    tri = const["tri"][:].rearrange("p (d i) -> p d i", d=2)
    trineg = const["trineg"][:].rearrange("p (d i) -> p d i", d=2)
    axial = const["axial"][:].rearrange("p (t c h) -> p t c h", t=NT, c=2)
    causal = const["causal"][:].rearrange("p (t k) -> p t k", t=NT)
    cmpmask = const["cmpmask"][:].rearrange("p (t c n) -> p t c n", t=NT, c=2)
    sel = const["sel"][:].rearrange("p (s q) -> p s q", s=2)

    gcol = sb("gcol", [P, 9, KD])
    gains = [("norm_mix_pre", 0), ("norm_mix_pre", 1), ("norm_ffn_pre", 0), ("norm_ffn_pre", 1),
             ("attn_gain_2", 0), ("attn_gain_2", 1), ("ffn_gain_2", 0), ("ffn_gain_2", 1), ("kv_gain_2", None)]
    for n, (name, l) in enumerate(gains):
        src = i[name] if l is None else i[name][l]
        param(gcol[:, n, :], src.rearrange("(p k) -> p k", k=KD))
    qkn = sb("qkn", [P, 2, 2, HD])
    dtp = sb("dtp", [P, 2, 3, 2, 8])
    ssdn = sb("ssdn", [P, 512])
    for l in range(2):
        param(qkn[:, l, 0, :], i["q_norm"][l].partition_broadcast(P))
        param(qkn[:, l, 1, :], i["k_norm"][l].partition_broadcast(P))
        for d, way in enumerate(("fwd", "bwd")):
            param(dtp[:, l, 0, d, :], i["dt_bias_" + way][l].partition_broadcast(P))
            param(dtp[:, l, 1, d, :], i["a_log_" + way][l].partition_broadcast(P))
        param(dtp[:, l, 2, 0, :], i["d_skip"][l].partition_broadcast(P))
        taps = (xn, tmp)[l]
        param(taps[0:5, :], i["conv_w"][l])
        param(taps[5:6, :], i["conv_b"][l:l + 1])
    posi = sb("posi", [P, NT], I32)
    with nc.allow_non_contiguous_dma(reason="256 positions"):
        param(posi[:], i["positions_2"][0].rearrange("(t p) -> p t", p=P))
    wr = sb("wr", [P, KD, NEXP])
    param(wr[:], i["moe_w_router_2"][0].rearrange("(p k) e -> p k e", k=KD))
    w2 = sb("w2", [P, 2, 2, HD])
    pe16 = sb("pe16", [16, 2, P])
    for n, kv in enumerate("kv"):
        param(w2[:, n], i[f"cmp_w2_{kv}_2"].rearrange("(c p) d -> p c d", p=P))
        param(pe16[:, n, :], i[f"cmp_pe_{kv}_2"].rearrange("(c a) d -> c (a d)", a=2))
    for s, name in ((LAT, "x"), (CTX, "ctx")):
        param(x[:, s], i[name][0].rearrange("(t p) d -> p t d", p=P))
    convp = sb("convp", [P, 2, KD, 6])
    col = sb("col", [P, 2, 3, 2, KD])
    st = sb("st", [P, 64])
    rope2 = sb("rope2", [P, NT, 2, HD])
    params = (s_par, par[0])
    s_row = nc.alloc_semaphore("s_row")
    rows = [0]

    def meet():
        marks = [e.now() for e in (pe, ve, ac)]
        for e in (pe, ve, ac):
            e.wait(*marks)

    def bank_for_pe(b):
        pe.wait(*bank_free[b])
        return psum[:, b, :]

    def read_by(b, *marks):
        bank_free[b] = list(marks)

    def load_rows(*pairs):
        ac.wait(ve.now(), ac.now())
        for dst, src in pairs:
            nc.scalar.dma_start(dst, src).then_inc(s_row, 16)
            rows[0] += 16

    def w_slot():
        s = w_slots[ring["w"] % 2]
        ring["w"] += 1
        return s

    def fetch(slot, *pairs):
        if slot.reader:
            sp.wait(slot.reader)
        for dst, src in pairs:
            nc.sync.dma_start(dst, src).then_inc(slot.sem, 16)
            slot.n += 16
        return (slot.sem, slot.n)

    NSTAGE = 3
    s_bias = [nc.alloc_semaphore(f"s_bias{u}") for u in range(NSTAGE)]
    s_kept = [nc.alloc_semaphore(f"s_kept{u}") for u in range(NSTAGE)]
    kept_n, bias_n = [0] * NSTAGE, [0] * NSTAGE
    jobs = [("mod0", i["w_mod"][0], i["b_mod"][0], 12, 0, 2), ("mod1", i["w_mod"][1], i["b_mod"][1], 12, 0, 2),
            ("ada0", i["w_ada_2"][0], i["b_ada_2"][0], 12, 2, 1),
            ("kv", i["w_kv_ada_2"], i["b_kv_ada_2"], 4, 2, 1), ("ada1", i["w_ada_2"][1], i["b_ada_2"][1], 12, 2, 1)]
    row_of = {j[0]: nc.dram_tensor("rows_" + j[0], (j[5], j[3] * 512), F32).ap() for j in jobs}
    ended = {}
    mod_tiles = [(job, j) for job in jobs for j in range(job[3])]
    slot_at, ahead, allow_ahead = {}, [0], [True]
    FIRST = 2 * jobs[0][3]

    def fetch_half(n):
        (name, w, b, nt, first, m), j = mod_tiles[n // 2]
        if n < FIRST and n % 4 >= 2:
            slot = w_slots[n % 2]
        else:
            slot = d_slots[ring["d"] % 2]
            ring["d"] += 1
        slot_at[n] = slot
        if slot.reader:
            sp.wait(slot.reader)
        wv = w.rearrange("(p k) n -> p k n", k=KD)
        nc.sync.dma_start(slot.ap[:, 0:2048].rearrange("p (k n) -> p k n", k=4),
                          wv[:, 4 * (n % 2):4 * (n % 2) + 4, j * 512:(j + 1) * 512]).then_inc(slot.sem, 16)
        slot.n += 16

    def look_ahead(n):
        while ahead[0] <= min(n, 2 * len(mod_tiles) - 1):
            fetch_half(ahead[0])
            ahead[0] += 1

    def load_bias(q):
        if q < len(mod_tiles):
            (name, w, b, nt, first, m), j = mod_tiles[q]
            u = q % NSTAGE
            sp.wait((s_kept[u], kept_n[u]))
            nc.sync.dma_start(stage[0:m, u * 512:(u + 1) * 512], b[j * 512:(j + 1) * 512].partition_broadcast(m)).then_inc(
                s_bias[u], 16)
            bias_n[u] += 16

    def store_rows(q, summed):
        (name, w, b, nt, first, m), j = mod_tiles[q]
        u = q % NSTAGE
        sp.wait(summed)
        nc.sync.dma_start(row_of[name][0:m, j * 512:(j + 1) * 512], stage[0:m, u * 512:(u + 1) * 512]).then_inc(s_kept[u], 16)
        kept_n[u] += 16
        if j == nt - 1:
            ended[name] = [(s_kept[x_], kept_n[x_]) for x_ in range(NSTAGE)]

    def modulations():
        load_bias(0)
        for q, ((name, w, b, nt, first, m), j) in enumerate(mod_tiles):
            u = q % NSTAGE
            rows_ = stage[0:m, u * 512:(u + 1) * 512]
            bank = 6 + q % 2 if 2 * q < FIRST else 7
            for half in range(2):
                n = 2 * q + half
                look_ahead(n if not allow_ahead[0] else max(min(n + 3, FIRST - 1), n + 1))
                if half == 0:
                    if q and j:
                        store_rows(q - 1, summed)
                    load_bias(q + 1)
                slot = slot_at.pop(n)
                for k in range(4):
                    if k == 0:
                        pe.wait((slot.sem, slot.n))
                        if half == 0:
                            pe.wait(*bank_free[bank])
                    mm = t.matmul(psum[0:m, bank, :], cs[:, 4 * half + k, first:first + m], slot.ap[:, k * 512:(k + 1) * 512],
                                  start=(half == 0 and k == 0), stop=(half == 1 and k == 3))
                    if k == 3:
                        mm.then_inc(pe.sem, 1)
                        pe.n += 1
                        slot.reader = pe.now()
                        if half == 1:
                            summed = ve.op(v.tensor_tensor, rows_, rows_, psum[0:m, bank, :], ALU.add,
                                           after=[pe.now(), (s_bias[u], bias_n[u])])
                            read_by(bank, summed)
                            if j == nt - 1:
                                store_rows(q, summed)
                    yield (n, k)

    progress = modulations()
    at_half = [None]

    def fill(n):
        for _ in range(n):
            at_half[0] = next(progress, None)
            if at_half[0] is None:
                return

    def settle():
        allow_ahead[0] = False
        while at_half[0] and at_half[0] != (ahead[0] - 1, 3) or (at_half[0] and at_half[0][0] % 2 == 0):
            fill(1)
        allow_ahead[0] = True

    pe.wait(conditioned)
    fill(24)
    for e in (pe, ve, ac):
        e.wait(params)
    ac.op(a.activation, dtp[:, :, 1], dtp[:, :, 1], ACT.Exp)
    ve.op(v.tensor_scalar, dtp[:, :, 1], dtp[:, :, 1], -1.0, None, ALU.mult, after=[ac.now()])
    for l in range(2):
        bk = bank_for_pe(l)
        for k in range(KD):
            pe.free(t.transpose, bk[:, 6 * k:6 * k + 6], (xn, tmp)[l][0:6, k * P:(k + 1) * P], ident[0:6, 0:6])
        ve.op(v.tensor_copy, convp[:, l], bk[:, 0:48].rearrange("p (k j) -> p k j", j=6), after=[pe.now()])
        read_by(l, ve.now())
    pe2 = sb("pe2", [P, 2, 16])
    bk = bank_for_pe(2)
    for n in range(2):
        pe.free(t.transpose, bk[:, 16 * n:16 * n + 16], pe16[:, n, :], ident[0:16, 0:16])
    ve.op(v.tensor_copy, pe2[:], bk[:, 0:32].rearrange("p (a b) -> p a b", a=2), after=[pe.now()])
    read_by(2, ve.now())

    tw = work[:, 0:512].rearrange("p (n t f) -> p n t f", n=8, t=NT)
    ang, kk, r, rc, m = (tw[:, n] for n in range(5))
    c1, c2 = 6.28125, float(np.float32(0.0019350052))
    c3 = 2 * math.pi - c1 - c2
    magic = 12582912.0
    posf = st[:, 0:NT]
    ve.op(v.tensor_copy, posf, posi[:])
    for n in range(NT):
        ve.op(v.tensor_scalar, ang[:, n], const["inv"][:], posf[:, n:n + 1], None, ALU.mult)
    ve.op(v.tensor_scalar, kk, ang, 1 / (2 * math.pi), magic, ALU.mult, ALU.add)
    ve.op(v.tensor_scalar, kk, kk, magic, None, ALU.subtract)
    ve.op(v.scalar_tensor_tensor, r, kk, -c1, ang, ALU.mult, ALU.add)
    ve.op(v.scalar_tensor_tensor, r, kk, -c2, r, ALU.mult, ALU.add)
    ve.op(v.scalar_tensor_tensor, r, kk, -c3, r, ALU.mult, ALU.add)
    ve.op(v.tensor_scalar, rc, r, math.pi / 2, None, ALU.add)
    ve.op(v.tensor_scalar, m, rc, math.pi, -2 * math.pi, ALU.is_gt, ALU.mult)
    ve.op(v.tensor_tensor, rc, rc, m, ALU.add)
    lim = 3.1415925
    for s in (r, rc):
        ve.op(v.tensor_scalar, s, s, lim, -lim, ALU.min, ALU.max)
    ac.op(a.activation, rope2[:, :, 0, 0:32], rc, ACT.Sin, after=[ve.now()])
    ac.op(a.activation, rope2[:, :, 0, 32:64], rc, ACT.Sin)
    ac.op(a.activation, rope2[:, :, 1, 32:64], r, ACT.Sin)
    ve.op(v.tensor_scalar, rope2[:, :, 1, 0:32], rope2[:, :, 1, 32:64], -1.0, None, ALU.mult, after=[ac.now()])

    s_col = nc.alloc_semaphore("s_col")
    cols_n = [0]
    s_grow = [nc.alloc_semaphore(f"s_grow{u}") for u in range(2)]
    grow_n, grow_of, grow_free = [0, 0], [], [None, None]

    def load_columns(job, m, *parts):
        while job not in ended:
            fill(1)
        ac.wait(*ended[job], ve.now(), ac.now())
        for which, blk, gain in parts:
            for s in range(m):
                for c, row in ((1, blk), (0, blk + 1)):
                    nc.scalar.dma_start(col[:, s, which, c, :], row_of[job][s, row * D:(row + 1) * D].rearrange(
                        "(p k) -> p k", k=KD)).then_inc(s_col, 16)
                    cols_n[0] += 16
        for which, blk, gain in parts:
            for s in range(m):
                c0 = col[:, s, which, 0, :]
                ve.op(v.scalar_tensor_tensor, c0, c0, 1.0, gcol[:, gain, :], ALU.add, ALU.mult, after=[(s_col, cols_n[0])])

    def ask_gates(job, *uses):
        grow_of.extend((job, s, blk) for s, blk in uses)
        for u in range(2):
            next_gate(u)

    def next_gate(u):
        if grow_of and len([1 for x_ in asked if x_[1] == u]) == 0:
            job, s, blk = grow_of.pop(0)
            po.wait(*ended[job])
            if grow_free[u]:
                po.wait(grow_free[u])
            nc.gpsimd.dma_start(grow[:, u, :], row_of[job][s, blk * D:(blk + 1) * D].partition_broadcast(P)).then_inc(s_grow[u], 16)
            grow_n[u] += 16
            asked.append(((job, s, blk), u))

    asked = []

    def take_gate():
        _, u = asked[0]
        return grow[:, u, :], (s_grow[u], grow_n[u])

    def gate_read():
        _, u = asked.pop(0)
        grow_free[u] = ve.now()
        next_gate(u)

    def rstd(dst, n, width):
        m_ = st[:, 48:48 + width]
        ve.op(v.tensor_scalar, m_, dst, 1.0 / n, EPS, ALU.mult, ALU.add, after=[ac.now()])
        ac.op(a.activation, dst, m_, ACT.Sqrt, after=[ve.now()])
        ve.op(v.reciprocal, dst, dst, after=[ac.now()])
        ve.op(v.tensor_tensor, m_, m_, dst, ALU.mult)
        ve.op(v.tensor_tensor, m_, m_, dst, ALU.mult)
        ve.op(v.tensor_scalar, m_, m_, -0.5, 1.5, ALU.mult, ALU.add)
        ve.op(v.tensor_tensor, dst, dst, m_, ALU.mult)

    px_hi = work[:, 0:2048].rearrange("p (k q) -> p k q", k=KD)

    def split_x(tt, half, src):
        part = (slice(4 * half, 4 * half + 4), slice(tt * P, (tt + 1) * P))
        hi, lo = px_hi[:, part[0], part[1]], XT[:, part[0], part[1]]
        ac.op(a.activation, one_pass(hi), src, ACT.Copy, after=[pe.now(), ve.now()])
        ve.op(low, lo, src, hi, after=[ac.now()])

    def normed_T(s, which, split=False):
        for tt in range(NT):
            ss = st[:, tt:tt + 1]
            ac.op(a.activation, xn, x[:, s, tt, :], ACT.Square, accum_out=ss, after=[ve.now(), pe.now()])
            rstd(ss, D, 1)
            ac.op(a.activation, xn, x[:, s, tt, :], ACT.Copy, scale=ss, after=[ve.now()])
            fill(3)
            for half in range(2):
                bk = bank_for_pe(half)
                pe.wait(ac.now())
                for k in range(4):
                    pe.free(t.transpose, bk[:, k * P:(k + 1) * P], xn[:, 4 * half + k:D:KD], ident[:])
                for k in range(4):
                    kk_ = 4 * half + k
                    ve.op(v.tensor_scalar, XT[:, kk_, tt * P:(tt + 1) * P], bk[:, k * P:(k + 1) * P],
                          col[:, s, which, 0, kk_:kk_ + 1], col[:, s, which, 1, kk_:kk_ + 1],
                          ALU.mult, ALU.add, after=[pe.now()])
                read_by(half, ve.now())
                if split:
                    split_x(tt, half, XT[:, 4 * half:4 * half + 4, tt * P:(tt + 1) * P])

    def cat_T():
        pe.wait(ve.now(), ac.now())
        for tt in range(NT):
            for half in range(2):
                b = 4 + half
                bk = bank_for_pe(b)
                for k in range(4):
                    pe.free(t.transpose, bk[:, k * P:(k + 1) * P], cat[:, tt, 4 * half + k:D:KD], ident[:])
                split_x(tt, half, bk.rearrange("p (k q) -> p k q", k=4))
                read_by(b, ve.now())

    def products3(out_, hi, lo, w_hi, w_lo, start, stop):
        hi, lo, w_hi, w_lo = (one_pass(z) for z in (hi, lo, w_hi, w_lo))
        t.matmul(out_, hi, w_hi, start=start, stop=False)
        t.matmul(out_, hi, w_lo, start=False, stop=False)
        return t.matmul(out_, lo, w_hi, start=False, stop=stop)

    def high(hi, src):
        return v.tensor_copy(one_pass(hi), src)

    def low(lo, src, hi):
        return v.tensor_tensor(one_pass(lo), src, one_pass(hi), ALU.subtract)

    w_late = [Slot(nc, f"s_v{u}", w_slots[u].ap) for u in range(2)]
    spare = [arena[:, 0:2048], arena[:, 3328:5376], arena[:, 5376:7424], scratch[:]]

    def begin_product(w, c0, c1):
        tiles = [(c, min(512, c1 - c)) for c in range(c0, c1, 512)]
        wv = w.rearrange("(p k) n -> p k n", k=KD)
        read = [None] * 2

        def next_tile(j):
            c, n = tiles[j]
            slot, u = w_slot(), j % 2
            late = w_late[w_slots.index(slot)]
            tile = slot.ap[:, 0:KD * n].rearrange("p (k n) -> p k n", k=KD)
            if slot.reader:
                sp.wait(slot.reader)
            for half, s in enumerate((slot, late)):
                ks = slice(4 * half, 4 * half + 4)
                nc.sync.dma_start(tile[:, ks, :], wv[:, ks, c:c + n]).then_inc(s.sem, 16)
                s.n += 16
            his, split = [], []
            free = read[u] or [pe.now(), ve.now(), ac.now()]
            for half, s in enumerate((slot, late)):
                lo = tile[:, 4 * half:4 * half + 4, :]
                his.append(spare[2 * u + half][:, 0:4 * n].rearrange("p (k n) -> p k n", k=4))
                ac.op(a.activation, one_pass(his[half]), lo, ACT.Copy, after=[(s.sem, s.n), *free])
                if j == 0:
                    split.append(po.op(nc.gpsimd.tensor_tensor, one_pass(lo), lo, one_pass(his[half]), ALU.subtract,
                                       after=[ac.now()]))
                else:
                    split.append(ve.op(low, lo, lo, his[half], after=[ac.now()]))
            return slot, tile, his, split

        return tiles, next_tile, read, next_tile(0)

    def product(begun, sink, banks):
        tiles, next_tile, read, ready = begun
        x_split = ve.now()
        nb = 0
        for j, (c, n) in enumerate(tiles):
            slot, tile, his, split = ready
            if j + 1 < len(tiles):
                ready = next_tile(j + 1)
            for tt in range(NT):
                b = banks[nb % len(banks)]
                nb += 1
                bk = bank_for_pe(b)
                q = slice(tt * P, (tt + 1) * P)
                for k in range(KD):
                    if k % 4 == 0:
                        pe.wait(split[k // 4], x_split)
                    mm = products3(bk[:, 0:n], px_hi[:, k, q], XT[:, k, q], his[k // 4][:, k % 4, :], tile[:, k, :],
                                   k == 0, k == KD - 1)
                mm.then_inc(pe.sem, 1)
                pe.n += 1
                if tt == NT - 1:
                    slot.reader = pe.now()
                    read[j % 2] = [pe.now()]
                sink(tt, c, n, b)

    def keep_in(buf):
        def sink(tt, c, n, b):
            if tt == 0:
                ac.op(a.activation, buf[:, tt, c:c + n], psum[:, b, 0:n], ACT.Copy, after=[pe.now()])
                read_by(b, ac.now())
            else:
                ve.op(v.tensor_copy, buf[:, tt, c:c + n], psum[:, b, 0:n], after=[pe.now()])
                read_by(b, ve.now())
        return sink

    def add_normed(s, n):
        g, there = take_gate()
        ve.op(v.tensor_tensor, g, g, prow[:, n, :], ALU.mult, after=[(s_row, rows[0]), there])
        for tt in range(NT):
            acc = acc_tile(tt)
            ss = st[:, tt:tt + 1]
            ac.op(a.activation, xn, acc, ACT.Square, accum_out=ss, after=[ve.now(), pe.now()])
            rstd(ss, D, 1)
            ve.op(v.scalar_tensor_tensor, tmp, acc, ss, g, ALU.mult, ALU.mult, after=[pe.now()])
            for b in (2 * tt, 2 * tt + 1):
                read_by(b, ve.now(), ac.now())
            ve.op(v.tensor_tensor, x[:, s, tt, :], x[:, s, tt, :], tmp, ALU.add)
        gate_read()

    def add_gated(source):
        g, there = take_gate()
        for tt in range(NT):
            ve.op(v.tensor_tensor, tmp, source(tt), g, ALU.mult, after=[pe.now(), there])
            for b in (2 * tt, 2 * tt + 1):
                read_by(b, ve.now())
            ve.op(v.tensor_tensor, x[:, LAT, tt, :], x[:, LAT, tt, :], tmp, ALU.add)
        gate_read()

    def project_out(begun):
        cat_T()
        product(begun, lambda tt, c, n, b: None, [0, 2, 1, 3])

    def acc_tile(tt):
        return psum[:, 2 * tt:2 * tt + 2, :].rearrange("p b n -> p (b n)")

    names = ["gu", "silu", "h", "tr", "eh", "ev", "dn", "wh", "wl", "dh", "dl"]
    fs = {n: nc.alloc_semaphore("s_f" + n) for n in names}
    fn = dict.fromkeys(names, 0)
    sg = work[:, 0:512].rearrange("p (t n) -> p t n", t=NT)
    hb = work[:, 512:1024].rearrange("p (t n) -> p t n", t=NT)
    hT = work[:, 1024:2048].rearrange("p (a k q) -> p a k q", a=2, k=2)
    moe_y = cat[:]

    def hold(engine, sem, value):
        if not isinstance(value, int) or value > 0:
            engine.wait_ge(sem, value)

    def open_slots():
        settle()
        ws, ds = [w_slots[(ring["w"] + u) % 2] for u in range(2)], [d_slots[(ring["d"] + u) % 2] for u in range(2)]
        for s in ws + ds:
            if s.reader:
                sp.wait(s.reader)
        return ws, ds

    def close_slots(ws, ds, total):
        ring["w"] += total
        ring["d"] += total
        for u in range(2):
            steps_u = (total + 1 - u) // 2
            ws[u].n += 32 * steps_u
            ds[u].n += 16 * steps_u
            ws[u].reader = (fs["gu"], fn["gu"])
            ds[u].reader = (fs["dn"], fn["dn"])

    def ffn(steps, gate_up, down):
        meet()
        base = dict(fn)
        ws, ds = open_slots()
        wl_ = [w_late[w_slots.index(s)] for s in ws]
        wn, dn_, wn2 = [s.n for s in ws], [s.n for s in ds], [s.n for s in wl_]
        w_hi = [arena[:, 0:4096], arena[:, 4096:8192]]
        d_hi = [arena[:, 8192:10240], cat[:].rearrange("p t n -> p (t n)")]
        x_hi = scratch[:].rearrange("p (k q) -> p k q", k=KD)
        hl = work[:, 2048:3072].rearrange("p (a k q) -> p a k q", a=2, k=2)

        def value(name, per, i_, plus):
            return i_ * per + (base[name] + plus)

        def landed(n0, per, u, i_):
            return (i_ - u) * (per // 2) + (n0[u] + per)

        def load(i_, u):
            hold(nc.sync, fs["gu"], value("gu", 2, i_, -2))
            tile = ws[u].ap[:].rearrange("p (k c n) -> p k c n", k=KD, c=2)
            for half, sem in ((0, ws[u].sem), (1, wl_[u].sem)):
                for c in range(2):
                    nc.sync.dma_start(tile[:, 4 * half:4 * half + 4, c, :],
                                      gate_up(c, i_)[:, 4 * half:4 * half + 4]).then_inc(sem, 16)
            hold(nc.sync, fs["dn"], value("dn", 1, i_, -1))
            nc.sync.dma_start(ds[u].ap[:].rearrange("p (k n) -> p k n", k=2), down(i_)).then_inc(ds[u].sem, 16)

        def split_w(i_, u, half):
            hold(v, (ws[u], wl_[u])[half].sem, landed((wn, wn2)[half], 32, u, i_))
            hold(v, fs["gu"], value("gu", 2, i_, -2))
            lo, hi = ws[u].ap[:, half * 2048:(half + 1) * 2048], w_hi[u][:, half * 2048:(half + 1) * 2048]
            high(hi, lo).then_inc(fs["wh"], 1)
            hold(v, fs["wh"], value("wh", 2, i_, half + 1))
            low(lo, lo, hi).then_inc(fs["wl"], 1)

        def split_d(i_, u):
            hold(v, ds[u].sem, landed(dn_, 16, u, i_))
            hold(v, fs["dn"], value("dn", 1, i_, -1))
            high(d_hi[u], ds[u].ap[:]).then_inc(fs["dh"], 1)
            hold(v, fs["dh"], value("dh", 1, i_, 1))
            low(ds[u].ap[:], ds[u].ap[:], d_hi[u]).then_inc(fs["dl"], 1)

        def up(i_, u, tt):
            hold(t, fs["h"], value("h", 2, i_, tt - 1))
            for k in range(KD):
                if k % 4 == 0:
                    hold(t, fs["wl"], value("wl", 2, i_, k // 4 + 1))
                cols = slice(k * 512, (k + 1) * 512)
                mm = products3(psum[:, 4 + tt, :], x_hi[:, k, tt * P:(tt + 1) * P], XT[:, k, tt * P:(tt + 1) * P],
                               w_hi[u][:, cols], ws[u].ap[:, cols], k == 0, k == KD - 1)
            mm.then_inc(fs["gu"], 1)
            hold(a, fs["gu"], value("gu", 2, i_, tt + 1))
            hold(a, fs["h"], value("h", 2, i_, tt - 1))
            a.activation(sg[:, tt, :], psum[:, 4 + tt, 0:FCOL], ACT.Silu).then_inc(fs["silu"], 1)

        def hidden(i_, tt):
            hold(v, fs["silu"], value("silu", 2, i_, tt + 1))
            hold(v, fs["tr"], value("tr", 2, i_, tt - 1))
            v.tensor_tensor(hb[:, tt, :], sg[:, tt, :], psum[:, 4 + tt, FCOL:512], ALU.mult).then_inc(fs["h"], 1)

        def turn(i_, u, tt):
            hold(t, fs["h"], value("h", 2, i_, tt + 1))
            hold(t, fs["ev"], value("ev", 2, i_, tt - 1))
            for k in range(2):
                mm = t.transpose(psum[:, 6 + tt, k * P:(k + 1) * P], hb[:, tt, k:FCOL:2], ident[:])
            mm.then_inc(fs["tr"], 1)
            hold(v, fs["tr"], value("tr", 2, i_, tt + 1))
            hold(v, fs["dn"], value("dn", 1, i_, -1))
            src = psum[:, 6 + tt, 0:256].rearrange("p (k q) -> p k q", k=2)
            hi, lo = (z[:, u, :, tt * P:(tt + 1) * P] for z in (hT, hl))
            high(hi, src).then_inc(fs["eh"], 1)
            hold(v, fs["eh"], value("eh", 2, i_, tt + 1))
            low(lo, src, hi).then_inc(fs["ev"], 1)

        def downs(i_, u, start, stop):
            hold(t, fs["dl"], value("dl", 1, i_, 1))
            hold(t, fs["ev"], value("ev", 2, i_, 2))
            for tt in range(NT):
                for k in range(2):
                    for h in range(2):
                        cols, q = slice(k * D + h * 512, k * D + (h + 1) * 512), slice(tt * P, (tt + 1) * P)
                        mm = products3(psum[:, 2 * tt + h, :], hT[:, u, k, q], hl[:, u, k, q], d_hi[u][:, cols],
                                       ds[u].ap[:, cols], start and k == 0, stop and k == 1)
            mm.then_inc(fs["dn"], 1)

        def step(i_, u, ahead_=True):
            up(i_, u, 0)
            if not isinstance(i_, int) or i_ > 0:
                turn(i_ - 1, 1 - u, 1)
            if ahead_:
                load(i_ + 1, 1 - u)
                split_w(i_ + 1, 1 - u, 0)
            hidden(i_, 0)
            split_d(i_, u)
            up(i_, u, 1)
            if ahead_:
                split_w(i_ + 1, 1 - u, 1)
            hidden(i_, 1)
            turn(i_, u, 0)

        ve.op(high, x_hi, XT[:])
        ve.op(low, XT[:], XT[:], x_hi)
        pe.wait(ve.now())
        load(0, 0)
        split_w(0, 0, 0)
        split_w(0, 0, 1)
        step(0, 0)
        step(1, 1)
        downs(0, 0, True, False)
        pairs = (steps - 3) // 2
        with nc.Fori(0, pairs) as r:
            for u in range(2):
                step(r * 2 + (2 + u), u)
                downs(r * 2 + (1 + u), 1 - u, False, False)
        for last in range(2 + 2 * pairs, steps):
            step(last, last % 2, last < steps - 1)
            downs(last - 1, (last - 1) % 2, False, False)
        turn(steps - 1, (steps - 1) % 2, 1)
        downs(steps - 1, (steps - 1) % 2, False, True)
        for n in ("gu", "silu", "h", "tr", "eh", "ev", "wh", "wl"):
            fn[n] += 2 * steps
        for n in ("dn", "dh", "dl"):
            fn[n] += steps
        close_slots(ws, ds, steps)
        for u in range(2):
            wl_[u].n += 32 * ((steps + 1 - u) // 2)
        for e_ in (pe, ve, ac):
            e_.wait((fs["dn"], fn["dn"]), (fs["ev"], fn["ev"]))

    def dense(wg, wu, wd):
        gv = [w.rearrange("(p k) n -> p k n", k=KD) for w in (wg, wu)]
        dv = wd.rearrange("(i p k) n -> p i k n", p=P, k=2)
        ffn(FDENSE // FCOL, lambda c, i_: gv[c][:, :, bass.ds(i_ * FCOL, FCOL)],
            lambda i_: dv[:, bass.ds(i_, 1)].rearrange("p i k n -> p (i k) n"))

    def heads_T(src, tt, heads, dst, offset):
        for h0 in range(0, heads, 4):
            n = min(4, heads - h0)
            b = 4 + (h0 // 4) % 2
            bk = bank_for_pe(b)
            pe.wait(ve.now(), ac.now())
            for h in range(n):
                pe.free(t.transpose, bk[0:HD, h * P:(h + 1) * P], src[:, (h0 + h) * HD:(h0 + h + 1) * HD], ident[:])
            ac.op(a.activation, dst[0:HD, h0:h0 + n, offset + tt * P:offset + (tt + 1) * P],
                  bk[0:HD, 0:n * P].rearrange("p (h q) -> p h q", h=n), ACT.Copy, after=[pe.now()])
            read_by(b, ac.now())

    def rope(src, heads, cos, sin):
        d = src.rearrange("p (h f) -> p h f", f=HD)
        o = tmp[:, 0:heads * HD].rearrange("p (h f) -> p h f", f=HD)
        ve.op(v.tensor_tensor, o[:, :, 0:32], d[:, :, 32:64], bc(sin[:, 0:32], 1, heads), ALU.mult, after=[ac.now(), pe.now()])
        ve.op(v.tensor_tensor, o[:, :, 32:64], d[:, :, 0:32], bc(sin[:, 32:64], 1, heads), ALU.mult)
        ve.op(v.tensor_tensor, d, d, bc(cos, 1, heads), ALU.mult)
        ve.op(v.tensor_tensor, d, d, o, ALU.add)

    Pm = work[:, 0:1536].rearrange("p (a n) -> p a n", a=3)
    PT = work[:, 1536:2560].rearrange("p (a n) -> p a n", a=2)
    msum = st[:, 16:40]

    def attention(heads, per_kv, qT, kT, keys, vals, bias, finish):
        units = [(tt, h) for tt in range(NT) for h in range(heads)]
        exp_of, pv_of, turned, copied, outs = {}, {}, {}, {}, {}
        pe.wait(ac.now(), ve.now())
        ac.wait(ve.now())
        ve.wait(pe.now(), ac.now())

        def scores(u):
            tt, h = units[u]
            nk, buf = keys(tt), u % 3
            sbank = (0, 1, 6)[buf]
            bk = bank_for_pe(sbank)
            qk = pe.free(t.matmul, bk[:, 0:nk], qT[0:HD, h, tt * P:(tt + 1) * P], kT[0:HD, h // per_kv, 0:nk],
                         start=True, stop=True)
            mx = msum[:, buf:buf + 1]
            sm = msum[:, 3 + 8 * ((u // 8) % 2) + u % 8:][:, 0:1]
            p_ = Pm[:, buf, 0:nk]
            free = [turned[u - 3]] if u >= 3 else []
            if bias is None:
                ve.op(v.tensor_reduce, mx, bk[:, 0:nk], AX, ALU.max, after=[qk] + ([exp_of[u - 3]] if u >= 3 else []))
                m_ = ve.op(v.tensor_scalar, mx, mx, -0.125, None, ALU.mult)
                exp_of[u] = ac.op(a.activation, p_, bk[:, 0:nk], ACT.Exp, bias=mx, scale=0.125, accum_out=sm,
                                  after=[m_] + free + ([outs[u // 8 - 2]] if u // 8 >= 2 else []))
                read_by(sbank, exp_of[u])
            else:
                m_ = ve.op(v.scalar_tensor_tensor, p_, bk[:, 0:nk], 0.125, bias(tt)[:, 0:nk], ALU.mult, ALU.add,
                           after=[qk] + free + ([exp_of[u - 3]] if u >= 3 else []))
                read_by(sbank, m_)
                m_ = ve.op(v.tensor_reduce, mx, p_, AX, ALU.max, negate=True)
                exp_of[u] = ac.op(a.activation, p_, p_, ACT.Exp, bias=mx, scale=1.0, accum_out=sm,
                                  after=[m_] + ([outs[u // 8 - 2]] if u // 8 >= 2 else []))

        def turn(u):
            nk, par_ = keys(units[u][0]), u % 2
            bk = bank_for_pe(2 + par_)
            pe.wait(exp_of[u])
            for b in range(nk // P):
                turned[u] = pe.free(t.transpose, bk[:, b * P:(b + 1) * P], Pm[:, u % 3, b * P:(b + 1) * P], ident[:])
            copied[u] = ve.op(v.tensor_copy, PT[:, par_, 0:nk], bk[:, 0:nk],
                              after=[turned[u]] + ([pv_of[u - 2]] if u >= 2 else []))
            read_by(2 + par_, copied[u])

        def values(u):
            tt, h = units[u]
            nk, par_ = keys(tt), u % 2
            ob = 4 + (u // 8) % 2
            o = bank_for_pe(ob)
            pe.wait(copied[u])
            for b in range(nk // P):
                mm = t.matmul(o[:, (h % 8) * HD:(h % 8 + 1) * HD], PT[:, par_, b * P:(b + 1) * P],
                              vals(h // per_kv, b), start=(b == 0), stop=(b == nk // P - 1))
            mm.then_inc(pe.sem, 1)
            pe.n += 1
            pv_of[u] = pe.now()
            if h % 8 == 7:
                sums = msum[:, 3 + 8 * ((u // 8) % 2):][:, 0:8]
                ve.op(v.reciprocal, sums, sums, after=[pv_of[u], exp_of[u]])
                finish(tt, h - 7, o.rearrange("p (h f) -> p h f", f=HD), sums)
                outs[u // 8] = ve.now()
                read_by(ob, ve.now())

        for u in range(len(units) + 3):
            if u < len(units):
                scores(u)
            if 0 <= u - 2 < len(units):
                turn(u - 2)
            if u >= 3:
                values(u - 3)

    def into_cat(tt, h0, o, inv):
        ve.op(v.tensor_tensor, cat[:, tt, h0 * HD:(h0 + 8) * HD].rearrange("p (h f) -> p h f", f=HD),
              o, bc(inv, 2, HD), ALU.mult)

    proj = wide[:, 0:NT * IN1].rearrange("p (t n) -> p t n", t=NT)
    off = [0]

    def cut(n):
        off[0] += n
        return arena[:, off[0] - n:off[0]]

    qT = cut(2048).rearrange("p (h q) -> p h q", h=8)
    kT = cut(1024).rearrange("p (g q) -> p g q", g=2)
    vctx = cut(256).rearrange("p (t n) -> p t n", t=NT)
    xbcT = cut(2080).rearrange("p (b q) -> p b q", b=8)
    convT = cut(2048).rearrange("p (b q) -> p b q", b=8)
    xtok = cut(1024).rearrange("p (t n) -> p t n", t=NT)
    btok = cut(512).rearrange("p (t n) -> p t n", t=NT)
    smat = cut(512).rearrange("p (t g q) -> p t g q", t=NT, g=2)
    state = cut(1024).rearrange("p (d n) -> p d n", d=2)
    xdt = cut(512)
    xde = cut(512)
    dts = cut(256).rearrange("p (n t d h) -> p n t d h", n=8, t=NT, d=2)
    ex = cut(64)
    dec = work[:, 0:1024].rearrange("p (h q) -> p h q", h=8)
    dtB = work[:, 1024:2048].rearrange("p (h q) -> p h q", h=8)

    def ssd(l, s, with_y):
        meet()
        ve.op(v.memset, xbcT[:, :, 0:2], 0.0)
        ve.op(v.memset, xbcT[:, :, 258:260], 0.0)
        for b2 in range(0, 8, 2):
            b = (b2 // 2) % 2
            bk = bank_for_pe(b)
            for n in range(4):
                blk, tt = b2 + n // 2, n % 2
                pe.free(t.transpose, bk[:, n * P:(n + 1) * P], proj[:, tt, XBC0 + blk * P:XBC0 + (blk + 1) * P], ident[:])
            ac.op(a.activation, xbcT[:, b2:b2 + 2, 2:258], bk.rearrange("p (b q) -> p b q", b=2), ACT.Copy, after=[pe.now()])
            read_by(b, ac.now())
        for b in range(8):
            fill(3)
            acc_ = convT[:, b, :]
            ve.op(v.tensor_scalar, acc_, xbcT[:, b, 0:T], convp[:, l, b, 0:1], None, ALU.mult, after=[ac.now()])
            for j in range(1, 5):
                ve.op(v.scalar_tensor_tensor, acc_, xbcT[:, b, j:j + T], convp[:, l, b, j:j + 1], acc_, ALU.mult, ALU.add)
            ac.op(a.activation, acc_, acc_, ACT.Silu, bias=convp[:, l, b, 5:6], after=[ve.now()])
        if with_y:
            for tt in range(NT):
                ac.op(a.activation, xn[:, tt * 512:(tt + 1) * 512], proj[:, tt, Z0:Z0 + 512], ACT.Silu, after=[ve.now(), pe.now()])
        for tt in range(NT):
            bk = bank_for_pe(6)
            pe.wait(ac.now())
            for b in range(4):
                pe.free(t.transpose, bk[:, b * P:(b + 1) * P], convT[:, b, tt * P:(tt + 1) * P], ident[:])
            ve.op(v.tensor_copy, xtok[:, tt, :], bk, after=[pe.now()])
            read_by(6, ve.now())
            bk = bank_for_pe(4)
            for b in range(2):
                pe.free(t.transpose, bk[:, b * P:(b + 1) * P], convT[:, 4 + b, tt * P:(tt + 1) * P], ident[:])
            ve.op(v.tensor_copy, btok[:, tt, :], bk[:, 0:256], after=[pe.now()])
            read_by(4, ve.now())
            if with_y:
                ve.op(v.tensor_tensor, cat[:, tt, 512:1024].rearrange("p (h f) -> p h f", f=HD),
                      xtok[:, tt, :].rearrange("p (h f) -> p h f", f=HD), bc(dtp[:, l, 2, 0, :], 2, HD), ALU.mult)
        xx, e_, u_, ln, m_, dt, dtA, sp_ = (dts[:, n] for n in range(8))
        for d in range(2):
            ve.op(v.tensor_tensor, xx[:, :, d, :], proj[:, :, DT0:DT0 + 8], bc(dtp[:, l, 0, d, :], 1, NT), ALU.add)
        ve.op(v.tensor_scalar, e_, xx, -1.0, None, ALU.mult)
        ve.op(v.tensor_tensor, e_, e_, xx, ALU.min)
        ac.op(a.activation, e_, e_, ACT.Exp, after=[ve.now()])
        ve.op(v.tensor_scalar, u_, e_, 1.0, None, ALU.add, after=[ac.now()])
        ac.op(a.activation, ln, u_, ACT.Ln, after=[ve.now()])
        ve.op(v.tensor_scalar, u_, u_, 1.0, None, ALU.subtract, after=[ac.now()])
        ve.op(v.tensor_scalar, m_, u_, 0.0, None, ALU.is_equal)
        ve.op(v.tensor_tensor, ln, ln, m_, ALU.add)
        ve.op(v.tensor_tensor, ln, ln, e_, ALU.mult)
        ve.op(v.tensor_tensor, u_, u_, m_, ALU.add)
        ve.op(v.reciprocal, u_, u_)
        ve.op(v.tensor_tensor, ln, ln, u_, ALU.mult)
        ve.op(v.tensor_scalar, xx, xx, 0.0, None, ALU.max)
        ve.op(v.tensor_tensor, dt, xx, ln, ALU.add)
        for d in range(2):
            ve.op(v.tensor_tensor, dtA[:, :, d, :], dt[:, :, d, :], bc(dtp[:, l, 1, d, :], 1, NT), ALU.mult)
        if with_y:
            bk = bank_for_pe(6)
            pe.wait(ac.now())
            for n in range(4):
                tt, g = n // 2, n % 2
                pe.free(t.matmul, bk[:, n * P:(n + 1) * P], convT[:, 4 + g, tt * P:(tt + 1) * P],
                        convT[:, 6 + g, tt * P:(tt + 1) * P], start=True, stop=True)
            ve.op(v.tensor_copy, smat, bk.rearrange("p (t g q) -> p t g q", t=2, g=2), after=[pe.now()])
            read_by(6, ve.now())
        for d in range(2):
            for n, tt in enumerate((0, 1) if d == 0 else (1, 0)):
                fresh = s == CTX and n == 0
                last = s == LAT and n == 1
                dA, dtc = dtA[:, tt, d, :], dt[:, tt, d, :]
                fill(2)
                bk = bank_for_pe(0)
                pe.wait(ve.now())
                pe.free(t.matmul, bk[:, 0:8], tri[:, d, :], dA, start=True, stop=True)
                pe.free(t.matmul, bk[:, 8:16], ones[:], dA, start=True, stop=True)
                acum, tot, dte, ea, cd = (ex[:, 8 * j:8 * j + 8] for j in range(5))
                ve.op(v.tensor_copy, ex[:, 0:16], bk[:, 0:16], after=[pe.now(), ac.now()])
                read_by(0, ve.now())
                ve.op(v.tensor_tensor, dte, tot, acum, ALU.subtract)
                ac.op(a.activation, dte, dte, ACT.Exp, after=[ve.now()])
                ac.op(a.activation, ea, acum, ACT.Exp)
                ac.op(a.activation, cd, tot, ACT.Exp)
                xh = xtok[:, tt, :].rearrange("p (h f) -> p h f", f=HD)
                ve.op(v.tensor_tensor, xdt.rearrange("p (h f) -> p h f", f=HD), xh, bc(dtc, 2, HD), ALU.mult)
                ve.op(v.tensor_tensor, xde.rearrange("p (h f) -> p h f", f=HD), xdt.rearrange("p (h f) -> p h f", f=HD),
                      bc(dte, 2, HD), ALU.mult, after=[ac.now()])
                if with_y:
                    ve.op(v.tensor_copy, dtB, bc(dA, 2, P))
                    pe.wait(*bank_free[2], *bank_free[3], ve.now())
                    for h in range(8):
                        pe.free(t.matmul, psum[:, 2 + h // 4, (h % 4) * P:(h % 4 + 1) * P], dtB[:, h, :], tri[:, d, :],
                                start=True, stop=True)
                    pair = psum[:, 2:4, :].rearrange("p b (h q) -> p (b h) q", q=P)
                    ve.op(v.tensor_tensor, dec, pair, bc(acum, 2, P), ALU.subtract, after=[pe.now()])
                    read_by(2, ve.now())
                    read_by(3, ve.now())
                    fill(6)
                    ve.op(v.tensor_tensor, dec, dec, bc(trineg[:, d, :], 1, 8), ALU.add)
                    ac.op(a.activation, dec, dec, ACT.Exp, after=[ve.now()])
                    for g in range(2):
                        ve.op(v.tensor_tensor, dec[:, 4 * g:4 * g + 4, :], dec[:, 4 * g:4 * g + 4, :],
                              bc(smat[:, tt, g, :], 1, 4), ALU.mult, after=[ac.now()])
                    o = bank_for_pe(4)
                    pe.wait(ve.now())
                    for h in range(8):
                        pe.free(t.matmul, o[:, h * HD:(h + 1) * HD], dec[:, h, :], xdt[:, h * HD:(h + 1) * HD],
                                start=True, stop=True)
                    y = cat[:, tt, 512:1024]
                    ve.op(v.tensor_tensor, y, y, o, ALU.add, after=[pe.now()])
                    read_by(4, ve.now())
                    if not fresh:
                        o = bank_for_pe(5)
                        for g in range(2):
                            pe.free(t.matmul, o[:, g * 256:(g + 1) * 256], convT[:, 6 + g, tt * P:(tt + 1) * P],
                                    state[:, d, g * 256:(g + 1) * 256], start=True, stop=True)
                        th = tmp[:, 0:512]
                        ve.op(v.tensor_tensor, th.rearrange("p (h f) -> p h f", f=HD),
                              o.rearrange("p (h f) -> p h f", f=HD), bc(ea, 2, HD), ALU.mult, after=[pe.now(), ac.now()])
                        read_by(5, ve.now())
                        ve.op(v.tensor_tensor, y, y, th, ALU.add)
                if not last:
                    bk = bank_for_pe(1)
                    pe.wait(ve.now())
                    for g in range(2):
                        pe.free(t.matmul, bk[:, g * 256:(g + 1) * 256], btok[:, tt, g * P:(g + 1) * P],
                                xde[:, g * 256:(g + 1) * 256], start=True, stop=True)
                    sh_ = state[:, d, :].rearrange("p (h f) -> p h f", f=HD)
                    if fresh:
                        ve.op(v.tensor_copy, state[:, d, :], bk, after=[pe.now()])
                    else:
                        ve.op(v.tensor_tensor, sh_, sh_, bc(cd, 2, HD), ALU.mult, after=[pe.now(), ac.now()])
                        ve.op(v.tensor_tensor, state[:, d, :], state[:, d, :], bk, ALU.add)
                    read_by(1, ve.now())
        if with_y:
            begun = begin_product(i["w_out"][l], 0, D)
            for tt in range(NT):
                y = cat[:, tt, 512:1024]
                ve.op(v.tensor_tensor, y, y, xn[:, tt * 512:(tt + 1) * 512], ALU.mult, after=[ac.now()])
                ac.op(a.activation, tmp[:, tt * 512:(tt + 1) * 512], y, ACT.Square, accum_out=st[:, tt:tt + 1], after=[ve.now()])
            rstd(st[:, 0:NT], 512, NT)
            for tt in range(NT):
                y = cat[:, tt, 512:1024]
                ve.op(v.scalar_tensor_tensor, y, y, st[:, tt:tt + 1], ssdn[:], ALU.mult, ALU.mult, after=[(s_row, rows[0])])
            return begun

    def mixer_in(l, s):
        begun = begin_product(i["w_in"][l], 0, IN1)
        normed_T(s, 0, split=True)
        product(begun, keep_in(proj), [0, 1, 2, 3])
        for tt in range(NT):
            qk = proj[:, tt, 0:640]
            q3 = qk.rearrange("p (h f) -> p h f", f=HD)
            sq = tmp[:, 0:640]
            ve.op(v.tensor_tensor, sq, qk, qk, ALU.mult, after=[ac.now()])
            ss = st[:, 0:10]
            ve.op(v.tensor_reduce, ss, sq.rearrange("p (h f) -> p h f", f=HD), AX, ALU.add)
            rstd(ss, HD, 10)
            ve.op(v.tensor_tensor, q3, q3, bc(ss, 2, HD), ALU.mult)
            ve.op(v.tensor_tensor, q3[:, 0:8], q3[:, 0:8], bc(qkn[:, l, 0, :], 1, 8), ALU.mult)
            ve.op(v.tensor_tensor, q3[:, 8:10], q3[:, 8:10], bc(qkn[:, l, 1, :], 1, 2), ALU.mult)
            fill(5)
            if s == LAT:
                rope(qk, 10, axial[:, tt, 0, :], axial[:, tt, 1, :])
            heads_T(proj[:, tt, 0:512], tt, 8, qT, 0)
            heads_T(proj[:, tt, 512:640], tt, 2, kT, 0 if s == CTX else T)
            if s == CTX:
                ve.op(v.tensor_copy, vctx[:, tt, :], proj[:, tt, V0:V0 + 128], after=[ac.now(), pe.now()])

    def mixer(l, s, with_out):
        mixer_in(l, s)
        if with_out:
            nkeys = T if s == CTX else 2 * T

            def vals(g, b):
                if b < NT:
                    return vctx[:, b, g * HD:(g + 1) * HD]
                return proj[:, b - NT, V0 + g * HD:V0 + (g + 1) * HD]
            attention(8, 4, qT, kT, lambda tt: nkeys, vals, None, into_cat)
        begun = ssd(l, s, with_out)
        if with_out:
            project_out(begun)
            add_normed(s, 0)

    meet()
    for l in range(2):
        job = f"mod{l}"
        load_columns(job, 2, (0, 0, l), (1, 3, 2 + l))
        ask_gates(job, *((CTX, 2), (LAT, 2), (CTX, 5), (LAT, 5)) if l == 0 else ((LAT, 2), (LAT, 5)))
        load_rows((ssdn[:], i["ssd_norm"][l].partition_broadcast(P)),
                  (prow[:, 0, :], i["norm_mix_post"][l].partition_broadcast(P)),
                  (prow[:, 1, :], i["norm_ffn_post"][l].partition_broadcast(P)))
        for s in (CTX, LAT):
            mixer(l, s, s == LAT or l == 0)
        for s in ((CTX, LAT) if l == 0 else (LAT,)):
            normed_T(s, 1)
            dense(i["w_gate"][l], i["w_up"][l], i["w_down"][l])
            add_normed(s, 1)

    load_columns("ada0", 1, (0, 0, 4), (1, 3, 6))
    ask_gates("ada0", (0, 2), (0, 5))
    off[0] = 0
    spare[1:3] = [arena[:, 2048:4096], arena[:, 6144:8192]]
    proj2 = wide[:, 0:NT * IN2].rearrange("p (t n) -> p t n", t=NT)
    qT2 = cut(4096).rearrange("p (h q) -> p h q", h=16)
    keep = off[0]
    kT2 = cut(1024).rearrange("p (g q) -> p g q", g=4)
    iqT = cut(2304).rearrange("p (h q) -> p h q", h=9)
    score = cut(512).rearrange("p (t k) -> p t k", t=NT)
    left = cut(256)
    rel = cut(512).rearrange("p (a k) -> p a k", a=2)
    m8 = cut(8)
    keys2 = lambda tt: (tt + 1) * P

    begun = begin_product(i["a_w_in_2"][0], 0, IN2)
    normed_T(LAT, 0, split=True)
    product(begun, keep_in(proj2), [0, 1, 2, 3])
    for tt in range(NT):
        cos, sin = rope2[:, tt, 0, :], rope2[:, tt, 1, :]
        fill(8)
        rope(proj2[:, tt, 0:1024], 16, cos, sin)
        rope(proj2[:, tt, DK0:DV0], 4, cos, sin)
        rope(proj2[:, tt, IQ0:IW0], 9, cos, sin)
        heads_T(proj2[:, tt, 0:1024], tt, 16, qT2, 0)
        heads_T(proj2[:, tt, DK0:DV0], tt, 4, kT2, 0)
        heads_T(proj2[:, tt, IQ0:IW0], tt, 9, iqT, 0)
        ve.op(v.tensor_scalar, proj2[:, tt, IW0:IN2], proj2[:, tt, IW0:IN2], IDX_SCALE, None, ALU.mult)
    for tt in range(NT):
        nk = keys2(tt)
        sc = score[:, tt, 0:nk]
        for h in range(8):
            u = h % 2
            bk = bank_for_pe(u)
            pe.wait(ac.now())
            pe.free(t.matmul, bk[:, 0:nk], iqT[0:HD, h, tt * P:(tt + 1) * P], iqT[0:HD, 8, 0:nk], start=True, stop=True)
            ac.op(a.activation, rel[:, u, 0:nk], bk[:, 0:nk], ACT.Relu, after=[pe.now(), ve.now()])
            read_by(u, ac.now())
            wi = proj2[:, tt, IW0 + h:IW0 + h + 1]
            if h == 0:
                ve.op(v.tensor_scalar, sc, rel[:, u, 0:nk], wi, None, ALU.mult, after=[ac.now()])
            else:
                ve.op(v.scalar_tensor_tensor, sc, rel[:, u, 0:nk], wi, sc, ALU.mult, ALU.add, after=[ac.now()])
        ve.op(v.tensor_tensor, sc, sc, causal[:, tt, 0:nk], ALU.add)
        ve.op(v.tensor_copy, left[:, 0:nk], sc)
        fill(20)
        for _ in range(TOPK // 8):
            ve.op(v.max, m8, left[:, 0:nk])
            ve.op(v.match_replace, left[:, 0:nk], m8, left[:, 0:nk], TAKEN)
        ve.op(v.tensor_scalar, sc, left[:, 0:nk], TAKEN / 2, NEG, ALU.is_gt, ALU.mult)
        ve.op(v.tensor_tensor, sc, sc, causal[:, tt, 0:nk], ALU.add)
    meet()
    spare[0:3] = [arena[:, 9856:11904], arena[:, 5120:7168], arena[:, 2048:4096]]
    begun = begin_product(i["a_w_out_2"][0], 0, D)
    attention(16, 4, qT2, kT2, keys2, lambda g, b: proj2[:, b, DV0 + g * HD:DV0 + (g + 1) * HD],
              lambda tt: score[:, tt, :], into_cat)
    project_out(begun)
    add_gated(acc_tile)
    normed_T(LAT, 1)
    dense(i["ffn_w_gate_2"][0], i["ffn_w_up_2"][0], i["ffn_w_down_2"][0])
    add_gated(acc_tile)

    load_columns("kv", 1, (2, 0, 8))
    load_columns("ada1", 1, (0, 0, 5), (1, 3, 7))
    ask_gates("ada1", (0, 2), (0, 5))
    meet()
    off[0] = keep
    spare[0:2] = [arena[:, 0:2048], arena[:, 2048:4096]]
    spare[2] = arena[:, 6144:8192]
    kv = wide[:, 0:NT * 1536].rearrange("p (t n) -> p t n", t=NT)
    projq = wide[:, 3072:3072 + NT * IN3].rearrange("p (t n) -> p t n", t=NT)
    ksT = cut(1024).rearrange("p (g q) -> p g q", g=4)
    kwT = cut(1024).rearrange("p (g q) -> p g q", g=4)
    dup = cut(512).rearrange("p (h a f) -> p h a f", h=4, a=2)
    win = cut(1024).rearrange("p (h q) -> p h q", h=4)
    xw = cut(16 * 60).rearrange("p (c h n) -> p c h n", c=16, h=4)
    hid = cut(256)
    hidT = cut(120).rearrange("p (c r) -> p c r", c=2)
    kcT = cut(60)
    vc = cut(256).rearrange("p (g f) -> p g f", g=4)
    pc = cut(240).rearrange("p (h n) -> p h n", h=16)
    pcT = cut(1024).rearrange("p (a h q) -> p a h q", a=2, h=4)
    gcf = cut(96).rearrange("p (t g) -> p t g", t=NT)
    cmx = cut(32)

    begun = begin_product(i["w_kv_2"], 0, 1536)
    normed_T(LAT, 2, split=True)
    product(begun, keep_in(kv), [0, 1, 2, 3])
    for tt in range(NT):
        cos, sin = rope2[:, tt, 0, :], rope2[:, tt, 1, :]
        for kind in (0, 2, 4):
            rope(kv[:, tt, kind * 256:(kind + 1) * 256], 4, cos, sin)
        heads_T(kv[:, tt, 512:768], tt, 4, ksT, 0)
        heads_T(kv[:, tt, 1024:1280], tt, 4, kwT, 0)
    for n in range(2):
        for tt in range(NT):
            ve.op(v.tensor_copy, dup, bc(kv[:, tt, n * 256:(n + 1) * 256].rearrange("p (h f) -> p h f", f=HD), 2, 2),
                  after=[ac.now(), pe.now()])
            bk = bank_for_pe(2)
            pe.wait(ve.now())
            for h in range(4):
                pe.free(t.transpose, bk[:, h * P:(h + 1) * P], dup[:, h].rearrange("p a f -> p (a f)"), ident[:])
            b3 = bk.rearrange("p (h q) -> p h q", h=4)
            ve.op(v.tensor_copy, win[0:HD, :, tt * P:(tt + 1) * P], b3[0:HD], after=[pe.now()])
            lo = 1 if tt == 0 else 0
            ve.op(v.tensor_copy, win[HD:P, :, tt * P + lo - 1:(tt + 1) * P - 1], b3[HD:P, :, lo:P])
            read_by(2, ve.now())
        for c in range(16):
            ve.op(v.tensor_scalar, xw[:, c], win[:, :, 2 * c:2 * c + CMPS * (NCMP - 1) + 1:CMPS], pe2[:, n, c:c + 1], None,
                  ALU.add)
        slot = w_slot()
        tile = slot.ap[:].rearrange("p (c n) -> p c n", c=16)
        pe.wait(fetch(slot, (tile, i["cmp_w1_%s_2" % "kv"[n]].rearrange("(c p) n -> p c n", p=P))))
        bk = bank_for_pe(3)
        pe.wait(ve.now())
        for c in range(16):
            pe.free(t.matmul, bk[0:60, 0:256], xw[:, c].rearrange("p h n -> p (h n)"), tile[:, c, :],
                    start=(c == 0), stop=(c == 15))
        slot.reader = pe.now()
        ac.op(a.activation, hid[0:60], bk[0:60, 0:256], ACT.Gelu_apprx_tanh, after=[pe.now()])
        read_by(3, ac.now())
        bk = bank_for_pe(2)
        pe.wait(ac.now())
        for c in range(2):
            pe.free(t.transpose, bk[:, c * 60:(c + 1) * 60], hid[0:60, c * P:(c + 1) * P], ident[0:60, 0:60])
        ve.op(v.tensor_copy, hidT, bk[:, 0:120].rearrange("p (c r) -> p c r", c=2), after=[pe.now()])
        read_by(2, ve.now())
        bk = bank_for_pe(3)
        pe.wait(ve.now())
        if n == 0:
            for c in range(2):
                pe.free(t.matmul, bk[0:HD, 0:60], w2[:, n, c, :], hidT[:, c, :], start=(c == 0), stop=(c == 1))
            ve.op(v.tensor_copy, kcT[0:HD], bk[0:HD, 0:60], after=[pe.now()])
        else:
            for g in range(4):
                for c in range(2):
                    pe.free(t.matmul, bk[0:NCMP, g * HD:(g + 1) * HD], hidT[:, c, g * NCMP:(g + 1) * NCMP], w2[:, n, c, :],
                            start=(c == 0), stop=(c == 1))
            ve.op(v.tensor_copy, vc[0:NCMP], bk[0:NCMP, 0:256].rearrange("p (g f) -> p g f", g=4), after=[pe.now()])
        read_by(3, ve.now())
    begun = begin_product(i["b_w_q_2"][0], 0, IN3)
    normed_T(LAT, 0, split=True)
    product(begun, keep_in(projq), [0, 1, 2, 3])
    for tt in range(NT):
        rope(projq[:, tt, 0:1024], 16, rope2[:, tt, 0, :], rope2[:, tt, 1, :])
        heads_T(projq[:, tt, 0:1024], tt, 16, qT2, 0)
    ac.op(a.activation, gcf, projq[:, :, 1024:IN3], ACT.Exp, scale=-1.0, after=[ve.now()])
    ve.op(v.tensor_scalar, gcf, gcf, 1.0, None, ALU.add, after=[ac.now()])
    ve.op(v.reciprocal, gcf, gcf)
    for tt in range(NT):
        bk = bank_for_pe(0)
        pe.wait(ac.now())
        for h in range(16):
            pe.free(t.matmul, bk[:, h * NCMP:(h + 1) * NCMP], qT2[0:HD, h, tt * P:(tt + 1) * P],
                    kcT[0:HD, (h // 4) * NCMP:(h // 4 + 1) * NCMP], start=True, stop=True)
        s3 = bk[:, 0:240].rearrange("p (h n) -> p h n", h=16)
        ve.op(v.tensor_scalar, pc, s3, 0.125, None, ALU.mult, after=[pe.now()])
        read_by(0, ve.now())
        ve.op(v.tensor_tensor, pc, pc, bc(cmpmask[:, tt, 0, :], 1, 16), ALU.add)
        ve.op(v.tensor_reduce, cmx[:, 0:16], pc, AX, ALU.max)
        ve.op(v.tensor_tensor, pc, pc, bc(cmx[:, 0:16], 2, NCMP), ALU.subtract)
        ac.op(a.activation, pc, pc, ACT.Exp, after=[ve.now()])
        ve.op(v.tensor_reduce, cmx[:, 16:32], pc, AX, ALU.add, after=[ac.now()])
        ve.op(v.tensor_tensor, pc, pc, bc(cmpmask[:, tt, 1, :], 1, 16), ALU.mult)
        ve.op(v.reciprocal, cmx[:, 16:32], cmx[:, 16:32])
        ve.op(v.tensor_tensor, cmx[:, 16:32], cmx[:, 16:32], gcf[:, tt, 0:48:3], ALU.mult)
        for h0 in range(0, 16, 4):
            u = (h0 // 4) % 2
            bk = bank_for_pe(2 + u)
            pe.wait(ve.now())
            for h in range(4):
                pe.free(t.transpose, bk[0:NCMP, h * P:(h + 1) * P], pc[:, h0 + h, :], ident[:])
            ve.op(v.tensor_copy, pcT[0:NCMP, u], bk[0:NCMP, :].rearrange("p (h q) -> p h q", h=4), after=[pe.now()])
            read_by(2 + u, ve.now())
            o = bank_for_pe(4 + h0 // 8)
            pe.wait(ve.now())
            for h in range(4):
                c0 = ((h0 + h) % 8) * HD
                pe.free(t.matmul, o[:, c0:c0 + HD], pcT[0:NCMP, u, h, :], vc[0:NCMP, h0 // 4, :], start=True, stop=True)
            if h0 % 8 == 4:
                ve.wait(pe.now())
                into_cat(tt, h0 - 4, o.rearrange("p (h f) -> p h f", f=HD), cmx[:, 16 + h0 - 4:16 + h0 + 4])
                read_by(4 + h0 // 8, ve.now())

    def add_branch(branch):
        def finish(tt, h0, o, inv):
            ve.op(v.tensor_tensor, inv, inv, gcf[:, tt, 3 * h0 + branch:3 * h0 + branch + 22:3], ALU.mult)
            th = tmp[:, 0:512].rearrange("p (h f) -> p h f", f=HD)
            ve.op(v.tensor_tensor, th, o, bc(inv, 2, HD), ALU.mult)
            dst = cat[:, tt, h0 * HD:(h0 + 8) * HD]
            ve.op(v.tensor_tensor, dst, dst, tmp[:, 0:512], ALU.add)
        return finish

    for branch, kTb, v0 in ((1, ksT, 768), (2, kwT, 1280)):
        attention(16, 4, qT2, kTb, keys2, lambda g, b: kv[:, b, v0 + g * HD:v0 + (g + 1) * HD],
                  lambda tt: causal[:, tt, :], add_branch(branch))
    project_out(begin_product(i["b_w_out_2"][0], 0, D))
    add_gated(acc_tile)

    normed_T(LAT, 1)
    load_rows((prow[:, 0, :], i["final_gain_2"].partition_broadcast(P)))
    off[0] = 0
    utok = cut(2 * D).rearrange("p (t n) -> p t n", t=NT)
    XTe = cut(D).rearrange("p (k q) -> p k q", k=KD)
    onehot = cut(256).rearrange("p (t q) -> p t q", t=NT)
    gated = cut(256).rearrange("p (t q) -> p t q", t=NT)
    scat = cut(256).rearrange("p (t q) -> p t q", t=NT)
    yexp = cut(D)
    w_hi = [cut(2048) for _ in range(2)]
    d_hi = [wide[:, 2048 * u:2048 * (u + 1)] for u in range(2)]
    xe_hi, xe_lo = (cut(512).rearrange("p (k q) -> p k q", k=4) for _ in range(2))
    gate = cut(2 * 9).rearrange("p (t e) -> p t e", t=NT)
    slot_of = cut(4 * 9).rearrange("p (c t e) -> p c t e", c=2, t=NT)
    member = cut(16).rearrange("p (t e) -> p t e", t=NT)
    top, topf, one, cnt = (cut(8) for _ in range(4))
    topi, full = sb("topi", [P, 8], U32), sb("full", [P, 1], I32)
    ve.op(v.memset, gate, 0.0)
    ve.op(v.memset, slot_of, -1.0)
    ve.op(v.memset, moe_y, 0.0)
    iota8, iotas = const["iota"][:, 0:8], const["iota"][:]
    for tt in range(NT):
        bk = bank_for_pe(4)
        pe.wait(ve.now())
        for k in range(KD):
            pe.free(t.matmul, bk[:, 0:NEXP], XT[:, k, tt * P:(tt + 1) * P], wr[:, k, :], start=(k == 0), stop=(k == KD - 1))
        ve.op(v.tensor_copy, one, bk[:, 0:NEXP], after=[pe.now()])
        read_by(4, ve.now())
        ve.op(v.max, top, one)
        ve.op(v.max_index, topi[:], top, one)
        ve.op(v.tensor_copy, topf, topi[:])
        ve.op(v.tensor_tensor, top[:, 2:3], top[:, 1:2], top[:, 0:1], ALU.subtract)
        ac.op(a.activation, top[:, 3:4], top[:, 2:3], ACT.Exp, after=[ve.now()])
        ve.op(v.tensor_scalar, top[:, 4:5], top[:, 3:4], 1.0, None, ALU.add, after=[ac.now()])
        ve.op(v.reciprocal, top[:, 5:6], top[:, 4:5])
        ve.op(v.tensor_tensor, top[:, 6:7], top[:, 3:4], top[:, 5:6], ALU.mult)
        g8, m8_ = gate[:, tt, 0:8], member[:, tt, :]
        ve.op(v.tensor_scalar, g8, iota8, topf[:, 0:1], top[:, 5:6], ALU.is_equal, ALU.mult)
        ve.op(v.tensor_scalar, one, iota8, topf[:, 1:2], top[:, 6:7], ALU.is_equal, ALU.mult)
        ve.op(v.tensor_tensor, g8, g8, one, ALU.add)
        ve.op(v.tensor_scalar, m8_, iota8, topf[:, 0:1], None, ALU.is_equal)
        ve.op(v.tensor_scalar, one, iota8, topf[:, 1:2], None, ALU.is_equal)
        ve.op(v.tensor_tensor, m8_, m8_, one, ALU.add)
    bk = bank_for_pe(4)
    pe.wait(ve.now())
    pe.free(t.matmul, bk[:, 0:8], tri[:, 0, :], member[:, 0, :], start=True, stop=True)
    pe.free(t.matmul, bk[:, 8:16], ones[:], member[:, 0, :], start=True, stop=False)
    pe.free(t.matmul, bk[:, 8:16], tri[:, 0, :], member[:, 1, :], start=False, stop=True)
    pe.free(t.matmul, bk[:, 16:24], ones[:], member[:, 0, :], start=True, stop=False)
    pe.free(t.matmul, bk[:, 16:24], ones[:], member[:, 1, :], start=False, stop=True)
    ve.op(v.tensor_tensor, slot_of[:, 0, :, 0:8], bk[:, 0:16].rearrange("p (t e) -> p t e", t=NT), member, ALU.mult,
          after=[pe.now()])
    ve.op(v.tensor_reduce, cnt[:, 0:1], bk[:, 16:24], AX, ALU.max)
    read_by(4, ve.now())
    ve.op(v.tensor_scalar, slot_of[:, 0, :, 0:8], slot_of[:, 0, :, 0:8], 1.0, None, ALU.subtract)
    ve.op(v.tensor_scalar, slot_of[:, 1, :, 0:8], slot_of[:, 0, :, 0:8], float(P), None, ALU.subtract)
    ve.op(v.tensor_scalar, full[:], cnt[:, 0:1], float(P), None, ALU.is_gt)
    for tt in range(NT):
        for half in range(2):
            bk = bank_for_pe(5)
            for k in range(4):
                pe.free(t.transpose, bk[:, k * P:(k + 1) * P], XT[:, 4 * half + k, tt * P:(tt + 1) * P], ident[:])
            ve.op(v.tensor_copy, utok[:, tt, half * 512:(half + 1) * 512], bk, after=[pe.now()])
            read_by(5, ve.now())
    gv = [i[n][0].rearrange("e (p k) n -> p e k n", k=KD) for n in ("moe_w_gate_2", "moe_w_up_2")]
    dv = i["moe_w_down_2"][0].rearrange("e (i p k) n -> p (e i) k n", p=P, k=2)
    steps = FEXP // FCOL
    for n in ("xh", "xl", "onehot", "xsum", "xte", "gated", "scat_t", "scat", "yexp", "back", "ysum"):
        fs[n] = nc.alloc_semaphore("s_m" + n)
        nc.gpsimd.sem_inc(fs[n], 1)
        fn[n] = 1
    s_start = nc.alloc_semaphore("s_start")
    nc.gpsimd.drain().then_inc(s_start, 1)
    for e_ in (pe, ve, ac):
        e_.wait((s_start, 1))
    meet()

    def moe(c):
        base = dict(fn)
        ws, ds = open_slots()
        wl_ = [w_late[w_slots.index(s)] for s in ws]
        wn, dn_, wn2 = [s.n for s in ws], [s.n for s in ds], [s.n for s in wl_]
        sg1, hb1 = sg, hb
        hT1 = hT[:, :, :, 0:P]
        hl1 = work[:, 2048:2560].rearrange("p (a k q) -> p a k q", a=2, k=2)

        def run(e):
            def at(name, i_, plus):
                return e * steps + i_ + (base[name] + plus)

            def of(name, per, plus):
                return e * per + (base[name] + plus)

            def landed(n0, per, u, i_):
                return (e * steps + i_) * (per // 2) + (n0[u] + per - u * (per // 2))

            def load(i_, u):
                nc.sync.wait_ge(fs["gu"], at("gu", i_, -1))
                tile = ws[u].ap[:].rearrange("p (k c n) -> p k c n", k=KD, c=2)
                for half, sem in ((0, ws[u].sem), (1, wl_[u].sem)):
                    ks = slice(4 * half, 4 * half + 4)
                    for g in range(2):
                        src = gv[g][:, bass.ds(e, 1), ks, bass.ds(i_ * FCOL, FCOL)].rearrange("p e k n -> p (e k) n")
                        nc.sync.dma_start(tile[:, ks, g, :], src).then_inc(sem, 16)

            def split_w(i_, u):
                v.wait_ge(wl_[u].sem, landed(wn2, 32, u, i_))
                v.wait_ge(fs["gu"], at("gu", i_, -1))
                lo = ws[u].ap[:, 2048:4096]
                high(w_hi[u], lo).then_inc(fs["wh"], 1)
                v.wait_ge(fs["wh"], e * (steps - 1) + i_ + base["wh"])
                low(lo, lo, w_hi[u]).then_inc(fs["wl"], 1)

            def split_d(i_, u):
                v.wait_ge(ds[u].sem, landed(dn_, 16, u, i_))
                v.wait_ge(fs["dn"], at("dn", i_, -1))
                high(d_hi[u], ds[u].ap[:]).then_inc(fs["dh"], 1)
                v.wait_ge(fs["dh"], at("dh", i_, 1))
                low(ds[u].ap[:], ds[u].ap[:], d_hi[u]).then_inc(fs["dl"], 1)

            def load_down(i_, u):
                nc.sync.wait_ge(fs["dn"], at("dn", i_, -1))
                nc.sync.dma_start(ds[u].ap[:].rearrange("p (k n) -> p k n", k=2),
                                  dv[:, bass.ds(e * steps + i_, 1)].rearrange("p i k n -> p (i k) n")).then_inc(ds[u].sem, 16)

            def up(i_, u):
                whole = isinstance(i_, int) and i_ == 0
                t.wait_ge(fs["h"], at("h", i_, -1))
                if whole:
                    t.wait_ge(fs["xte"], of("xte", 2, 2))
                t.wait_ge(ws[u].sem, landed(wn, 32, u, i_))
                for k in range(KD):
                    if k == 4 and whole:
                        t.wait_ge(wl_[u].sem, landed(wn2, 32, u, i_))
                    if k == 4 and not whole:
                        t.wait_ge(fs["wl"], e * (steps - 1) + i_ + base["wl"])
                        if isinstance(i_, int) and i_ == 1:
                            t.wait_ge(fs["xl"], of("xl", 1, 1))
                    if k >= 4 and not whole:
                        cols, half = slice(k * 512, (k + 1) * 512), slice((k - 4) * 512, (k - 3) * 512)
                        mm = products3(psum[:, 2 + u, :], xe_hi[:, k - 4, :], xe_lo[:, k - 4, :], w_hi[u][:, half],
                                       ws[u].ap[:, cols], False, k == KD - 1)
                        continue
                    mm = t.matmul(psum[:, 2 + u, :], XTe[:, k, :], ws[u].ap[:, k * 512:(k + 1) * 512],
                                  start=(k == 0), stop=(k == KD - 1))
                mm.then_inc(fs["gu"], 1)
                a.wait_ge(fs["gu"], at("gu", i_, 1))
                a.wait_ge(fs["h"], at("h", i_, -1))
                a.activation(sg1[:, u, :], psum[:, 2 + u, 0:FCOL], ACT.Silu).then_inc(fs["silu"], 1)

            def hidden(i_, u):
                v.wait_ge(fs["silu"], at("silu", i_, 1))
                v.wait_ge(fs["tr"], at("tr", i_, -1))
                v.tensor_tensor(hb1[:, u, :], sg1[:, u, :], psum[:, 2 + u, FCOL:512], ALU.mult).then_inc(fs["h"], 1)

            def turn(i_, u):
                t.wait_ge(fs["h"], at("h", i_, 1))
                t.wait_ge(fs["ev"], at("ev", i_, -1))
                for k in range(2):
                    mm = t.transpose(psum[:, 4 + u, k * P:(k + 1) * P], hb1[:, u, k:FCOL:2], ident[:])
                mm.then_inc(fs["tr"], 1)
                v.wait_ge(fs["tr"], at("tr", i_, 1))
                v.wait_ge(fs["dn"], at("dn", i_, -1))
                src = psum[:, 4 + u, 0:256].rearrange("p (k q) -> p k q", k=2)
                high(hT1[:, u], src).then_inc(fs["eh"], 1)
                v.wait_ge(fs["eh"], at("eh", i_, 1))
                low(hl1[:, u], src, hT1[:, u]).then_inc(fs["ev"], 1)

            def downs(i_, u, start=False, stop=False):
                t.wait_ge(fs["dl"], at("dl", i_, 1))
                t.wait_ge(fs["ev"], at("ev", i_, 1))
                if start:
                    t.wait_ge(fs["yexp"], of("yexp", 2, 0))
                for k in range(2):
                    for h in range(2):
                        cols = slice(k * D + h * 512, k * D + (h + 1) * 512)
                        mm = products3(psum[:, h, :], hT1[:, u, k, :], hl1[:, u, k, :], d_hi[u][:, cols], ds[u].ap[:, cols],
                                       start and k == 0, stop and k == 1)
                mm.then_inc(fs["dn"], 1)

            def step(i_, u, ahead_=True):
                if not isinstance(i_, int) or i_ > 1:
                    split_d(i_ - 2, u)
                up(i_, u)
                if ahead_:
                    load(i_ + 1, 1 - u)
                if not isinstance(i_, int) or i_ > 0:
                    load_down(i_ - 1, 1 - u)
                    turn(i_ - 1, 1 - u)
                elif isinstance(i_, int):
                    v.wait_ge(fs["xte"], of("xte", 2, 2))
                    high(xe_hi, XTe[:, 4:8]).then_inc(fs["xh"], 1)
                    v.wait_ge(fs["xh"], of("xh", 1, 1))
                    low(xe_lo, XTe[:, 4:8], xe_hi).then_inc(fs["xl"], 1)
                hidden(i_, u)
                if ahead_:
                    split_w(i_ + 1, 1 - u)
                if not isinstance(i_, int) or i_ > 1:
                    downs(i_ - 2, u, start=isinstance(i_, int) and i_ == 2)

            load(0, 0)
            for i_ in range(4):
                step(i_, i_ % 2)
            with nc.Fori(0, (steps - 6) // 2) as r:
                for u in range(2):
                    step(r * 2 + (4 + u), u)
            for i_ in (steps - 2, steps - 1):
                step(i_, i_ % 2, i_ < steps - 1)
            load_down(steps - 1, 1)
            split_d(steps - 2, 0)
            gather(e + 1, of)
            turn(steps - 1, 1)
            downs(steps - 2, 0)
            split_d(steps - 1, 1)
            v.wait_ge(fs["scat_t"], of("scat_t", 1, 0))
            for tt in range(NT):
                ins = v.tensor_scalar(gated[:, tt, :], iotas, slot_of[:, c, tt, bass.ds(e, 1)], gate[:, tt, bass.ds(e, 1)],
                                      ALU.is_equal, ALU.mult)
            ins.then_inc(fs["gated"], 1)
            t.wait_ge(fs["gated"], of("gated", 1, 1))
            t.wait_ge(fs["xte"], of("xte", 2, 4))
            for tt in range(NT):
                mm = t.transpose(psum[:, 6, tt * P:(tt + 1) * P], gated[:, tt, :], ident[:])
            mm.then_inc(fs["scat_t"], 1)
            v.wait_ge(fs["scat_t"], of("scat_t", 1, 1))
            v.wait_ge(fs["back"], of("back", 4, 0))
            v.tensor_copy(scat, psum[:, 6, 0:256].rearrange("p (t q) -> p t q", t=NT)).then_inc(fs["scat"], 1)
            downs(steps - 1, 1, stop=True)
            a.wait_ge(fs["dn"], at("dn", steps, 0))
            a.wait_ge(fs["back"], of("back", 4, 0))
            for h in range(2):
                a.activation(yexp[:, h * 512:(h + 1) * 512], psum[:, h, :], ACT.Copy).then_inc(fs["yexp"], 1)
            t.wait_ge(fs["scat"], of("scat", 1, 1))
            for q in range(4):
                h, tt = q // 2, q % 2
                t.wait_ge(fs["yexp"], of("yexp", 2, h + 1))
                if q >= 2:
                    t.wait_ge(fs["ysum"], of("ysum", 4, q - 1))
                t.matmul(psum[:, 6 + tt, :], scat[:, tt, :], yexp[:, h * 512:(h + 1) * 512],
                         start=True, stop=True).then_inc(fs["back"], 1)
                v.wait_ge(fs["back"], of("back", 4, q + 1))
                v.wait_ge(fs["ysum"], of("ysum", 4, 0))
                y = moe_y[:, tt, h * 512:(h + 1) * 512]
                v.tensor_tensor(y, y, psum[:, 6 + tt, :], ALU.add).then_inc(fs["ysum"], 1)

        def gather(e, of):
            v.wait_ge(fs["xsum"], of("xsum", 2, 2))
            for tt in range(NT):
                ins = v.tensor_scalar(onehot[:, tt, :], iotas, slot_of[:, c, tt, bass.ds(e, 1)], None, ALU.is_equal)
            ins.then_inc(fs["onehot"], 1)
            t.wait_ge(fs["onehot"], of("onehot", 1, 2))
            t.wait_ge(fs["ysum"], of("ysum", 4, 0))
            for half in range(2):
                for k in range(4):
                    kk_ = 4 * half + k
                    for tt in range(NT):
                        mm = t.matmul(psum[:, 6 + half, k * P:(k + 1) * P], utok[:, tt, kk_ * P:(kk_ + 1) * P],
                                      onehot[:, tt, :], start=(tt == 0), stop=(tt == NT - 1))
                mm.then_inc(fs["xsum"], 1)
                a.wait_ge(fs["xsum"], of("xsum", 2, 3 + half))
                a.activation(XTe[:, 4 * half:4 * half + 4, :], psum[:, 6 + half, :].rearrange("p (k q) -> p k q", k=4),
                             ACT.Copy).then_inc(fs["xte"], 1)

        gather(0, lambda name, per, plus: base[name] + plus - (per if name != "ysum" else 0))
        with nc.Fori(0, NEXP) as e:
            run(e)
        total = NEXP * steps
        for n in ("gu", "silu", "h", "tr", "eh", "ev", "dn", "dh", "dl"):
            fn[n] += total
        for n, count in (("wh", total - NEXP), ("wl", total - NEXP), ("xh", NEXP), ("xl", NEXP)):
            fn[n] += count
        for u in range(2):
            wl_[u].n += 16 * total
        for n, per, more in (("onehot", 1, 1), ("xsum", 2, 2), ("xte", 2, 2), ("gated", 1, 0), ("scat_t", 1, 0),
                             ("scat", 1, 0), ("yexp", 2, 0), ("back", 4, 0), ("ysum", 4, 0)):
            fn[n] += per * NEXP + more
        close_slots(ws, ds, total)
        for e_ in (nc.tensor, nc.vector, nc.scalar):
            e_.wait_ge(fs["ysum"], fn["ysum"])
            e_.wait_ge(fs["xte"], fn["xte"])

    moe(0)
    for e_ in (nc.tensor, nc.vector, nc.scalar, nc.sync, nc.gpsimd):
        e_.wait_ge(ve.sem, ve.n)
    overfull = nc.values_load(full[0:1, 0:1], min_val=0, max_val=1)
    with nc.If(overfull > 0):
        moe(1)
    add_gated(lambda tt: moe_y[:, tt, :])

    s_out = nc.alloc_semaphore("s_out")
    ov = out[0].rearrange("(t p) d -> p t d", p=P)
    for tt in range(NT):
        ss = st[:, tt:tt + 1]
        ac.op(a.activation, xn, x[:, LAT, tt, :], ACT.Square, accum_out=ss, after=[ve.now()])
        rstd(ss, D, 1)
        ve.op(v.scalar_tensor_tensor, cat[:, tt, :], x[:, LAT, tt, :], ss, prow[:, 0, :], ALU.mult, ALU.mult,
              after=[(s_row, rows[0])])
        nc.sync.wait_ge(ve.sem, ve.n)
        nc.sync.dma_start(ov[:, tt, :], cat[:, tt, :]).then_inc(s_out, 16)
    nc.sync.wait_ge(s_out, 16 * NT)


NAMES = ["x", "c", "ctx", "c_ctx", "w_mod", "b_mod", "norm_mix_pre", "norm_mix_post", "norm_ffn_pre",
         "norm_ffn_post", "w_in", "q_norm", "k_norm", "conv_w", "conv_b", "dt_bias_fwd", "dt_bias_bwd",
         "a_log_fwd", "a_log_bwd", "d_skip", "ssd_norm", "w_out", "w_gate", "w_up", "w_down", "c_2",
         "positions_2", "attn_gain_2", "ffn_gain_2", "w_ada_2", "b_ada_2", "a_w_in_2", "a_w_out_2",
         "b_w_q_2", "b_w_out_2", "kv_gain_2", "w_kv_ada_2", "b_kv_ada_2", "w_kv_2", "cmp_pe_k_2",
         "cmp_w1_k_2", "cmp_w2_k_2", "cmp_pe_v_2", "cmp_w1_v_2", "cmp_w2_v_2", "ffn_w_gate_2",
         "ffn_w_up_2", "ffn_w_down_2", "moe_w_router_2", "moe_w_gate_2", "moe_w_up_2", "moe_w_down_2",
         "final_gain_2"]


def kernel(**inputs):
    import numpy as _np
    import concourse.bacc as _bacc
    from concourse import mybir as _mybir
    from concourse.bass_utils import run_bass_kernel_spmd as _run

    nc = _bacc.Bacc("TRN2", target_bir_lowering=False, num_devices=1)
    arrays, args = {}, {}
    for name in NAMES:
        a = _np.ascontiguousarray(inputs[name])
        arrays["in_" + name] = a
        args[name] = nc.dram_tensor("in_" + name, a.shape, _mybir.dt.from_np(a.dtype), kind="ExternalInput").ap()
    out = nc.dram_tensor("out", (1, T, D), F32, kind="ExternalOutput").ap()
    build(nc, args, out)
    r = _run(nc, [arrays], core_ids=[0])
    return r.results[0]["out"]
```
